# Optimizing a Trainium2 kernel written in Bass

```python
import math
import jax, jax.numpy as jnp
from jax import lax
import numpy as np

D_MODEL = 1024
BATCH = 1
SEQ = 512
DEPTH = 2

N_A = DEPTH // 2
N_B = DEPTH - N_A
N_HEADS = 16
HEAD_DIM = D_MODEL // N_HEADS
CONV_W = 31
FFN_DIM = 2816
FFN_CONV_W = 3
PLE_DIM = 256
Q_BLOCK = 128
LN_EPS = 1e-5
DN_ALPHA = (2.0 * DEPTH) ** 0.25
DN_BETA = (8.0 * DEPTH) ** -0.25


def layer_norm(x, g, b):
    xf = x.astype(jnp.float32)
    mu = jnp.mean(xf, axis=-1, keepdims=True)
    var = jnp.mean(jnp.square(xf - mu), axis=-1, keepdims=True)
    y = (xf - mu) * lax.rsqrt(var + LN_EPS)
    return (y * g.astype(jnp.float32) + b.astype(jnp.float32)).astype(x.dtype)

def causal_dwconv(x, w, b):
    k = w.shape[0]
    y = lax.conv_general_dilated(
        x, w[:, None, :].astype(x.dtype), window_strides=(1,), padding=[(k - 1, 0)],
        dimension_numbers=("NWC", "WIO", "NWC"), feature_group_count=x.shape[-1])
    return y + b

def conformer_conv(x, pw1_w, pw1_b, dw_w, dw_b, ln_g, ln_b, pw2_w, pw2_b):
    h = x @ pw1_w + pw1_b
    a, g = jnp.split(h, 2, axis=-1)
    h = a * jax.nn.sigmoid(g)
    h = causal_dwconv(h, dw_w, dw_b)
    h = layer_norm(h, ln_g, ln_b)
    h = jax.nn.silu(h)
    return h @ pw2_w + pw2_b

def stick_breaking_attention(q, k, v):
    b, s, h, dh = q.shape
    nb = s // Q_BLOCK
    scale = 1.0 / math.sqrt(dh)
    kh = jnp.transpose(k, (0, 2, 1, 3))
    vh = jnp.transpose(v, (0, 2, 1, 3))
    qb = jnp.transpose(q.reshape(b, nb, Q_BLOCK, h, dh), (1, 0, 3, 2, 4))
    t0s = jnp.arange(nb, dtype=jnp.int32) * Q_BLOCK
    ts = jnp.arange(s, dtype=jnp.int32)

    def block(args):
        qblk, t0 = args
        z = jnp.einsum('bhqd,bhkd->bhqk', qblk, kh).astype(jnp.float32) * scale
        tq = t0 + jnp.arange(Q_BLOCK, dtype=jnp.int32)
        mask = ts[None, :] < tq[:, None]
        log_1m = jnp.where(mask, jax.nn.log_sigmoid(-z), 0.0)
        rev = lax.cumsum(log_1m, axis=3, reverse=True)
        log_a = jax.nn.log_sigmoid(z) + (rev - log_1m)
        a = jnp.where(mask, jnp.exp(log_a), 0.0)
        return jnp.einsum('bhqk,bhkd->bhqd', a.astype(vh.dtype), vh)

    out = lax.map(block, (qb, t0s))
    return jnp.transpose(out, (1, 0, 3, 2, 4)).reshape(b, s, h * dh)

def conv_gated_ffn(x, w_up, w_gate, conv_w, conv_b, w_down):
    u = x @ w_up
    g = causal_dwconv(x @ w_gate, conv_w, conv_b)
    return (jax.nn.silu(g) * u) @ w_down

def first_inputs(seed: int = 0) -> dict:
    key = jax.random.key(seed)
    ks = jax.random.split(key, 32)
    D, F = D_MODEL, FFN_DIM

    def nrm(k, shape, scale):
        return jax.random.normal(k, shape, jnp.float32) * scale

    return {
        "x": nrm(ks[0], (BATCH, SEQ, D), 1.0),
        "p": nrm(ks[1], (DEPTH, BATCH, SEQ, PLE_DIM), 1.0),
        "a_pw1_w": nrm(ks[2], (N_A, D, 2 * D), D ** -0.5),
        "a_pw1_b": nrm(ks[3], (N_A, 2 * D), 0.02),
        "a_dw_w": nrm(ks[4], (N_A, CONV_W, D), CONV_W ** -0.5),
        "a_dw_b": nrm(ks[5], (N_A, D), 0.02),
        "a_ln_g": 1.0 + nrm(ks[6], (N_A, D), 0.02),
        "a_ln_b": nrm(ks[7], (N_A, D), 0.02),
        "a_pw2_w": nrm(ks[8], (N_A, D, D), D ** -0.5 * DN_BETA),
        "a_pw2_b": nrm(ks[9], (N_A, D), 0.02),
        "b_wq": nrm(ks[10], (N_B, D, D), D ** -0.5),
        "kv_wk": nrm(ks[11], (D, D), D ** -0.5),
        "kv_wv": nrm(ks[12], (D, D), D ** -0.5 * DN_BETA),
        "b_wo": nrm(ks[13], (N_B, D, D), D ** -0.5 * DN_BETA),
        "ln_mix_g": 1.0 + nrm(ks[14], (DEPTH, D), 0.02),
        "ln_mix_b": nrm(ks[15], (DEPTH, D), 0.02),
        "ffn_w_up": nrm(ks[16], (DEPTH, D, F), D ** -0.5),
        "ffn_w_gate": nrm(ks[17], (DEPTH, D, F), D ** -0.5),
        "ffn_conv_w": nrm(ks[18], (DEPTH, FFN_CONV_W, F), FFN_CONV_W ** -0.5),
        "ffn_conv_b": nrm(ks[19], (DEPTH, F), 0.02),
        "ffn_w_down": nrm(ks[20], (DEPTH, F, D), F ** -0.5 * DN_BETA),
        "ple_w_gate": nrm(ks[21], (DEPTH, D, D), D ** -0.5),
        "ple_w_proj": nrm(ks[22], (DEPTH, PLE_DIM, D), PLE_DIM ** -0.5 * DN_BETA),
        "ln_ffn_g": 1.0 + nrm(ks[23], (DEPTH, D), 0.02),
        "ln_ffn_b": nrm(ks[24], (DEPTH, D), 0.02),
    }

def first_block(x, p, a_pw1_w, a_pw1_b, a_dw_w, a_dw_b, a_ln_g, a_ln_b, a_pw2_w, a_pw2_b,
              b_wq, kv_wk, kv_wv, b_wo, ln_mix_g, ln_mix_b,
              ffn_w_up, ffn_w_gate, ffn_conv_w, ffn_conv_b, ffn_w_down,
              ple_w_gate, ple_w_proj, ln_ffn_g, ln_ffn_b):
    b, s, d = x.shape
    k_shared = None
    v_shared = None
    for i in range(DEPTH):
        if i < N_A:
            mix = conformer_conv(x, a_pw1_w[i], a_pw1_b[i], a_dw_w[i], a_dw_b[i],
                                 a_ln_g[i], a_ln_b[i], a_pw2_w[i], a_pw2_b[i])
        else:
            j = i - N_A
            if k_shared is None:
                k_shared = (x @ kv_wk).reshape(b, s, N_HEADS, HEAD_DIM)
                v_shared = (x @ kv_wv).reshape(b, s, N_HEADS, HEAD_DIM)
            q = (x @ b_wq[j]).reshape(b, s, N_HEADS, HEAD_DIM)
            mix = stick_breaking_attention(q, k_shared, v_shared) @ b_wo[j]
        x = layer_norm(DN_ALPHA * x + mix, ln_mix_g[i], ln_mix_b[i])
        ffn = conv_gated_ffn(x, ffn_w_up[i], ffn_w_gate[i], ffn_conv_w[i], ffn_conv_b[i], ffn_w_down[i])
        ple = jax.nn.sigmoid(x @ ple_w_gate[i]) * (p[i] @ ple_w_proj[i])
        x = layer_norm(DN_ALPHA * x + ffn + ple, ln_ffn_g[i], ln_ffn_b[i])
    return x


D_MIX = D_MODEL
GLA_HEADS = 4
GLA_DK = 64
GLA_DV = 128
GLA_WIDTH = GLA_HEADS * GLA_DV
GLA_KEY_WIDTH = GLA_HEADS * GLA_DK
GLA_GATE_RANK = 16
GLA_GATE_TEMP = 16.0
GLA_CHUNK = 64
MLA_HEADS = 4
MLA_NOPE = 128
MLA_ROPE = 64
MLA_QK = MLA_NOPE + MLA_ROPE
MLA_DV = 128
MLA_WIDTH = MLA_HEADS * MLA_DV
MLA_Q_RANK = 256
MLA_KV_RANK = 128
ROPE_THETA = 10000.0
EPS = 1e-6

IN_SPLITS = (GLA_KEY_WIDTH, GLA_KEY_WIDTH, GLA_WIDTH, GLA_GATE_RANK, GLA_WIDTH,
             MLA_Q_RANK, MLA_KV_RANK, MLA_ROPE, MLA_WIDTH)
D_IN = sum(IN_SPLITS)


def rmsnorm(t, g):
    t32 = t.astype(jnp.float32)
    y = t32 * lax.rsqrt(jnp.mean(t32 * t32, axis=-1, keepdims=True) + EPS)
    return (y * g.astype(jnp.float32)).astype(t.dtype)

def apply_rope(t, cos, sin):
    half = t.shape[-1] // 2
    t32 = t.astype(jnp.float32)
    t1, t2 = t32[..., :half], t32[..., half:]
    return jnp.concatenate([t1 * cos - t2 * sin, t1 * sin + t2 * cos], axis=-1).astype(t.dtype)

def gla_mix(q, k, v, log_a, norm_g):
    B, S = q.shape[0], q.shape[1]
    n_chunks = S // GLA_CHUNK

    def to_chunks(t):
        return t.astype(jnp.float32).reshape(B, n_chunks, GLA_CHUNK, GLA_HEADS, -1).transpose(0, 3, 1, 2, 4)

    qc = to_chunks(q) * (GLA_DK ** -0.5)
    kc, vc, lac = to_chunks(k), to_chunks(v), to_chunks(log_a)
    b = jnp.cumsum(lac, axis=3)
    b_last = b[:, :, :, -1:, :]
    q_dec = qc * jnp.exp(b)
    k_inv = kc * jnp.exp(-b)
    k_end = kc * jnp.exp(b_last - b)

    causal = jnp.tril(jnp.ones((GLA_CHUNK, GLA_CHUNK), dtype=bool))
    a_intra = jnp.where(causal, jnp.einsum('bhnik,bhnjk->bhnij', q_dec, k_inv), 0.0)
    o_intra = jnp.einsum('bhnij,bhnjv->bhniv', a_intra, vc)

    chunk_update = jnp.einsum('bhnjk,bhnjv->bhnkv', k_end, vc)
    chunk_decay = jnp.exp(b_last[:, :, :, 0, :])

    def step(state, inp):
        decay, upd = inp
        return decay[..., None] * state + upd, state

    state0 = jnp.zeros((B, GLA_HEADS, GLA_DK, GLA_DV), jnp.float32)
    _, state_prev = lax.scan(step, state0,
                             (jnp.moveaxis(chunk_decay, 2, 0), jnp.moveaxis(chunk_update, 2, 0)))
    state_prev = jnp.moveaxis(state_prev, 0, 2)
    o_inter = jnp.einsum('bhnik,bhnkv->bhniv', q_dec, state_prev)

    o = (o_intra + o_inter).transpose(0, 2, 3, 1, 4).reshape(B, S, GLA_HEADS, GLA_DV)
    o = rmsnorm(o.astype(q.dtype), norm_g)
    return o.reshape(B, S, GLA_WIDTH)

def block_causal_attention(q, k, v):
    B, S = q.shape[0], q.shape[1]
    n_blocks = S // Q_BLOCK
    scale = MLA_QK ** -0.5
    kt = k.transpose(0, 2, 1, 3)
    vt = v.transpose(0, 2, 1, 3)
    qb = q.transpose(0, 2, 1, 3).reshape(B, MLA_HEADS, n_blocks, Q_BLOCK, MLA_QK).transpose(2, 0, 1, 3, 4)
    key_idx = jnp.arange(S)

    def one_block(args):
        q_blk, i = args
        s = jnp.einsum('bhqd,bhkd->bhqk', q_blk, kt).astype(jnp.float32) * scale
        q_idx = i * Q_BLOCK + jnp.arange(Q_BLOCK)
        s = jnp.where(key_idx[None, :] <= q_idx[:, None], s, -jnp.inf)
        p = jax.nn.softmax(s, axis=-1).astype(v.dtype)
        return jnp.einsum('bhqk,bhkd->bhqd', p, vt)

    o = lax.map(one_block, (qb, jnp.arange(n_blocks)))
    return o.transpose(1, 0, 3, 2, 4).reshape(B, S, MLA_HEADS * MLA_DV)

def second_inputs(seed: int = 0) -> dict:
    key = jax.random.key(seed)
    ks = jax.random.split(key, 16)
    f32 = jnp.float32

    def w(k, shape, fan_in):
        return jax.random.normal(k, shape, f32) * (fan_in ** -0.5)

    def gain(k, shape):
        return 1.0 + 0.02 * jax.random.normal(k, shape, f32)

    x = jax.random.normal(ks[0], (BATCH, SEQ, D_MODEL), f32)
    offsets = jax.random.randint(ks[1], (BATCH, 1), 0, 1024, dtype=jnp.int32)
    positions = offsets + jnp.arange(SEQ, dtype=jnp.int32)[None, :]
    return {
        "x": x,
        "positions": positions,
        "norm_g": gain(ks[2], (DEPTH, D_MODEL)),
        "w_in": w(ks[3], (DEPTH, D_MODEL, D_IN), D_MODEL),
        "w_gla_gate_up": w(ks[4], (DEPTH, GLA_GATE_RANK, GLA_KEY_WIDTH), GLA_GATE_RANK),
        "b_gla_gate": 0.01 * jax.random.normal(ks[5], (DEPTH, GLA_KEY_WIDTH), f32),
        "gla_norm_g": gain(ks[6], (DEPTH, GLA_DV)),
        "mla_q_norm_g": gain(ks[7], (DEPTH, MLA_Q_RANK)),
        "w_uq": w(ks[8], (DEPTH, MLA_Q_RANK, MLA_HEADS * MLA_QK), MLA_Q_RANK),
        "mla_kv_norm_g": gain(ks[9], (DEPTH, MLA_KV_RANK)),
        "w_ukv": w(ks[10], (DEPTH, MLA_KV_RANK, MLA_HEADS * (MLA_NOPE + MLA_DV)), MLA_KV_RANK),
        "q_head_g": gain(ks[11], (DEPTH, MLA_QK)),
        "k_head_g": gain(ks[12], (DEPTH, MLA_QK)),
        "w_out": w(ks[13], (DEPTH, D_MIX, D_MODEL), D_MIX),
    }

def second_block(x, positions, norm_g, w_in, w_gla_gate_up, b_gla_gate, gla_norm_g,
              mla_q_norm_g, w_uq, mla_kv_norm_g, w_ukv, q_head_g, k_head_g, w_out):
    B, S = x.shape[0], x.shape[1]
    split_idx = [int(v) for v in np.cumsum(IN_SPLITS)[:-1]]

    inv_freq = ROPE_THETA ** (-jnp.arange(0, MLA_ROPE, 2, dtype=jnp.float32) / MLA_ROPE)
    ang = positions.astype(jnp.float32)[..., None] * inv_freq
    cos = jnp.cos(ang)[:, :, None, :]
    sin = jnp.sin(ang)[:, :, None, :]

    for l in range(DEPTH):
        h = rmsnorm(x, norm_g[l])
        z = h @ w_in[l]
        (g_q, g_k, g_v, g_lr, g_gate,
         c_q, c_kv, k_pe, m_gate) = jnp.split(z, split_idx, axis=-1)

        gate_logit = (g_lr @ w_gla_gate_up[l] + b_gla_gate[l]).astype(jnp.float32)
        log_a = jax.nn.log_sigmoid(gate_logit) / GLA_GATE_TEMP
        o_gla = gla_mix(g_q.reshape(B, S, GLA_HEADS, GLA_DK),
                        g_k.reshape(B, S, GLA_HEADS, GLA_DK),
                        g_v.reshape(B, S, GLA_HEADS, GLA_DV),
                        log_a.reshape(B, S, GLA_HEADS, GLA_DK),
                        gla_norm_g[l])
        o_gla = o_gla * jax.nn.silu(g_gate)

        q = (rmsnorm(c_q, mla_q_norm_g[l]) @ w_uq[l]).reshape(B, S, MLA_HEADS, MLA_QK)
        kv = (rmsnorm(c_kv, mla_kv_norm_g[l]) @ w_ukv[l]).reshape(B, S, MLA_HEADS, MLA_NOPE + MLA_DV)
        k_nope, v = kv[..., :MLA_NOPE], kv[..., MLA_NOPE:]
        k_rope = jnp.broadcast_to(k_pe[:, :, None, :], (B, S, MLA_HEADS, MLA_ROPE))
        k = jnp.concatenate([k_nope, k_rope], axis=-1)
        q = rmsnorm(q, q_head_g[l])
        k = rmsnorm(k, k_head_g[l])
        q = jnp.concatenate([q[..., :MLA_NOPE], apply_rope(q[..., MLA_NOPE:], cos, sin)], axis=-1)
        k = jnp.concatenate([k[..., :MLA_NOPE], apply_rope(k[..., MLA_NOPE:], cos, sin)], axis=-1)
        o_mla = block_causal_attention(q, k, v) * jax.nn.silu(m_gate)

        x = x + jnp.concatenate([o_gla, o_mla], axis=-1) @ w_out[l]
    return x


def setup_inputs(seed=0):
    out = dict(first_inputs(seed))
    for name, value in second_inputs(seed + 1).items():
        if name != "x":
            out[name + "_2"] = value
    return out


def reference(
    x, p, a_pw1_w, a_pw1_b, a_dw_w, a_dw_b, a_ln_g, a_ln_b, a_pw2_w, a_pw2_b, b_wq, kv_wk,
    kv_wv, b_wo, ln_mix_g, ln_mix_b, ffn_w_up, ffn_w_gate, ffn_conv_w, ffn_conv_b, ffn_w_down,
    ple_w_gate, ple_w_proj, ln_ffn_g, ln_ffn_b, positions_2, norm_g_2, w_in_2, w_gla_gate_up_2,
    b_gla_gate_2, gla_norm_g_2, mla_q_norm_g_2, w_uq_2, mla_kv_norm_g_2, w_ukv_2, q_head_g_2,
    k_head_g_2, w_out_2,
):
    x = first_block(
        x, p, a_pw1_w, a_pw1_b, a_dw_w, a_dw_b, a_ln_g, a_ln_b, a_pw2_w, a_pw2_b, b_wq, kv_wk,
        kv_wv, b_wo, ln_mix_g, ln_mix_b, ffn_w_up, ffn_w_gate, ffn_conv_w, ffn_conv_b,
        ffn_w_down, ple_w_gate, ple_w_proj, ln_ffn_g, ln_ffn_b,
    )
    return second_block(
        x, positions_2, norm_g_2, w_in_2, w_gla_gate_up_2, b_gla_gate_2, gla_norm_g_2,
        mla_q_norm_g_2, w_uq_2, mla_kv_norm_g_2, w_ukv_2, q_head_g_2, k_head_g_2, w_out_2,
    )


_drawn_inputs = setup_inputs


def setup_inputs(seed=0):
    import zlib

    import numpy as np

    out = dict(_drawn_inputs(seed))
    spreads = {}
    factors = {'a_pw1_b': 4.223,
     'a_dw_b': 3.973,
     'a_ln_g': 7.214,
     'a_ln_b': 8.0,
     'ffn_conv_b': 6.864,
     'b_gla_gate_2': 8.0,
     'gla_norm_g_2': 4.676,
     'mla_q_norm_g_2': 8.0,
     'mla_kv_norm_g_2': 8.0,
     'q_head_g_2': 8.0,
     'k_head_g_2': 8.0}
    for name, (base, spread) in spreads.items():
        noise = np.random.default_rng([zlib.crc32(name.encode()), seed]).standard_normal(out[name].shape)
        drawn = base * np.exp(spread * noise) if base else spread * noise
        out[name] = __import__('jax').numpy.asarray(drawn.astype(out[name].dtype))
    for name, factor in factors.items():
        out[name] = (out[name] * factor).astype(out[name].dtype)
    return out
```

```python
from contextlib import ExitStack

import concourse.bass as bass
from concourse import mybir

ALU = mybir.AluOpType
ACT = mybir.ActivationFunctionType
AX = mybir.AxisListType
F32 = mybir.dt.float32
FR = mybir.dt.float32r
BF = mybir.dt.bfloat16
I32 = mybir.dt.int32

S = 512
D = 1024
KD = 8
FT = 22
NU = 8
RAW, SLOTS, AHEAD = 4, 4, 3
ALPHA = 4.0 ** 0.25
TAPS = 31
PE_TAPS = 12
NEG = -1e30


def grouped(mat, nk, cols, g):
    out = []
    for c0 in range(0, len(cols), g):
        out += [(mat, k, c) for k in range(nk) for c in cols[c0:c0 + g]]
    return out


def ffn_order(layer):
    out = []
    for f in range(FT):
        out += [(f"up{layer}", k, f) for k in range(KD)] + [(f"gate{layer}", k, f) for k in range(KD)]
    return out


def weight_order():
    o = []

    def align():
        while len(o) % 4:
            o.append(None)

    for f in range(8):
        o.extend([("pw1", k, f) for k in range(KD)] + [("pw1", k, 8 + f) for k in range(KD)])
    o += grouped("pw2", KD, list(range(8)), 4)
    for layer in range(2):
        if layer == 1:
            o += grouped("wq", KD, list(range(8)), 4)
            o += grouped("wk", KD, list(range(8)), 4)
            align()
            for half in range(2):
                o += [("wv", k, 4 * half + c) for k in range(KD) for c in range(4)]
            o += grouped("wo", KD, list(range(8)), 1)
        for f0 in range(0, 8, 2):
            o += grouped(f"pg{layer}", KD, [f0, f0 + 1], 2)
            o += grouped(f"pp{layer}", 2, [f0, f0 + 1], 2)
        o += ffn_order(layer)
        o += grouped(f"down{layer}", FT, list(range(8)), 1)
    for layer in range(2):
        align()
        o += grouped(f"in{layer}", KD, list(range(4)), 4)
        o += grouped(f"in{layer}", KD, list(range(4, 8)), 4)
        align()
        o += [(f"in{layer}", k, 8 + c) for k in range(KD) for c in range(4)]
        o += grouped(f"in{layer}", KD, list(range(12, 20)), 1)
        o += grouped(f"uq{layer}", 2, list(range(8)), 1)
        o += grouped(f"ukv{layer}", 1, list(range(4)), 1)
        align()
        o += [(f"ukv{layer}", 0, 4 + c) for c in range(4)]
        o += grouped(f"out{layer}", KD, list(range(8)), 1)
    while len(o) % NU:
        o.append(None)
    return o


def param_order():
    o = [("b1", 16), ("dww", 8 * TAPS), ("dwb", 8), ("lng", 8), ("lnb", 8), ("b2", 8)]
    for i in range(2):
        o += [(f"mixg{i}", 8), (f"mixb{i}", 8), (f"fcw{i}", 3 * FT), (f"fcb{i}", FT),
              (f"fg{i}", 8), (f"fb{i}", 8), (f"ng{i}", 8), (f"bgg{i}", 2), (f"glag{i}", 1),
              (f"mqg{i}", 2), (f"mkvg{i}", 1), (f"qgn{i}", 1), (f"qga{i}", 1), (f"qgb{i}", 1),
              (f"kgn{i}", 1), (f"kga{i}", 1), (f"kgb{i}", 1)]
    at, n = {}, 0
    for name, w in o:
        at[name] = n
        n += w
    return at, n


CONST = {"ident": (0, 128), "ones": (128, 128), "tri": (256, 128), "msb": (384, 128), "mml": (512, 128),
         "mgl": (640, 128), "scan": (768, 512), "invf": (1280, 1), "sgn": (1281, 1), "mhalf": (1282, 8),
         "one": (1290, 1), "epsr": (1291, 1)}
NCONST = 1292


class Queue:

    def __init__(self):
        self.items = {e: [] for e in ("pe", "act", "dve", "pool", "sp")}
        self.count = {}

    def put(self, eng, fn, *deps, inc=True, sem=None, by=1):
        sem = sem or eng
        tok = None
        if inc:
            self.count[sem] = self.count.get(sem, 0) + by
            tok = (sem, self.count[sem])
        self.items[eng].append((fn, flat(deps), sem if inc else None, by))
        return tok

    def last(self):
        return [(e, self.count[e]) for e in ("pe", "act", "dve", "pool") if e in self.count]

    def emit(self, eng, e, sems):
        seen = {}
        for fn, deps, sem, by in self.items[eng]:
            for s, v in deps:
                if seen.get(s, 0) < v:
                    e.wait_ge(sems[s], v)
                    seen[s] = v
            ins = fn(e)
            if sem is not None:
                ins.then_inc(sems[sem], by)


def flat(deps):
    out = []
    for d in deps:
        if d is None:
            continue
        if isinstance(d, tuple) and len(d) == 2 and isinstance(d[0], str):
            out.append(d)
        else:
            out += flat(d)
    need = {}
    for s, v in out:
        need[s] = max(need.get(s, 0), v)
    return list(need.items())


class Buf:

    def __init__(self, t, free=()):
        self.t = t
        self.free = list(free)


def build(nc, a, out):
    q = Queue()
    ctx = ExitStack()
    par, npar = param_order()
    order = weight_order()
    nunit = len(order) // NU

    def sb(stack, name, shape, dt=F32):
        return stack.enter_context(nc.sbuf_tensor(name, shape, dt))

    with ctx:
        bank = [Buf(ctx.enter_context(nc.psum_tensor(f"bank{i}", [128, 512], F32))) for i in range(8)]
        cst = sb(ctx, "cst", [128, NCONST])
        prm = sb(ctx, "prm", [128, npar])
        identb = sb(ctx, "identb", [128, 128], BF)
        msb = sb(ctx, "msb", [128, 128], BF)
        mml = sb(ctx, "mml", [128, 128], BF)
        trir = sb(ctx, "trir", [128, 128], FR)
        onesr = sb(ctx, "onesr", [128, 128], FR)
        X = sb(ctx, "X", [128, KD, S])
        XH = sb(ctx, "XH", [128, KD, S], FR)
        XL = sb(ctx, "XL", [128, KD, S], FR)
        wraw = [Buf(sb(ctx, f"wraw{i}", [128, NU * 128])) for i in range(RAW)]
        wh = [Buf(sb(ctx, f"wh{i}", [128, NU * 128], FR)) for i in range(SLOTS)]
        wl = [sb(ctx, f"wl{i}", [128, NU * 128], FR) for i in range(SLOTS)]
        st = sb(ctx, "st", [128, 48])

        def C(name, rows=slice(0, 128)):
            o, n = CONST[name]
            return cst[rows, o:o + n]

        def P(name, j=0, rows=slice(0, 128)):
            return prm[rows, par[name] + j:par[name] + j + 1]

        def act(o, i, f, *deps, bias=None, scale=None, accum=None):
            kw = {}
            if bias is not None:
                kw["bias"] = bias
            if scale is not None:
                kw["scale"] = scale
            if accum is not None:
                kw["accum_out"] = accum
            return q.put("act", lambda e: e.activation(o, i, f, **kw), *deps)

        def stt(o, i0, s, i1, op0, op1, *deps):
            return q.put("dve", lambda e: e.scalar_tensor_tensor(out=o, in0=i0, scalar=s, in1=i1,
                                                                  op0=op0, op1=op1), *deps)

        def tt(o, i0, i1, op, *deps, eng="dve"):
            return q.put(eng, lambda e: e.tensor_tensor(o, i0, i1, op), *deps)

        def ts(o, i0, s1, s2, op0, op1, *deps, eng="dve"):
            if op1 is None:
                return q.put(eng, lambda e: e.tensor_scalar(o, i0, s1, None, op0), *deps)
            return q.put(eng, lambda e: e.tensor_scalar(o, i0, s1, s2, op0, op1), *deps)

        def cp(o, i, *deps, eng="dve"):
            return q.put(eng, lambda e: e.tensor_copy(o, i), *deps)

        def mm(o, l, r, start, stop, *deps, inc=False):
            return q.put("pe", lambda e: e.matmul(o, l, r, start=start, stop=stop, skip_group_check=True),
                         *deps, inc=inc)

        def dma(sem, o, i, *deps, eng="sp"):
            return q.put(eng, lambda e: e.dma_start(o, i), *deps, sem=sem, by=16)

        def split(h, l, x, *deps, hi="act"):
            if hi == "act":
                t = act(h, x, ACT.Copy, *deps)
            else:
                t = cp(h, x, *deps)
            return tt(l, x, h.bitcast(F32), ALU.subtract, t, *deps)

        t_c = dma("d_c", cst[:, :], a["consts"])
        t_x = dma("d_x", X[:, :, :], a["xt"].rearrange("p (k n) -> p k n", k=KD))
        t_p = dma("d_p", prm[:, :], a["params"])

        ready = {}
        state = {"pos": 0, "made": 0, "read": 0}

        def read_unit(u):
            r = wraw[u % RAW]
            ready[("raw", u)] = dma(f"d_w{u % RAW}", r.t[:, :], a["wstream"][u], r.free)

        def make_unit(u):
            r, h, l = wraw[u % RAW], wh[u % SLOTS], wl[u % SLOTS]
            t1 = act(h.t[:, :], r.t[:, :], ACT.Copy, ready[("raw", u)], h.free)
            t2 = tt(l[:, :], r.t[:, :], h.t[:, :].bitcast(F32), ALU.subtract, t1, ready[("raw", u)], h.free)
            r.free = [t1, t2]
            ready[u] = t2

        def ensure(u):
            while state["made"] <= min(u + AHEAD, nunit - 1):
                n = state["made"]
                while state["read"] <= min(n + RAW - 1, nunit - 1):
                    read_unit(state["read"])
                    state["read"] += 1
                make_unit(n)
                state["made"] += 1

        def take(what, n=1):
            while order[state["pos"]] is None:
                skip()
            p = state["pos"]
            assert order[p] == what, (order[p], what)
            u, j = p // NU, p % NU
            assert j + n <= NU
            if j == 0 or u >= state["made"]:
                ensure(u)
            state["pos"] += n
            s = u % SLOTS
            ends = state["pos"] % NU == 0
            return (wh[s].t[:, j * 128:(j + n) * 128], wl[s][:, j * 128:(j + n) * 128], ready[u], ends, wh[s])

        def skip():
            p = state["pos"]
            if p % NU == 0:
                ensure(p // NU)
            state["pos"] += 1
            if state["pos"] % NU == 0:
                wh[(p // NU) % SLOTS].free = [("pe", q.count["pe"])]

        def group(mat, nk, cols, banks, rhs, n=S):
            toks = []
            for k in range(nk):
                xh, xl, dep = rhs(k)
                for c, b in zip(cols, banks):
                    h, l, wd, ends, slot = take((mat, k, c))
                    o = b.t[:, 0:n]
                    last = k == nk - 1
                    mm(o, h, xh, k == 0, False, wd, dep, b.free if k == 0 else None)
                    mm(o, h, xl, False, False)
                    t = mm(o, l, xh, False, last, inc=last or ends)
                    if ends:
                        slot.free = [t]
                    if last:
                        toks.append(t)
            return toks

        nb = [0]

        def banks(n, pool=6):
            got = [bank[(nb[0] + i) % pool] for i in range(n)]
            nb[0] += n
            return got

        def linear(mat, nk, cols, g, rhs, evac, pool=6):
            for c0 in range(0, len(cols), g):
                cc = cols[c0:c0 + g]
                bb = banks(len(cc), pool)
                for c, b, t in zip(cc, bb, group(mat, nk, cc, bb, rhs)):
                    b.free = [evac(c, b.t, t)]

        def token_major(mat, nk, c0, bb, lhs):
            toks = []
            for k in range(nk):
                h, l, wd, ends, slot = take((mat, k, c0), 4)
                xh, xl, dep = lhs(k)
                for i, b in enumerate(bb):
                    ts_ = slice(i * 128, (i + 1) * 128)
                    last = k == nk - 1
                    mm(b.t[:, :], xh[:, ts_], h, k == 0, False, wd, dep, b.free if k == 0 else None)
                    mm(b.t[:, :], xl[:, ts_], h, False, False)
                    t = mm(b.t[:, :], xh[:, ts_], l, False, last, inc=last or (ends and i == 3))
                    if last:
                        toks.append(t)
                if ends:
                    slot.free = [t]
            return toks

        class Ring:
            def __init__(self, stack, name, n, shape, dt=F32, free=()):
                self.b = [Buf(sb(stack, f"{name}{i}", shape, dt), free) for i in range(n)]
                self.n = 0

            def get(self):
                self.n += 1
                return self.b[(self.n - 1) % len(self.b)]

        tmp = Ring(ctx, "tmp", 4, [128, S])
        sqr = Ring(ctx, "sqr", 2, [128, S])

        t_idb = act(identb[:, :], C("ident"), ACT.Copy, t_c)
        act(msb[:, :], C("msb"), ACT.Copy, t_c)
        act(mml[:, :], C("mml"), ACT.Copy, t_c)
        cp(trir[:, :], C("tri"), t_c)
        t_ones = cp(onesr[:, :], C("ones"), t_c)
        t_cb = [("act", q.count["act"]), t_ones]

        class Stats:
            def __init__(self, centred=True):
                self.c = centred
                self.b = bank[6]
                self.n = 0

            def add(self, x, dep):
                s = sqr.get()
                t2 = act(s.t[:, :], x, ACT.Square, dep, s.free)
                first = self.n == 0
                for j in range(4):
                    if self.c:
                        mm(self.b.t[:, j:j + 1], x[:, j * 128:(j + 1) * 128], C("ones")[:, 0:1],
                           first and j == 0, False, dep, t_c, self.b.free if first else None)
                for j in range(4):
                    self.t = mm(self.b.t[:, 4 + j:5 + j], s.t[:, j * 128:(j + 1) * 128], C("ones")[:, 0:1],
                                first and j == 0 and not self.c, False, t2, t_c,
                                self.b.free if first else None, inc=(j == 3))
                s.free = [self.t]
                self.n += 1

            def done(self, n, eps):
                m, v, r, nm = st[:, 0:4], st[:, 4:8], st[:, 8:12], st[:, 12:16]
                inv = 1.0 / n
                if self.c:
                    t = ts(m, self.b.t[:, 0:4], inv, None, ALU.mult, None, self.t)
                    t1 = stt(v, m, -1.0, m, ALU.mult, ALU.mult, t)
                    t1 = stt(v, self.b.t[:, 4:8], inv, v, ALU.mult, ALU.add, t1)
                    t1 = ts(v, v, 0.0, eps, ALU.max, ALU.add, t1)
                else:
                    t1 = ts(v, self.b.t[:, 4:8], inv, eps, ALU.mult, ALU.add, self.t)
                tr = q.put("pool", lambda e: e.tensor_tensor(r, v, C("mhalf")[:, 0:4], ALU.pow), t1, t_c)
                da = tmp.get()
                idb = C("ident").unsqueeze(1).broadcast_to([128, 4, 128])
                t2 = tt(da.t[:, :].rearrange("p (j n) -> p j n", j=4), idb,
                        r.unsqueeze(2).broadcast_to([128, 4, 128]), ALU.mult, tr, da.free)
                ta = mm(bank[6].t[:, :], C("ones"), da.t[:, :], True, True, t2, t1, inc=True)
                da.free = [ta]
                self.tb = None
                if self.c:
                    t3 = stt(nm, m, -1.0, r, ALU.mult, ALU.mult, tr)
                    db = tmp.get()
                    t4 = tt(db.t[:, :].rearrange("p (j n) -> p j n", j=4), idb,
                            nm.unsqueeze(2).broadcast_to([128, 4, 128]), ALU.mult, t3, db.free)
                    self.tb = mm(bank[7].t[:, :], C("ones"), db.t[:, :], True, True, t4, bank[7].free, inc=True)
                    db.free = [self.tb]
                self.ta = ta
                return ta

        def normalise(sx, src, dst, dh, dl, g, b, func=ACT.Identity, free=()):
            toks = []
            for f in range(KD):
                u = tmp.get()
                t = tt(u.t[:, :], src(f), bank[6].t[:, :], ALU.mult, sx.ta, u.free)
                t = tt(u.t[:, :], u.t[:, :], bank[7].t[:, :], ALU.add, t, sx.tb)
                tb = t
                t1 = act(dst(f), u.t[:, :], func, t, free, bias=P(b, f), scale=P(g, f))
                u.free = [t1]
                toks.append(split(dh(f), dl(f), dst(f), t1, free))
            bank[6].free = [tb]
            bank[7].free = [tb]
            return toks

        xa = lambda f: X[:, f, :]
        xh = lambda f: XH[:, f, :]
        xl = lambda f: XL[:, f, :]

        ph = ExitStack()
        Y = sb(ph, "Y", [128, KD, S])
        GH = sb(ph, "GH", [128, KD, S], FR)
        GL = sb(ph, "GL", [128, KD, S], FR)
        PAD = TAPS - 1
        cr = Ring(ph, "cin", 2, [128, PAD + S])
        chr_ = Ring(ph, "cinh", 2, [128, PAD + S], FR)
        clr = Ring(ph, "cinl", 2, [128, PAD + S], FR)
        accr = Ring(ph, "acc", 2, [128, S])
        dgh = Ring(ph, "dgh", 4, [128, 128], FR)
        dgl = Ring(ph, "dgl", 4, [128, 128], FR)
        for b in cr.b:
            b.free = [q.put("dve", lambda e, b=b: e.memset(b.t[:, 0:PAD], 0.0))]

        ensure(0)
        xt = [split(xh(k), xl(k), xa(k), t_x) for k in range(KD)]
        rx = lambda k: (xh(k), xl(k), xt[k])

        s1 = Stats()
        taps = []

        def pe_taps():
            for f, ci, ch, cl, tsp, b, dv in taps:
                for n in range(PE_TAPS):
                    k = TAPS - 1 - n
                    dh_, dl_ = dgh.get(), dgl.get()
                    t1 = act(dh_.t[:, :], C("ident"), ACT.Copy, dh_.free, t_c, t_p, scale=P("dww", f * TAPS + k))
                    t2 = stt(dl_.t[:, :], C("ident"), P("dww", f * TAPS + k), dh_.t[:, :].bitcast(F32), ALU.mult,
                             ALU.subtract, t1, dl_.free)
                    mm(b.t[:, :], dh_.t[:, :], ch.t[:, k:k + S], n == 0, False, t2, tsp, b.free)
                    mm(b.t[:, :], dh_.t[:, :], cl.t[:, k:k + S], False, False)
                    t = mm(b.t[:, :], dl_.t[:, :], ch.t[:, k:k + S], False, n == PE_TAPS - 1, inc=True)
                    dh_.free = [t]
                    dl_.free = [t]
                ch.free = [t]
                cl.free = [t]
                dv(t)
            taps.clear()

        for f in range(8):
            ba, bg = banks(2)
            ta, = group("pw1", KD, [f], [ba], rx)
            tg, = group("pw1", KD, [8 + f], [bg], rx)
            if taps:
                pe_taps()
            sg = tmp.get()
            t = act(sg.t[:, :], bg.t[:, :], ACT.Sigmoid, tg, sg.free, t_p, bias=P("b1", 8 + f))
            bg.free = [t]
            ci, ch, cl = cr.get(), chr_.get(), clr.get()
            tc_ = stt(ci.t[:, PAD:], ba.t[:, :], P("b1", f), sg.t[:, :], ALU.add, ALU.mult, t, ta, ci.free)
            ba.free = [tc_]
            sg.free = [tc_]
            tsp = split(ch.t[:, :], cl.t[:, :], ci.t[:, :], tc_, ch.free, cl.free)
            nv = TAPS - PE_TAPS
            accs = [accr.get(), accr.get()]
            last = [None, None]
            for k in range(nv):
                j = k % 2
                ac = accs[j]
                w = P("dww", f * TAPS + k)
                src = ci.t[:, k:k + S]
                if k == 0:
                    last[j] = ts(ac.t[:, :], src, w, P("dwb", f), ALU.mult, ALU.add, tc_, ac.free)
                elif k == 1:
                    last[j] = ts(ac.t[:, :], src, w, None, ALU.mult, None, tc_, ac.free)
                else:
                    last[j] = stt(ac.t[:, :], src, w, ac.t[:, :], ALU.mult, ALU.add, last[j])
            ci.free = [last[0], last[1], tsp]
            t = tt(Y[:, f, :], accs[0].t[:, :], accs[1].t[:, :], ALU.add, last)
            accs[0].free = [t]
            accs[1].free = [t]
            bt, = banks(1)

            def dv(tp, f=f, bt=bt, t=t):
                t = tt(Y[:, f, :], Y[:, f, :], bt.t[:, :], ALU.add, t, tp)
                bt.free = [t]
                s1.add(Y[:, f, :], t)
            taps.append((f, ci, ch, cl, tsp, bt, dv))
        pe_taps()
        s1.done(D, 1e-5)
        ty = normalise(s1, lambda f: Y[:, f, :], lambda f: Y[:, f, :], lambda f: GH[:, f, :],
                       lambda f: GL[:, f, :], "lng", "lnb", ACT.Silu)

        s2 = Stats()

        def evac_mix(c, b, t):
            u = tmp.get()
            t1 = act(u.t[:, :], b[:, :], ACT.Identity, t, u.free, bias=P("b2", c))
            t2 = stt(xa(c), xa(c), ALPHA, u.t[:, :], ALU.mult, ALU.add, t1)
            u.free = [t2]
            s2.add(xa(c), t2)
            return t1

        linear("pw2", KD, list(range(8)), 4, lambda k: (GH[:, k, :], GL[:, k, :], ty[k]), evac_mix)
        s2.done(D, 1e-5)
        xt = normalise(s2, xa, xa, xh, xl, "mixg0", "mixb0")
        rx = lambda k: (xh(k), xl(k), xt[k])
        ph.close()

        def ffn(layer, xt, over):
            ph = ExitStack()
            HH = sb(ph, f"HH{layer}", [128, FT, S], FR)
            HL = sb(ph, f"HL{layer}", [128, FT, S], FR)
            pth = HH[:, FT - 2:FT, :]
            ptl = HL[:, FT - 2:FT, :]
            tp = []
            for k in range(2):
                pt = tmp.get()
                t = dma(f"d_p{layer}{k}", pt.t[:, :], a["pt"][layer][:, k * S:(k + 1) * S], pt.free)
                tp.append(split(pth[:, k, :], ptl[:, k, :], pt.t[:, :], t, over))
                pt.free = [tp[-1]]
            rx = lambda k: (xh(k), xl(k), xt[k])
            for f0 in range(0, 8, 2):
                cols = [f0, f0 + 1]
                b1, b2 = banks(2), banks(2)
                t1 = group(f"pg{layer}", KD, cols, b1, rx)
                t2 = group(f"pp{layer}", 2, cols, b2, lambda k: (pth[:, k, :], ptl[:, k, :], tp))
                for i, c in enumerate(cols):
                    u, w = tmp.get(), tmp.get()
                    t = act(u.t[:, :], b1[i].t[:, :], ACT.Sigmoid, t1[i], u.free)
                    b1[i].free = [t]
                    t = tt(w.t[:, :], u.t[:, :], b2[i].t[:, :], ALU.mult, t, t2[i], w.free)
                    b2[i].free = [t]
                    u.free = [t]
                    t = stt(xa(c), xa(c), ALPHA, w.t[:, :], ALU.mult, ALU.add, t, xt)
                    w.free = [t]
            tpe = t2[1]
            th = []
            fcw, fcb = f"fcw{layer}", f"fcb{layer}"
            for f in range(FT):
                bu, bg = banks(2)
                tu, = group(f"up{layer}", KD, [f], [bu], rx)
                tg, = group(f"gate{layer}", KD, [f], [bg], rx)
                u = tmp.get()
                w = lambda j: P(fcw, 3 * f + j)
                t = act(u.t[:, :], bg.t[:, :], ACT.Identity, tg, u.free, scale=w(2), bias=P(fcb, f))
                t = stt(u.t[:, 1:S], bg.t[:, 0:S - 1], w(1), u.t[:, 1:S], ALU.mult, ALU.add, t)
                t = stt(u.t[:, 2:S], bg.t[:, 0:S - 2], w(0), u.t[:, 2:S], ALU.mult, ALU.add, t)
                bg.free = [t]
                t = act(u.t[:, :], u.t[:, :], ACT.Silu, t)
                v = tmp.get()
                t = tt(v.t[:, :], u.t[:, :], bu.t[:, :], ALU.mult, t, tu, v.free)
                u.free = [t]
                bu.free = [t]
                t = split(HH[:, f, :], HL[:, f, :], v.t[:, :], t, over, tpe)
                v.free = [t]
                th.append(t)
            s = Stats()

            def evac(c, b, t):
                t = tt(xa(c), xa(c), b[:, :], ALU.add, t)
                s.add(xa(c), t)
                return t

            linear(f"down{layer}", FT, list(range(8)), 1, lambda k: (HH[:, k, :], HL[:, k, :], th[k]), evac)
            s.done(D, 1e-5)
            over = q.last()
            ph.close()
            return s, over

        s3, over = ffn(0, xt, q.last())
        xt = normalise(s3, xa, xa, xh, xl, "fg0", "fb0")

        ph = ExitStack()
        Q = sb(ph, "Q", [128, KD, S])
        K = sb(ph, "K", [128, KD, S])
        pair = {n: Ring(ph, n, 2, [128, S], FR, over) for n in ("qh", "ql", "kh", "kl")}
        V = sb(ph, "V", [128, 4, D])
        rx = lambda k: (xh(k), xl(k), xt[k])
        tq, tk = {}, {}

        def evac_qk(dst, scale, toks):
            def evac(c, b, t):
                toks[c] = act(dst[:, c, :], b[:, :], ACT.Copy, t, over, scale=scale)
                return toks[c]
            return evac

        linear("wq", KD, list(range(8)), 4, rx, evac_qk(Q, 0.125, tq))
        linear("wk", KD, list(range(8)), 4, rx, evac_qk(K, 1.0, tk))
        tv = []
        for half in range(2):
            bb = banks(4)
            for i, t in enumerate(token_major("wv", KD, 4 * half, bb, rx)):
                t = act(V[:, i, half * 512:(half + 1) * 512], bb[i].t[:, :], ACT.Copy, t, over)
                bb[i].free = [t]
                tv.append(t)
        tpx = ("pe", q.count["pe"])
        W4 = [512, 384, 256, 128]
        OFF = [0, 512, 1024, 1280]
        ZB = [(0, 0), (1, 0), (2, 0), (1, 384)]
        SO = [0, 512, 896, 1152]
        mr = Ring(ph, "sbm", 2, [128, 1280])
        shr = Ring(ph, "sbh", 1, [128, 1280], FR)
        slr = Ring(ph, "sbl", 1, [128, 1280], FR)
        ar = Ring(ph, "sba", 1, [128, 1280])
        for r in (mr, shr, slr, ar):
            for b in r.b:
                b.free = over
        split_pair = {}

        def make_pair(hp):
            qh, ql, kh, kl = (pair[n].get() for n in ("qh", "ql", "kh", "kl"))
            t1 = split(qh.t[:, :], ql.t[:, :], Q[:, hp, :], tq[hp], qh.free)
            t2 = split(kh.t[:, :], kl.t[:, :], K[:, hp, :], tk[hp], kh.free)
            split_pair[hp] = (qh, ql, kh, kl, [t1, t2])

        def zap(bs, kb):
            j, o = ZB[kb]
            return bs[j].t[:, o:o + W4[kb]]

        def sb_scores(h):
            hp, r = h // 2, slice(64 * (h % 2), 64 * (h % 2) + 64)
            bs = [bank[3 * (h % 2) + i] for i in range(3)]
            if h % 2 == 0:
                make_pair(hp)
            qh, ql, kh, kl, tsp = split_pair[hp]
            toks = [None] * 4
            for kb in range(4):
                z = zap(bs, kb)
                ks, qs = slice(kb * 128, kb * 128 + 128), slice(kb * 128, S)
                fr = bs[ZB[kb][0]].free
                mm(z, kh.t[r, ks], qh.t[r, qs], kb != 3, False, tsp, fr)
                mm(z, kh.t[r, ks], ql.t[r, qs], False, False)
                mm(z, kl.t[r, ks], qh.t[r, qs], False, False)
                toks[kb] = mm(z[:, 0:128], identb[:, :], msb[:, :], False, False, t_cb, inc=True)
            qh.free = kh.free = [toks[3]]
            return bs, toks

        def sb_soft(h, bs, zt):
            m, sh, sl = mr.get(), shr.get(), slr.get()
            tm = []
            for kb in range(4):
                tm.append(act(m.t[:, SO[kb]:SO[kb] + W4[kb]], zap(bs, kb), ACT.Abs, zt[3], m.free))
            t = act(m.t[:, :], m.t[:, :], ACT.Exp, tm, scale=-1.0)
            t = act(m.t[:, :], m.t[:, :], ACT.Ln, t, t_c, bias=1.0)
            tz = []
            for kb in range(4):
                c = slice(SO[kb], SO[kb] + W4[kb])
                tz.append(stt(m.t[:, c], zap(bs, kb), 0.0, m.t[:, c], ALU.max, ALU.add, t))
            t1 = cp(sh.t[:, :], m.t[:, :], tz, sh.free)
            t2 = tt(sl.t[:, :], m.t[:, :], sh.t[:, :].bitcast(F32), ALU.subtract, t1, sl.free)
            m.free = [t1, t2]
            return sh, sl, tz, t2

        def sb_sum(bs, so):
            sh, sl, tz, td = so
            toks = []
            for kb in range(4):
                for k2 in range(kb, 4):
                    z = zap(bs, kb)[:, 128 * (k2 - kb):]
                    c = slice(SO[k2], SO[k2] + W4[k2])
                    l = trir if k2 == kb else onesr
                    mm(z, l[:, :], sh.t[:, c], False, False, td, tz, t_cb)
                    t = mm(z, l[:, :], sl.t[:, c], False, k2 == 3, inc=k2 == 3)
                toks.append(t)
            sh.free = [t]
            sl.free = [t]
            return toks

        def sb_out(h, bs, zt):
            am = ar.get()
            te = []
            for kb in range(4):
                te.append(act(am.t[:, SO[kb]:SO[kb] + W4[kb]], zap(bs, kb), ACT.Exp, zt[3], am.free))
            for b in bs:
                b.free = [te[-1]]
            hp, r = h // 2, slice(64 * (h % 2), 64 * (h % 2) + 64)
            ob = bank[6 + hp % 2]
            for kb in range(4):
                t = mm(ob.t[r, kb * 128:S], V[:, kb, h * 64:h * 64 + 64], am.t[:, SO[kb]:SO[kb] + W4[kb]],
                       kb == 0, kb == 3, te[kb], tv, ob.free if h % 2 == 0 else None, inc=kb == 3)
            am.free = [t]
            if h % 2:
                u = tmp.get()
                t = act(u.t[:, :], ob.t[:, :], ACT.Copy, t, u.free)
                ob.free = [t]
                t = split(xh(hp), xl(hp), u.t[:, :], t, tpx, hi="dve")
                u.free = [t]
                return t

        to = []
        onr = sb(ph, "onneg", [128, 128], FR)
        t_on = ts(onr[:, :], C("ones"), -1.0, None, ALU.mult, None, over)
        onesr_pos, onesr = onesr, onr
        t_cb = t_cb + [t_on]
        nxt = sb_scores(0)
        for h in range(16):
            cur = nxt
            so = sb_soft(h, *cur)
            if h < 15:
                nxt = sb_scores(h + 1)
            zt = sb_sum(cur[0], so)
            t = sb_out(h, cur[0], zt)
            if h % 2:
                to.append(t)
        s4 = Stats()

        def evac_wo(c, b, t):
            t = stt(xa(c), xa(c), ALPHA, b[:, :], ALU.mult, ALU.add, t)
            s4.add(xa(c), t)
            return t

        linear("wo", KD, list(range(8)), 1, lambda k: (xh(k), xl(k), to[k]), evac_wo)
        s4.done(D, 1e-5)
        over = q.last()
        ph.close()
        xt = normalise(s4, xa, xa, xh, xl, "mixg1", "mixb1", free=over)
        s5, over = ffn(1, xt, over)
        xt = normalise(s5, xa, xa, xh, xl, "fg1", "fb1")

        ph = ExitStack()
        cosT = sb(ph, "cosT", [128, S])
        sinT = sb(ph, "sinT", [128, S])
        ang, rr, kk = tmp.get(), tmp.get(), tmp.get()
        posi = rr.t[:, :].bitcast(I32)
        t = dma("d_pos", posi, a["pos"].partition_broadcast(128), rr.free)
        t = cp(ang.t[:, :], posi, t, ang.free)
        rr.free = [t]
        t = ts(ang.t[:, :], ang.t[:, :], C("invf"), None, ALU.mult, None, t)
        MAGIC = 12582912.0
        TP1, TP2, TP3 = 6.28125, 0.0019340515136718750, 1.2556659146679e-06
        for dst, quarter, shift in ((sinT, 0.0, 0.0), (cosT, 0.25, 1.5707963267948966)):
            t1 = ts(kk.t[:, :], ang.t[:, :], 0.15915494309189535, quarter, ALU.mult, ALU.add, t, kk.free)
            t1 = ts(kk.t[:, :], kk.t[:, :], MAGIC, None, ALU.add, None, t1)
            t1 = ts(kk.t[:, :], kk.t[:, :], -MAGIC, None, ALU.add, None, t1)
            t1 = stt(rr.t[:, :], kk.t[:, :], -TP1, ang.t[:, :], ALU.mult, ALU.add, t1, rr.free)
            t1 = stt(rr.t[:, :], kk.t[:, :], -TP2, rr.t[:, :], ALU.mult, ALU.add, t1)
            t1 = stt(rr.t[:, :], kk.t[:, :], -TP3, rr.t[:, :], ALU.mult, ALU.add, t1)
            if shift:
                t1 = ts(rr.t[:, :], rr.t[:, :], shift, None, ALU.add, None, t1)
            t1 = ts(rr.t[:, :], rr.t[:, :], 3.1415925, -3.1415925, ALU.min, ALU.max, t1)
            t2 = act(dst[:, :], rr.t[:, :], ACT.Sin, t1, over)
            rr.free = [t2]
            kk.free = [t1]
        t_rope = ts(sinT[:, :], sinT[:, :], C("sgn"), None, ALU.mult, None, t2)
        ang.free = [t_rope]

        R128 = slice(0, 128)
        wgu = sb(ph, "wgu", [128, 256])
        gq = sb(ph, "gq", [128, 2, S])
        gk = sb(ph, "gk", [128, 2, S])
        gv = sb(ph, "gv", [128, 4, S])
        gates = sb(ph, "gates", [128, 8, S])
        lab = sb(ph, "lab", [128, 2, S])
        eb = sb(ph, "eb", [128, 2, S])
        PT = sb(ph, "PT", [128, 4, S])
        ket = PT[:, 0:2, :].rearrange("p a (b n) -> p (a b) n", b=2)
        atm = [PT[:, 2 + i, :] for i in range(2)]
        stt_ = sb(ph, "states", [128, 2, 8, 128])
        cq = sb(ph, "cq", [128, 2, S])
        ckv = sb(ph, "ckv", [128, S])
        kpa = sb(ph, "kpa", [128, S])
        kpb = sb(ph, "kpb", [128, S])
        cqh, cql, ckh, ckl = XH[:, 4:6, :], XL[:, 4:6, :], XH[:, 6, :], XL[:, 6, :]
        qr, kr = eb, kpb
        rmq = Ring(ph, "rmq", 2, [128, S], free=over)
        qn = sb(ph, "qn", [128, S])
        kn = sb(ph, "kn", [128, S])
        qrh = sb(ph, "qrh", [128, S])
        krh = sb(ph, "krh", [128, S])
        sm = sb(ph, "sm", [128, 64])

        def rms_rows(pairs, n, gdeps=()):
            b = bank[7]
            for i, (x, rows, dep) in enumerate(pairs):
                s = sqr.get()
                t = act(s.t[rows, :], x, ACT.Square, dep, s.free)
                t = mm(b.t[:, :], C("ones", rows), s.t[rows, :], i == 0, i == len(pairs) - 1, t,
                       b.free if i == 0 else None, inc=True)
                s.free = [t]
            r = rmq.get()
            t = act(r.t[:, :], b.t[:, :], ACT.Ln, t, r.free, t_c, scale=1.0 / n, bias=C("epsr"))
            b.free = [t]
            t = act(r.t[:, :], r.t[:, :], ACT.Exp, t, scale=-0.5)
            return r, t

        for layer in range(2):
            L = str(layer)
            t_wgu = dma(f"d_g{layer}", wgu[64:80, :], a["wgu"][layer], over if layer == 0 else q.last())
            s = Stats(centred=False)
            for f in range(KD):
                s.add(xa(f), xt[f])
            tprev = ("pe", q.count["pe"])
            s.done(D, 1e-6)
            ht = []
            for f in range(KD):
                u = tmp.get()
                t = stt(u.t[:, :], xa(f), P("ng" + L, f), bank[6].t[:, :], ALU.mult, ALU.mult, s.ta, u.free)
                t1 = split(xh(f), xl(f), u.t[:, :], t, tprev, xt[f])
                u.free = [t1]
                ht.append(t1)
            bank[6].free = [t]
            rh = lambda k: (xh(k), xl(k), ht[k])
            fl = over if layer == 0 else q.last()
            atf = [[q.put("dve", lambda e, i=i: e.memset(atm[i], 0.0), fl)] for i in range(2)]
            lrb = tmp.get()
            lr = lrb.t
            got = {}

            def to_sbuf(dst):
                def evac(c, b, t):
                    t = act(dst(c), b[:, :], ACT.Copy, t, fl)
                    got[c] = t
                    return t
                return evac

            def evac0(c, b, t):
                if c == 0:
                    act(kpa[0:64, :], b[0:64, :], ACT.Copy, t, fl)
                    t1 = act(kpa[64:128, :], b[0:64, :], ACT.Copy, t, fl)
                    t2 = cp(lr[64:80, :], b[64:80, :], t, t1, lrb.free)
                    for r0, r1 in ((0, 32), (32, 0), (64, 32), (96, 0)):
                        t2 = cp(kpb[r0:r0 + 32, :], b[r1:r1 + 32, :], t, t1, fl)
                    got[c] = [t1, t2]
                    return t2
                dst = ckv[:, :] if c == 1 else cq[:, c - 2, :]
                return to_sbuf(lambda c: dst)(c, b, t)

            linear("in" + L, KD, [0, 1, 2, 3], 4, rh, evac0)
            linear("in" + L, KD, [4, 5, 6, 7], 4, rh,
                   to_sbuf(lambda c: gq[:, c - 4, :] if c < 6 else gk[:, c - 6, :]))
            bb = banks(4)
            tgv = []
            for i, t in enumerate(token_major("in" + L, KD, 8, bb, rh)):
                t = act(gv[:, i, :], bb[i].t[:, :], ACT.Copy, t, fl)
                bb[i].free = [t]
                tgv.append(t)

            tb, teb = [None, None], [None, None]
            for i in range(2):
                b, = banks(1)
                t = mm(b.t[:, :], wgu[64:80, i * 128:(i + 1) * 128], lr[64:80, :], True, True, got[0], t_wgu,
                       b.free, inc=True)
                lrb.free = [t]
                u, v = tmp.get(), tmp.get()
                t = ts(u.t[:, :], b.t[:, :], P("bgg" + L, i), None, ALU.add, None, t, u.free)
                b.free = [t]
                t = stt(v.t[:, :], u.t[:, :], -1.0, u.t[:, :], ALU.mult, ALU.min, t, v.free)
                t = act(v.t[:, :], v.t[:, :], ACT.Exp, t)
                t = act(v.t[:, :], v.t[:, :], ACT.Ln, t, bias=1.0)
                t = stt(u.t[:, :], u.t[:, :], 0.0, v.t[:, :], ALU.min, ALU.subtract, t)
                v.free = [t]
                t = q.put("dve", lambda e, i=i, u=u: e.tensor_tensor_scan(
                    lab[:, i, :], C("scan"), u.t[:, :], 0.0, ALU.mult, ALU.add), t, fl)
                u.free = [t]
                tb[i] = t
                teb[i] = act(eb[:, i, :], lab[:, i, :], ACT.Exp, t, fl, scale=0.0625)
            tqd, tki, tke = [None] * 2, [None] * 2, [None] * 2
            for i in range(2):
                tqd[i] = stt(gq[:, i, :], gq[:, i, :], 0.125, eb[:, i, :], ALU.mult, ALU.mult, got[4 + i], teb[i])
                u, v = tmp.get(), tmp.get()
                t = act(u.t[:, :], lab[:, i, :], ACT.Exp, tb[i], u.free, scale=-0.0625)
                lc = lab[:, i, :].rearrange("p (c n) -> p c n", c=8)
                bl = lc[:, :, 63:64].broadcast_to([128, 8, 64])
                t2 = tt(v.t[:, :].rearrange("p (c n) -> p c n", c=8), bl, lc, ALU.subtract, tb[i], v.free)
                t2 = act(v.t[:, :], v.t[:, :], ACT.Exp, t2, scale=0.0625)
                t2 = tt(v.t[:, :], v.t[:, :], gk[:, i, :], ALU.mult, t2, got[6 + i])
                tki[i] = tt(gk[:, i, :], gk[:, i, :], u.t[:, :], ALU.mult, t, t2)
                u.free = [tki[i]]
                b, = banks(1)
                for j in range(4):
                    o, x = b.t[:, j * 128:(j + 1) * 128], v.t[:, j * 128:(j + 1) * 128]
                    t3 = q.put("pe", lambda e, o=o, x=x: e.transpose(o, x, C("ident")), t2, b.free, inc=j == 3)
                v.free = [t3]
                t4 = cp(ket[:, :, i * 128:(i + 1) * 128], b.t[:, :].rearrange("p (j n) -> p j n", j=4), t3, fl)
                b.free = [t4]
                tke[i] = t4

            tst = [[None] * 8 for _ in range(2)]
            for i in range(2):
                tst[i][0] = q.put("pool", lambda e, i=i: e.memset(stt_[:, i, 0, :], 0.0), fl)
                for n in range(7):
                    if n % 4 == 0:
                        be, bo = banks(2)
                        for m in range(n, min(n + 4, 7)):
                            r = slice(64 * (m % 2), 64 * (m % 2) + 64)
                            b, c = (be, bo)[m % 2], (m % 4) // 2 * 256
                            t = mm(b.t[:, c:c + 256], ket[r, m // 2, i * 128:(i + 1) * 128],
                                   gv[r, m // 2, i * 256:(i + 1) * 256], True, True, tke[i], tgv, b.free, inc=True)
                    b, c = (be, bo)[n % 2], (n % 4) // 2 * 256
                    o = b.t[:, c:c + 256]
                    for hh in range(2):
                        rr_ = slice(64 * hh, 64 * hh + 64)
                        t2 = stt(stt_[rr_, i, n + 1, :], stt_[rr_, i, n, :], eb[rr_, i, 64 * n + 63:64 * n + 64],
                                 o[rr_, 128 * hh:128 * hh + 128], ALU.mult, ALU.add, t, tst[i][n], teb[i], fl)
                        if hh == 0:
                            t1 = t2
                    b.free = [t2]
                    tst[i][n + 1] = [t1, t2]

            def evac_gate(c, b, t):
                t = act(gates[:, c - 12, :], b[:, :], ACT.Silu, t, fl)
                got[c] = t
                return t

            linear("in" + L, KD, list(range(12, 20)), 1, rh, evac_gate)
            tx_free = ("pe", q.count["pe"])
            mt = {}

            for h in range(4):
                i, r = h // 2, slice(64 * (h % 2), 64 * (h % 2) + 64)
                at = atm[h % 2]
                b, = banks(1)
                for p in range(4):
                    c = slice(p * 128, (p + 1) * 128)
                    t = mm(b.t[:, c], gk[r, i, c], gq[r, i, c], True, True, tki[i], tqd[i],
                           b.free if p == 0 else None, inc=p == 3)
                ta_ = []
                for p in range(4):
                    c = slice(p * 128, (p + 1) * 128)
                    ta_.append(q.put("dve", lambda e, at=at, b=b, c=c: e.copy_predicated(
                        at[:, c], C("mgl").bitcast(I32), b.t[:, c]), t, atf[h % 2]))
                b.free = [ta_[-1]]
                b, = banks(1)
                for p in range(4):
                    c = slice(p * 128, (p + 1) * 128)
                    mm(b.t[:, c], gv[:, p, h * 128:(h + 1) * 128], at[:, c], p == 0, False, ta_, tgv,
                       b.free if p == 0 else None)
                for n in range(8):
                    c = slice(n * 64, n * 64 + 64)
                    t = mm(b.t[:, c], stt_[r, i, n, :], gq[r, i, c], False, n == 7, tst[i], inc=n == 7)
                atf[h % 2] = [t]
                rs, t1 = rms_rows([(b.t[:, :], R128, t)], 128)
                u = tmp.get()
                t = stt(u.t[:, :], b.t[:, :], P("glag" + L), rs.t[:, :], ALU.mult, ALU.mult, t1, u.free)
                b.free = [t]
                rs.free = [t]
                t = tt(u.t[:, :], u.t[:, :], gates[:, h, :], ALU.mult, t, got[12 + h])
                mt[h] = split(xh(h), xl(h), u.t[:, :], t, tx_free)
                u.free = [mt[h]]

            rs, t = rms_rows([(cq[:, 0, :], R128, got[2]), (cq[:, 1, :], R128, got[3])], 256)
            tcq = []
            for k in range(2):
                t1 = stt(cq[:, k, :], cq[:, k, :], P("mqg" + L, k), rs.t[:, :], ALU.mult, ALU.mult, t)
                tcq.append(split(cqh[:, k, :], cql[:, k, :], cq[:, k, :], t1, tx_free))
            rs.free = [t1]
            rs, t = rms_rows([(ckv[:, :], R128, got[1])], 128)
            t1 = stt(ckv[:, :], ckv[:, :], P("mkvg" + L), rs.t[:, :], ALU.mult, ALU.mult, t)
            rs.free = [t1]
            tck = split(ckh, ckl, ckv[:, :], t1, tx_free)

            tla = q.last()
            qraw = [gq[:, 0, :], gq[:, 1, :], gk[:, 0, :], gk[:, 1, :]]
            ra, rb = cq, eb

            def evac_q(c, b, t):
                dst = qraw[c] if c < 4 else (lab[:, c - 4, :] if c < 6 else rb[:, c - 6, :])
                t = act(dst, b[:, :], ACT.Copy, t, tla)
                got[("q", c)] = t
                return t

            linear("uq" + L, 2, list(range(8)), 1, lambda k: (cqh[:, k, :], cql[:, k, :], tcq[k]), evac_q)
            kraw = [stt_[:, 0, 0:4, :], stt_[:, 0, 4:8, :], stt_[:, 1, 0:4, :], stt_[:, 1, 4:8, :]]
            kraw = [x.rearrange("p c n -> p (c n)") for x in kraw]

            def evac_k(c, b, t):
                t = act(kraw[c], b[:, :], ACT.Copy, t, tla)
                got[("k", c)] = t
                return t

            rk = lambda k: (ckh, ckl, tck)
            linear("ukv" + L, 1, list(range(4)), 1, rk, evac_k)
            bb = banks(4)
            tmv = []
            for i, t in enumerate(token_major("ukv" + L, 1, 4, bb, rk)):
                t = act(gv[:, i, :], bb[i].t[:, :], ACT.Copy, t, tla)
                bb[i].free = [t]
                tmv.append(t)

            def rope(dst, xa_, xb_, ga, gb, deps, free):
                u, v = tmp.get(), tmp.get()
                t1 = stt(u.t[:, :], xa_, ga, cosT[:, :], ALU.mult, ALU.mult, deps, u.free, t_rope)
                t2 = stt(v.t[:, :], xb_, gb, sinT[:, :], ALU.mult, ALU.mult, deps, v.free)
                t3 = tt(dst, u.t[:, :], v.t[:, :], ALU.add, t1, t2, free)
                u.free = [t3]
                v.free = [t3]
                return t3

            tkr = rope(kr[:, :], kpa[:, :], kpb[:, :], P("kga" + L), P("kgb" + L), got[0], fl)
            tqr = [rope(qr[:, i, :], lab[:, i, :], rb[:, i, :], P("qga" + L), P("qgb" + L),
                        [got[("q", 4 + i)], got[("q", 6 + i)]], fl) for i in range(2)]

            SC = 192 ** -0.5
            hfree = fl
            ptf = tla
            for h in range(4):
                r = slice(64 * (h % 2), 64 * (h % 2) + 64)
                rs, t = rms_rows([(qraw[h], R128, got[("q", h)]), (lab[r, h // 2, :], r, got[("q", 4 + h // 2)])], 192)
                t1 = stt(qn[:, :], qraw[h], P("qgn" + L), rs.t[:, :], ALU.mult, ALU.mult, t, hfree)
                t2 = tt(qrh[r, :], qr[r, h // 2, :], rs.t[r, :], ALU.mult, t, tqr, hfree)
                rs.free = [t2]
                rs, t = rms_rows([(kraw[h], R128, got[("k", h)]), (kpa[0:64, :], slice(0, 64), got[0])], 192)
                t3 = stt(kn[:, :], kraw[h], P("kgn" + L), rs.t[:, :], ALU.mult, ALU.mult, t, hfree)
                t4 = tt(krh[r, :], kr[r, :], rs.t[r, :], ALU.mult, t, tkr, hfree)
                rs.free = [t4]
                tqk = [t1, t2, t3, t4]
                tpt = []
                for qb in range(4):
                    n = 128 * (qb + 1)
                    qs = slice(qb * 128, qb * 128 + 128)
                    b, = banks(1)
                    mm(b.t[:, 0:n], qn[:, qs], kn[:, 0:n], True, False, tqk, b.free)
                    mm(b.t[:, 0:n], qrh[r, qs], krh[r, 0:n], False, False)
                    t = mm(b.t[:, qs], identb[:, :], mml[:, :], False, True, t_cb, inc=True)
                    j = 4 * ((4 * h + qb) % 4)
                    mx, nm, sumr, rc = (sm[:, j + i_ * 16:j + i_ * 16 + 1] for i_ in range(4))
                    t = q.put("dve", lambda e, mx=mx, b=b, n=n: e.reduce_max(mx, b.t[:, 0:n], AX.X), t, fl)
                    t = ts(nm, mx, -SC, None, ALU.mult, None, t)
                    p = tmp.get()
                    t = act(p.t[:, 0:n], b.t[:, 0:n], ACT.Exp, t, p.free, bias=nm, scale=SC, accum=sumr)
                    b.free = [t]
                    t = q.put("dve", lambda e, rc=rc, sumr=sumr: e.reciprocal(rc, sumr), t)
                    t = ts(p.t[:, 0:n], p.t[:, 0:n], rc, None, ALU.mult, None, t)
                    b, = banks(1)
                    for kb in range(qb + 1):
                        o, x = b.t[:, kb * 128:(kb + 1) * 128], p.t[:, kb * 128:(kb + 1) * 128]
                        t1 = q.put("pe", lambda e, o=o, x=x: e.transpose(o, x, C("ident")), t, b.free, inc=kb == qb)
                    p.free = [t1]
                    t = act(PT[:, 0:qb + 1, qs], b.t[:, 0:n].rearrange("p (k n) -> p k n", n=128), ACT.Copy, t1, ptf)
                    b.free = [t]
                    tpt.append(t)
                hfree = [("pe", q.count["pe"])]
                b, = banks(1)
                for kb in range(4):
                    t = mm(b.t[:, kb * 128:S], gv[:, kb, h * 128:(h + 1) * 128], PT[:, kb, kb * 128:S], kb == 0, kb == 3,
                           tpt, tmv, b.free if kb == 0 else None, inc=kb == 3)
                ptf = [t]
                u = tmp.get()
                t = tt(u.t[:, :], b.t[:, :], gates[:, 4 + h, :], ALU.mult, t, got[16 + h], u.free)
                b.free = [t]
                mt[4 + h] = split(xh(4 + h), xl(4 + h), u.t[:, :], t, tx_free)
                u.free = [mt[4 + h]]

            xn = [None] * KD

            def evac_out(c, b, t):
                t = tt(xa(c), xa(c), b[:, :], ALU.add, t)
                xn[c] = t
                if layer == 1:
                    dma("d_o", a["o"][:, c * S:(c + 1) * S], xa(c), t)
                return t

            linear("out" + L, KD, list(range(8)), 1, lambda k: (xh(k), xl(k), mt[k]), evac_out)
            xt = xn
        ph.close()

        names = sorted({s for s in q.count})
        sems = {n: ctx.enter_context(nc.semaphore("s_" + n)) for n in names}
        block = ctx.enter_context(nc.Block())

        @block.sync
        def _(e):
            q.emit("sp", e, sems)
            e.wait_ge(sems["d_o"], q.count["d_o"])

        @block.tensor
        def _(e):
            q.emit("pe", e, sems)

        @block.scalar
        def _(e):
            q.emit("act", e, sems)

        @block.vector
        def _(e):
            q.emit("dve", e, sems)

        @block.gpsimd
        def _(e):
            q.emit("pool", e, sems)


def lay_out(x):
    import numpy as np

    f = {k: np.asarray(v) for k, v in x.items()}
    mats = {"pw1": f["a_pw1_w"][0], "pw2": f["a_pw2_w"][0], "wq": f["b_wq"][0], "wk": f["kv_wk"], "wv": f["kv_wv"],
            "wo": f["b_wo"][0]}
    for i in range(2):
        mats[f"up{i}"] = f["ffn_w_up"][i]
        mats[f"gate{i}"] = f["ffn_w_gate"][i]
        mats[f"down{i}"] = f["ffn_w_down"][i]
        mats[f"pg{i}"] = f["ple_w_gate"][i]
        mats[f"pp{i}"] = f["ple_w_proj"][i]
        w = f["w_in_2"][i]
        edges = [0, 256, 512, 1024, 1040, 1552, 1808, 1936, 2000, 2512]
        gq, gk, gv, lr, gg, cq, ck, kp, mg = (w[:, a:b] for a, b in zip(edges, edges[1:]))
        mats[f"in{i}"] = np.concatenate([kp, lr, np.zeros((D, 48), w.dtype), ck, cq, gq, gk, gv, gg, mg], 1)
        w = f["w_uq_2"][i].reshape(256, 4, 192)
        r, s = w[:, :, 128:192], np.concatenate([w[:, :, 160:192], w[:, :, 128:160]], 2)
        mats[f"uq{i}"] = np.concatenate([w[:, :, 0:128].reshape(256, 512), r.reshape(256, 256), s.reshape(256, 256)], 1)
        w = f["w_ukv_2"][i].reshape(128, 4, 256)
        mats[f"ukv{i}"] = np.concatenate([w[:, :, 0:128].reshape(128, 512), w[:, :, 128:256].reshape(128, 512)], 1)
        mats[f"out{i}"] = f["w_out_2"][i]
    order = weight_order()
    ws = np.zeros((len(order) // NU, 128, NU * 128), np.float32)
    for n, w in enumerate(order):
        if w is not None:
            m, k, c = w
            ws[n // NU, :, (n % NU) * 128:(n % NU + 1) * 128] = mats[m][k * 128:(k + 1) * 128, c * 128:(c + 1) * 128]

    at, npar = param_order()
    pr = np.zeros((128, npar), np.float32)

    def put(name, v):
        v = v.reshape(-1, 128).T
        pr[:, at[name]:at[name] + v.shape[1]] = v

    put("b1", f["a_pw1_b"][0])
    put("dww", np.ascontiguousarray(f["a_dw_w"][0].reshape(TAPS, 8, 128).transpose(1, 0, 2)))
    put("dwb", f["a_dw_b"][0])
    put("lng", f["a_ln_g"][0])
    put("lnb", f["a_ln_b"][0])
    put("b2", f["a_pw2_b"][0])
    for i in range(2):
        put(f"mixg{i}", f["ln_mix_g"][i])
        put(f"mixb{i}", f["ln_mix_b"][i])
        put(f"fcw{i}", np.ascontiguousarray(f["ffn_conv_w"][i].reshape(3, FT, 128).transpose(1, 0, 2)))
        put(f"fcb{i}", f["ffn_conv_b"][i])
        put(f"fg{i}", f["ln_ffn_g"][i])
        put(f"fb{i}", f["ln_ffn_b"][i])
        put(f"ng{i}", f["norm_g_2"][i])
        put(f"bgg{i}", f["b_gla_gate_2"][i])
        put(f"glag{i}", f["gla_norm_g_2"][i])
        put(f"mqg{i}", f["mla_q_norm_g_2"][i])
        put(f"mkvg{i}", f["mla_kv_norm_g_2"][i])
        for c, g in (("q", f["q_head_g_2"][i]), ("k", f["k_head_g_2"][i])):
            put(f"{c}gn{i}", g[0:128])
            a, b = g[128:160], g[160:192]
            put(f"{c}ga{i}", np.concatenate([a, b, a, b]))
            put(f"{c}gb{i}", np.concatenate([b, a, b, a]))

    def turn(v, k):
        return np.ascontiguousarray(v.T.reshape(k, 128, S).transpose(1, 0, 2).reshape(128, k * S))

    return {"wstream": ws, "params": pr, "xt": turn(f["x"][0], KD),
            "pt": np.stack([turn(f["p"][i, 0], 2) for i in range(2)]),
            "pos": np.ascontiguousarray(f["positions_2"]), "wgu": np.ascontiguousarray(f["w_gla_gate_up_2"])}


def constants():
    import numpy as np

    c = np.zeros((128, NCONST), np.float32)

    def put(name, v):
        o, n = CONST[name]
        c[:, o:o + n] = v

    i, j = np.meshgrid(np.arange(128), np.arange(128), indexing="ij")
    put("ident", i == j)
    put("ones", 1.0)
    put("tri", np.where(i >= j, -1.0, 0.0))
    put("msb", np.where(i >= j, NEG, 0.0))
    put("mml", np.where(j > i, NEG, 0.0))
    put("mgl", (i <= j) & (i // 64 == j // 64))
    put("scan", np.arange(512)[None, :] % 64 != 0)
    p = np.arange(128)[:, None]
    put("invf", np.float32(10000.0) ** (-(2.0 * (p % 32)).astype(np.float32) / np.float32(64)))
    put("sgn", np.where(p % 64 < 32, -1.0, 1.0))
    put("mhalf", -0.5)
    put("one", 1.0)
    put("epsr", 1e-6)
    return c


def kernel(**inputs):
    import numpy as _np
    import concourse.bacc as _bacc
    from concourse import mybir as _mybir
    from concourse.bass_utils import run_bass_kernel_spmd as _run

    nc = _bacc.Bacc("TRN2", target_bir_lowering=False, num_devices=1)
    arrays = lay_out(inputs)
    arrays["consts"] = constants()
    aps = {}
    for name in sorted(arrays):
        v = arrays[name]
        aps[name] = nc.dram_tensor(f"in_{name}", v.shape, _mybir.dt.from_np(v.dtype), kind="ExternalInput").ap()
    aps["o"] = nc.dram_tensor("out_0", (128, KD * S), _mybir.dt.float32, kind="ExternalOutput").ap()
    build(nc, aps, aps["o"])
    r = _run(nc, [{f"in_{n}": arrays[n] for n in arrays}], core_ids=[0])
    o = _np.asarray(r.results[0]["out_0"])
    return _np.ascontiguousarray(o.reshape(128, KD, S).transpose(2, 1, 0).reshape(1, S, D))
```

```python
from contextlib import ExitStack

import concourse.bass as bass
from concourse import mybir

ALU = mybir.AluOpType
ACT = mybir.ActivationFunctionType
AX = mybir.AxisListType
F32 = mybir.dt.float32
FR = mybir.dt.float32r
BF = mybir.dt.bfloat16
I32 = mybir.dt.int32

S = 512
D = 1024
KD = 8
FT = 22
NU = 8
RAW, SLOTS, AHEAD = 3, 4, 3
ALPHA = 4.0 ** 0.25
TAPS = 31
PE_TAPS = 9
POOL_TAPS = 8
NEG = -1e30
LNEXP = 6


def grouped(mat, nk, cols, g):
    out = []
    for c0 in range(0, len(cols), g):
        out += [(mat, k, c) for k in range(nk) for c in cols[c0:c0 + g]]
    return out


def ffn_order(layer):
    out = []
    for f in range(FT):
        out += [(f"up{layer}", k, f) for k in range(KD)] + [(f"gate{layer}", k, f) for k in range(KD)]
    return out


def weight_order():
    o = []

    def align():
        while len(o) % 4:
            o.append(None)

    for f in range(8):
        o.extend([("pw1", k, f) for k in range(KD)] + [("pw1", k, 8 + f) for k in range(KD)])
    o += grouped("pw2", KD, list(range(8)), 4)
    for layer in range(2):
        if layer == 1:
            o += grouped("wq", KD, list(range(8)), 4)
            o += grouped("wk", KD, list(range(8)), 4)
            align()
            for half in range(2):
                o += [("wv", k, 4 * half + c) for k in range(KD) for c in range(4)]
            o += grouped("wo", KD, list(range(8)), 1)
        for f0 in range(0, 8, 4):
            o += grouped(f"pg{layer}", KD, list(range(f0, f0 + 4)), 4)
            o += grouped(f"pp{layer}", 2, list(range(f0, f0 + 4)), 1)
        o += ffn_order(layer)
        o += grouped(f"down{layer}", FT, list(range(8)), 1)
    for layer in range(2):
        align()
        o += grouped(f"in{layer}", KD, list(range(4)), 4)
        o += grouped(f"in{layer}", KD, list(range(12, 20)), 4)
        align()
        o += [(f"in{layer}", k, 8 + c) for k in range(KD) for c in range(4)]
        o += grouped(f"in{layer}", KD, list(range(4, 8)), 4)
        o += grouped(f"uq{layer}", 2, [4, 5, 6, 7, 0, 1, 2, 3], 4)
        o += grouped(f"ukv{layer}", 1, list(range(4)), 4)
        align()
        o += [(f"ukv{layer}", 0, 4 + c) for c in range(4)]
        o += grouped(f"out{layer}", KD, list(range(8)), 4)
    while len(o) % NU:
        o.append(None)
    return o


def param_order():
    o = [("b1", 16), ("dww", 8 * TAPS), ("dwb", 8), ("lng", 8), ("lnb", 8), ("b2", 8)]
    for i in range(2):
        o += [(f"mixg{i}", 8), (f"mixb{i}", 8), (f"fcw{i}", 3 * FT), (f"fcb{i}", FT),
              (f"fg{i}", 8), (f"fb{i}", 8), (f"ng{i}", 8), (f"bgg{i}", 2), (f"glag{i}", 1),
              (f"mqg{i}", 2), (f"mkvg{i}", 1), (f"qgn{i}", 1), (f"qga{i}", 1), (f"qgb{i}", 1),
              (f"kgn{i}", 1), (f"kga{i}", 1), (f"kgb{i}", 1)]
    at, n = {}, 0
    for name, w in o:
        at[name] = n
        n += w
    return at, n


CONST = {"ident": (0, 128), "ones": (128, 128), "tri": (256, 128), "msb": (384, 128), "mml": (512, 128),
         "mgl": (640, 128), "scan": (768, 512), "invf": (1280, 1), "sgn": (1281, 1), "mhalf": (1282, 8),
         "one": (1290, 1), "epsr": (1291, 1), "lnsc": (1292, 1)}
NCONST = 1293


class Queue:

    def __init__(self):
        self.items = {e: [] for e in ("pe", "act", "dve", "pool", "sp")}
        self.count = {}

    def put(self, eng, fn, *deps, inc=True, sem=None, by=1):
        sem = sem or eng
        tok = None
        if inc:
            self.count[sem] = self.count.get(sem, 0) + by
            tok = (sem, self.count[sem])
        self.items[eng].append((fn, flat(deps), sem if inc else None, by))
        return tok

    def last(self):
        return [(e, self.count[e]) for e in ("pe", "act", "dve", "pool") if e in self.count]

    def emit(self, eng, e, sems):
        seen = {}
        for fn, deps, sem, by in self.items[eng]:
            for s, v in deps:
                if seen.get(s, 0) < v:
                    e.wait_ge(sems[s], v)
                    seen[s] = v
            ins = fn(e)
            if sem is not None:
                ins.then_inc(sems[sem], by)


def flat(deps):
    out = []
    for d in deps:
        if d is None:
            continue
        if isinstance(d, tuple) and len(d) == 2 and isinstance(d[0], str):
            out.append(d)
        else:
            out += flat(d)
    need = {}
    for s, v in out:
        need[s] = max(need.get(s, 0), v)
    return list(need.items())


class Buf:

    def __init__(self, t, free=()):
        self.t = t
        self.free = list(free)


def build(nc, a, out):
    q = Queue()
    ctx = ExitStack()
    par, npar = param_order()
    order = weight_order()
    nunit = len(order) // NU

    def sb(stack, name, shape, dt=F32):
        return stack.enter_context(nc.sbuf_tensor(name, shape, dt))

    with ctx:
        bank = [Buf(ctx.enter_context(nc.psum_tensor(f"bank{i}", [128, 512], F32))) for i in range(8)]
        cst = sb(ctx, "cst", [128, NCONST])
        prm = sb(ctx, "prm", [128, npar])
        identb = sb(ctx, "identb", [128, 128], BF)
        msb = sb(ctx, "msb", [128, 128], BF)
        mml = sb(ctx, "mml", [128, 128], BF)
        acc_s = Buf(sb(ctx, "acc_s", [128, S]))
        acc_q = Buf(sb(ctx, "acc_q", [128, S]))
        X = sb(ctx, "X", [128, KD, S])
        XH = sb(ctx, "XH", [128, KD, S], FR)
        XL = sb(ctx, "XL", [128, KD, S], FR)
        wraw = [Buf(sb(ctx, f"wraw{i}", [128, NU * 128])) for i in range(RAW)]
        wh = [Buf(sb(ctx, f"wh{i}", [128, NU * 128], FR)) for i in range(SLOTS)]
        wl = [sb(ctx, f"wl{i}", [128, NU * 128], FR) for i in range(SLOTS)]
        st = sb(ctx, "st", [128, 48])

        def C(name, rows=slice(0, 128)):
            o, n = CONST[name]
            return cst[rows, o:o + n]

        def P(name, j=0, rows=slice(0, 128)):
            return prm[rows, par[name] + j:par[name] + j + 1]

        def act(o, i, f, *deps, bias=None, scale=None, accum=None):
            kw = {}
            if bias is not None:
                kw["bias"] = bias
            if scale is not None:
                kw["scale"] = scale
            if accum is not None:
                kw["accum_out"] = accum
            return q.put("act", lambda e: e.activation(o, i, f, **kw), *deps)

        def stt(o, i0, s, i1, op0, op1, *deps):
            return q.put("dve", lambda e: e.scalar_tensor_tensor(out=o, in0=i0, scalar=s, in1=i1,
                                                                  op0=op0, op1=op1), *deps)

        def tt(o, i0, i1, op, *deps, eng="dve"):
            return q.put(eng, lambda e: e.tensor_tensor(o, i0, i1, op), *deps)

        def ts(o, i0, s1, s2, op0, op1, *deps, eng="dve"):
            if op1 is None:
                return q.put(eng, lambda e: e.tensor_scalar(o, i0, s1, None, op0), *deps)
            return q.put(eng, lambda e: e.tensor_scalar(o, i0, s1, s2, op0, op1), *deps)

        def cp(o, i, *deps, eng="dve"):
            return q.put(eng, lambda e: e.tensor_copy(o, i), *deps)

        def table(n):
            q.put("act", lambda e: e.add_instruction(mybir.InstLoadActFuncSet(
                name=nc.get_next_instruction_name(), engine=mybir.EngineType.Activation, act_func_set_id=n)), inc=False)

        def mm(o, l, r, start, stop, *deps, inc=False):
            return q.put("pe", lambda e: e.matmul(o, l, r, start=start, stop=stop, skip_group_check=True),
                         *deps, inc=inc)

        def dma(sem, o, i, *deps, eng="sp"):
            return q.put(eng, lambda e: e.dma_start(o, i), *deps, sem=sem, by=16)

        def split(h, l, x, *deps, hi="act"):
            if hi == "act":
                t = act(h, x, ACT.Copy, *deps)
            else:
                t = cp(h, x, *deps)
            return tt(l, x, h.bitcast(F32), ALU.subtract, t, *deps)

        t_c = dma("d_c", cst[:, :], a["consts"])
        t_x = dma("d_x", X[:, :, :], a["xt"].rearrange("p (k n) -> p k n", k=KD))
        t_p = dma("d_p", prm[:, :], a["params"])

        ready = {}
        state = {"pos": 0, "made": 0, "read": 0}

        def read_unit(u):
            r = wraw[u % RAW]
            ready[("raw", u)] = dma(f"d_w{u % RAW}", r.t[:, :], a["wstream"][u], r.free)

        def make_unit(u):
            r, h, l = wraw[u % RAW], wh[u % SLOTS], wl[u % SLOTS]
            t1 = act(h.t[:, :], r.t[:, :], ACT.Copy, ready[("raw", u)], h.free)
            t2 = tt(l[:, :], r.t[:, :], h.t[:, :].bitcast(F32), ALU.subtract, t1, ready[("raw", u)], h.free)
            r.free = [t1, t2]
            ready[u] = t2

        def ensure(u):
            while state["made"] <= min(u + AHEAD, nunit - 1):
                n = state["made"]
                while state["read"] <= min(n + RAW - 1, nunit - 1):
                    read_unit(state["read"])
                    state["read"] += 1
                make_unit(n)
                state["made"] += 1

        def take(what, n=1):
            while order[state["pos"]] is None:
                skip()
            p = state["pos"]
            assert order[p] == what, (order[p], what)
            u, j = p // NU, p % NU
            assert j + n <= NU
            if j == 0 or u >= state["made"]:
                ensure(u)
            state["pos"] += n
            s = u % SLOTS
            ends = state["pos"] % NU == 0
            return (wh[s].t[:, j * 128:(j + n) * 128], wl[s][:, j * 128:(j + n) * 128], ready[u], ends, wh[s])

        def skip():
            p = state["pos"]
            if p % NU == 0:
                ensure(p // NU)
            state["pos"] += 1
            if state["pos"] % NU == 0:
                wh[(p // NU) % SLOTS].free = [("pe", q.count["pe"])]

        chains = []

        def step():
            if chains:
                c = chains.pop(0)
                try:
                    next(c)
                    chains.append(c)
                except StopIteration:
                    pass

        def drain():
            while chains:
                step()

        def group(mat, nk, cols, banks, rhs, n=S):
            toks = []
            for k in range(nk):
                xh, xl, dep = rhs(k)
                for c, b in zip(cols, banks):
                    h, l, wd, ends, slot = take((mat, k, c))
                    o = b.t[:, 0:n]
                    last = k == nk - 1
                    mm(o, h, xh, k == 0, False, wd, dep, b.free if k == 0 else None)
                    mm(o, h, xl, False, False)
                    t = mm(o, l, xh, False, last, inc=last or ends)
                    if ends:
                        slot.free = [t]
                    if last:
                        toks.append(t)
                if (k + 1) * len(cols) % 4 == 0:
                    step()
            return toks

        nb = [0]

        def banks(n, pool=6):
            got = [bank[(nb[0] + i) % pool] for i in range(n)]
            nb[0] += n
            return got

        def linear(mat, nk, cols, g, rhs, evac, pool=6):
            for c0 in range(0, len(cols), g):
                cc = cols[c0:c0 + g]
                bb = banks(len(cc), pool)
                for c, b, t in zip(cc, bb, group(mat, nk, cc, bb, rhs)):
                    b.free = [evac(c, b.t, t)]

        def token_major(mat, nk, c0, bb, lhs):
            toks = []
            for k in range(nk):
                h, l, wd, ends, slot = take((mat, k, c0), 4)
                xh, xl, dep = lhs(k)
                for i, b in enumerate(bb):
                    ts_ = slice(i * 128, (i + 1) * 128)
                    last = k == nk - 1
                    mm(b.t[:, :], xh[:, ts_], h, k == 0, False, wd, dep, b.free if k == 0 else None)
                    mm(b.t[:, :], xl[:, ts_], h, False, False)
                    t = mm(b.t[:, :], xh[:, ts_], l, False, last, inc=last or (ends and i == 3))
                    if last:
                        toks.append(t)
                if ends:
                    slot.free = [t]
                step()
            return toks

        class Ring:
            def __init__(self, stack, name, n, shape, dt=F32, free=()):
                self.b = [Buf(sb(stack, f"{name}{i}", shape, dt), free) for i in range(n)]
                self.n = 0

            def get(self):
                self.n += 1
                return self.b[(self.n - 1) % len(self.b)]

        tmp = Ring(ctx, "tmp", 4, [128, S])
        sqr = Ring(ctx, "sqr", 2, [128, S])

        t_idb = act(identb[:, :], C("ident"), ACT.Copy, t_c)
        act(msb[:, :], C("msb"), ACT.Copy, t_c)
        act(mml[:, :], C("mml"), ACT.Copy, t_c)
        t_cb = [("act", q.count["act"])]

        class Stats:

            def __init__(self, centred=True, eng="dve"):
                self.c, self.eng, self.n = centred, eng, 0
                self.b = bank[6]

            def add(self, x, dep):
                if self.n == 0:
                    self.x0, self.d0 = x, dep
                    self.tq = act(acc_q.t[:, :], x, ACT.Square, dep, acc_q.free)
                else:
                    s = sqr.get()
                    t = act(s.t[:, :], x, ACT.Square, dep, s.free)
                    if self.c:
                        a0 = self.x0 if self.n == 1 else acc_s.t[:, :]
                        self.ts = tt(acc_s.t[:, :], a0, x, ALU.add, self.d0, dep,
                                     acc_s.free if self.n == 1 else self.ts, eng=self.eng)
                    self.tq = tt(acc_q.t[:, :], acc_q.t[:, :], s.t[:, :], ALU.add, t, self.tq, eng=self.eng)
                    s.free = [self.tq]
                self.n += 1

            def rows(self):
                for i, (a, t) in enumerate([(acc_s, self.ts), (acc_q, self.tq)] if self.c else [(acc_q, self.tq)]):
                    for j in range(4):
                        o = self.b.t[:, 4 * (i + (not self.c)) + j:][:, 0:1]
                        self.t = mm(o, a.t[:, j * 128:(j + 1) * 128], C("ones")[:, 0:1], i == 0 and j == 0, False, t, t_c,
                                    self.b.free if i == 0 and j == 0 else None, inc=j == 3)
                    a.free = [self.t]

            def done(self, n, eps):
                m, v, r, nm = st[:, 0:4], st[:, 4:8], st[:, 8:12], st[:, 12:16]
                inv = 1.0 / n
                self.rows()
                if self.c:
                    t = ts(m, self.b.t[:, 0:4], inv, None, ALU.mult, None, self.t)
                    t1 = stt(v, m, -1.0, m, ALU.mult, ALU.mult, t)
                    t1 = stt(v, self.b.t[:, 4:8], inv, v, ALU.mult, ALU.add, t1)
                    t1 = ts(v, v, 0.0, eps, ALU.max, ALU.add, t1)
                else:
                    t1 = ts(v, self.b.t[:, 4:8], inv, eps, ALU.mult, ALU.add, self.t)
                tr = q.put("pool", lambda e: e.tensor_tensor(r, v, C("mhalf")[:, 0:4], ALU.pow), t1, t_c)
                da = tmp.get()
                idb = C("ident").unsqueeze(1).broadcast_to([128, 4, 128])
                t2 = tt(da.t[:, :].rearrange("p (j n) -> p j n", j=4), idb,
                        r.unsqueeze(2).broadcast_to([128, 4, 128]), ALU.mult, tr, da.free)
                ta = mm(bank[6].t[:, :], C("ones"), da.t[:, :], True, True, t2, t1, inc=True)
                da.free = [ta]
                self.tb = None
                if self.c:
                    t3 = stt(nm, m, -1.0, r, ALU.mult, ALU.mult, tr)
                    db = tmp.get()
                    t4 = tt(db.t[:, :].rearrange("p (j n) -> p j n", j=4), idb,
                            nm.unsqueeze(2).broadcast_to([128, 4, 128]), ALU.mult, t3, db.free)
                    self.tb = mm(bank[7].t[:, :], C("ones"), db.t[:, :], True, True, t4, bank[7].free, inc=True)
                    db.free = [self.tb]
                self.ta = ta
                return ta

        def normalise(sx, src, dst, dh, dl, g, b, func=ACT.Identity, free=()):
            toks = []
            for f in range(KD):
                u = tmp.get()
                t = tt(u.t[:, :], src(f), bank[6].t[:, :], ALU.mult, sx.ta, u.free)
                t = tt(u.t[:, :], u.t[:, :], bank[7].t[:, :], ALU.add, t, sx.tb)
                tb = t
                t1 = act(dst(f), u.t[:, :], func, t, free, bias=P(b, f), scale=P(g, f))
                u.free = [t1]
                toks.append(split(dh(f), dl(f), dst(f), t1, free))
            bank[6].free = [tb]
            bank[7].free = [tb]
            return toks

        xa = lambda f: X[:, f, :]
        xh = lambda f: XH[:, f, :]
        xl = lambda f: XL[:, f, :]

        ph = ExitStack()
        Y = sb(ph, "Y", [128, KD, S])
        PAD = TAPS - 1
        cr = Ring(ph, "cin", 2, [128, PAD + S])
        chr_ = Ring(ph, "cinh", 2, [128, PAD + S], FR)
        clr = Ring(ph, "cinl", 2, [128, PAD + S], FR)
        accr = Ring(ph, "acc", 4, [128, S])
        prr = Ring(ph, "prod", 2, [128, S])
        acp = Ring(ph, "accp", 1, [128, S])
        dgh = Ring(ph, "dgh", 2 * PE_TAPS, [128, 128], FR)
        dgl = Ring(ph, "dgl", 2 * PE_TAPS, [128, 128], FR)
        dwh = sb(ph, "dwh", [128, 8 * TAPS], FR)
        dwl = sb(ph, "dwl", [128, 8 * TAPS])
        dww = prm[:, par["dww"]:par["dww"] + 8 * TAPS]
        t = cp(dwh[:, :], dww, t_p)
        t_dw = tt(dwl[:, :], dww, dwh[:, :].bitcast(F32), ALU.subtract, t)
        for b in cr.b:
            b.free = [q.put("dve", lambda e, b=b: e.memset(b.t[:, 0:PAD], 0.0))]

        ensure(0)
        xt = [split(xh(k), xl(k), xa(k), t_x) for k in range(KD)]
        rx = lambda k: (xh(k), xl(k), xt[k])

        s1 = Stats(eng="pool")
        taps = []

        def make_diags(f):
            got = []
            for n in range(PE_TAPS):
                c = f * TAPS + TAPS - 1 - n
                dh_, dl_ = dgh.get(), dgl.get()
                t1 = act(dh_.t[:, :], C("ident"), ACT.Copy, dh_.free, t_c, t_dw, scale=dwh[:, c:c + 1].bitcast(F32))
                t2 = act(dl_.t[:, :], C("ident"), ACT.Copy, dl_.free, scale=dwl[:, c:c + 1])
                got.append((dh_, dl_, t2))
            return got

        def pe_taps():
            for f, ch, cl, tsp, b, diags, dv in taps:
                for n, (dh_, dl_, td) in enumerate(diags):
                    k = TAPS - 1 - n
                    mm(b.t[:, :], dh_.t[:, :], ch.t[:, k:k + S], n == 0, False, td, tsp, b.free)
                    mm(b.t[:, :], dh_.t[:, :], cl.t[:, k:k + S], False, False)
                    t = mm(b.t[:, :], dl_.t[:, :], ch.t[:, k:k + S], False, n == PE_TAPS - 1, inc=True)
                    dh_.free = [t]
                    dl_.free = [t]
                ch.free = [t]
                cl.free = [t]
                dv(t)
            taps.clear()

        diags = make_diags(0)
        for f in range(8):
            ba, bg = banks(2)
            ta, = group("pw1", KD, [f], [ba], rx)
            tg, = group("pw1", KD, [8 + f], [bg], rx)
            if taps:
                pe_taps()
            sg = tmp.get()
            t = act(sg.t[:, :], bg.t[:, :], ACT.Sigmoid, tg, sg.free, t_p, bias=P("b1", 8 + f))
            bg.free = [t]
            ci, ch, cl = cr.get(), chr_.get(), clr.get()
            tc_ = stt(ci.t[:, PAD:], ba.t[:, :], P("b1", f), sg.t[:, :], ALU.add, ALU.mult, t, ta, ci.free)
            ba.free = [tc_]
            sg.free = [tc_]
            tsp = split(ch.t[:, :], cl.t[:, :], ci.t[:, :], tc_, ch.free, cl.free)
            nv = TAPS - PE_TAPS - POOL_TAPS
            ap_ = acp.get()
            tpl = ap_.free
            for k in range(nv, nv + POOL_TAPS):
                w, src = P("dww", f * TAPS + k), ci.t[:, k:k + S]
                if k == nv:
                    tpl = act(ap_.t[:, :], src, ACT.Copy, tc_, tpl, scale=w)
                else:
                    pb = prr.get()
                    t1 = act(pb.t[:, :], src, ACT.Copy, pb.free, scale=w)
                    tpl = tt(ap_.t[:, :], ap_.t[:, :], pb.t[:, :], ALU.add, t1, tpl, eng="pool")
                    pb.free = [tpl]
            accs = [accr.get(), accr.get()]
            last = [None, None]
            for k in range(nv):
                j = k % 2
                ac = accs[j]
                w = P("dww", f * TAPS + k)
                src = ci.t[:, k:k + S]
                if k == 0:
                    last[j] = ts(ac.t[:, :], src, w, P("dwb", f), ALU.mult, ALU.add, tc_, ac.free)
                elif k == 1:
                    last[j] = ts(ac.t[:, :], src, w, None, ALU.mult, None, tc_, ac.free)
                else:
                    last[j] = stt(ac.t[:, :], src, w, ac.t[:, :], ALU.mult, ALU.add, last[j])
            ci.free = [last[0], last[1], tsp, t1]
            t = tt(accs[0].t[:, :], accs[0].t[:, :], accs[1].t[:, :], ALU.add, last)
            accs[1].free = [t]
            bt = bank[6 + f % 2]

            def dv(tp, f=f, bt=bt, t=t, ac=accs[0], ap_=ap_, tpl=tpl):
                t = tt(ac.t[:, :], ac.t[:, :], ap_.t[:, :], ALU.add, t, tpl)
                ap_.free = [t]
                t = tt(Y[:, f, :], ac.t[:, :], bt.t[:, :], ALU.add, t, tp)
                ac.free = [t]
                bt.free = [t]
                s1.add(Y[:, f, :], t)
            taps.append((f, ch, cl, tsp, bt, diags, dv))
            if f < 7:
                diags = make_diags(f + 1)
        pe_taps()
        s1.done(D, 1e-5)
        ty = normalise(s1, lambda f: Y[:, f, :], lambda f: Y[:, f, :], xh, xl, "lng", "lnb", ACT.Silu,
                       free=("pe", q.count["pe"]))

        s2 = Stats()

        def evac_mix(c, b, t):
            u = tmp.get()
            t1 = act(u.t[:, :], b[:, :], ACT.Identity, t, u.free, bias=P("b2", c))
            t2 = stt(xa(c), xa(c), ALPHA, u.t[:, :], ALU.mult, ALU.add, t1)
            u.free = [t2]
            s2.add(xa(c), t2)
            return t1

        linear("pw2", KD, list(range(8)), 4, lambda k: (xh(k), xl(k), ty[k]), evac_mix)
        s2.done(D, 1e-5)
        xt = normalise(s2, xa, xa, xh, xl, "mixg0", "mixb0")
        rx = lambda k: (xh(k), xl(k), xt[k])
        ph.close()

        def ffn(layer, xt, over):
            ph = ExitStack()
            HH = sb(ph, f"HH{layer}", [128, FT, S], FR)
            HL = sb(ph, f"HL{layer}", [128, FT, S], FR)
            pth = HH[:, FT - 2:FT, :]
            ptl = HL[:, FT - 2:FT, :]
            tp = []
            for k in range(2):
                pt = tmp.get()
                t = dma(f"d_p{layer}{k}", pt.t[:, :], a["pt"][layer][:, k * S:(k + 1) * S], pt.free)
                tp.append(split(pth[:, k, :], ptl[:, k, :], pt.t[:, :], t, over))
                pt.free = [tp[-1]]
            rx = lambda k: (xh(k), xl(k), xt[k])
            for f0 in range(0, 8, 4):
                cols = list(range(f0, f0 + 4))
                b1 = banks(4)
                t1 = group(f"pg{layer}", KD, cols, b1, rx)
                sg = []
                for i, c in enumerate(cols):
                    u = tmp.get()
                    t = act(u.t[:, :], b1[i].t[:, :], ACT.Sigmoid, t1[i], u.free)
                    b1[i].free = [t]
                    sg.append((u, t))
                for i, c in enumerate(cols):
                    b2, = banks(1)
                    t2, = group(f"pp{layer}", 2, [c], [b2], lambda k: (pth[:, k, :], ptl[:, k, :], tp))
                    u, t = sg[i]
                    t = tt(u.t[:, :], u.t[:, :], b2.t[:, :], ALU.mult, t, t2)
                    b2.free = [t]
                    t = stt(xa(c), xa(c), ALPHA, u.t[:, :], ALU.mult, ALU.add, t, xt)
                    u.free = [t]
            tpe = t2
            th = []
            fcw, fcb = f"fcw{layer}", f"fcb{layer}"
            for f in range(FT):
                bu, bg = banks(2)
                tu, = group(f"up{layer}", KD, [f], [bu], rx)
                tg, = group(f"gate{layer}", KD, [f], [bg], rx)
                u = tmp.get()
                w = lambda j: P(fcw, 3 * f + j)
                t = act(u.t[:, :], bg.t[:, :], ACT.Identity, tg, u.free, scale=w(2), bias=P(fcb, f))
                t = stt(u.t[:, 1:S], bg.t[:, 0:S - 1], w(1), u.t[:, 1:S], ALU.mult, ALU.add, t)
                t = stt(u.t[:, 2:S], bg.t[:, 0:S - 2], w(0), u.t[:, 2:S], ALU.mult, ALU.add, t)
                bg.free = [t]
                t = act(u.t[:, :], u.t[:, :], ACT.Silu, t)
                v = tmp.get()
                t = tt(v.t[:, :], u.t[:, :], bu.t[:, :], ALU.mult, t, tu, v.free)
                u.free = [t]
                bu.free = [t]
                t = split(HH[:, f, :], HL[:, f, :], v.t[:, :], t, over, tpe)
                v.free = [t]
                th.append(t)
            s = Stats()

            def evac(c, b, t):
                t = tt(xa(c), xa(c), b[:, :], ALU.add, t)
                s.add(xa(c), t)
                return t

            linear(f"down{layer}", FT, list(range(8)), 1, lambda k: (HH[:, k, :], HL[:, k, :], th[k]), evac)
            s.done(D, 1e-5)
            over = q.last()
            ph.close()
            return s, over

        s3, over = ffn(0, xt, q.last())
        xt = normalise(s3, xa, xa, xh, xl, "fg0", "fb0")

        ph = ExitStack()
        Q = sb(ph, "Q", [128, KD, S])
        K = sb(ph, "K", [128, KD, S])
        pair = {n: Ring(ph, n, 2, [128, S], FR, over) for n in ("qh", "ql", "kh", "kl")}
        V = sb(ph, "V", [128, 4, D])
        rx = lambda k: (xh(k), xl(k), xt[k])
        tq, tk = {}, {}

        def evac_qk(dst, scale, toks):
            def evac(c, b, t):
                toks[c] = act(dst[:, c, :], b[:, :], ACT.Copy, t, over, scale=scale)
                return toks[c]
            return evac

        linear("wq", KD, list(range(8)), 4, rx, evac_qk(Q, 0.125, tq))
        linear("wk", KD, list(range(8)), 4, rx, evac_qk(K, 1.0, tk))
        tv = []
        for half in range(2):
            bb = banks(4)
            for i, t in enumerate(token_major("wv", KD, 4 * half, bb, rx)):
                t = act(V[:, i, half * 512:(half + 1) * 512], bb[i].t[:, :], ACT.Copy, t, over)
                bb[i].free = [t]
                tv.append(t)
        tpx = ("pe", q.count["pe"])
        W4 = [512, 384, 256, 128]
        OFF = [0, 512, 1024, 1280]
        ZB = [(0, 0), (1, 0), (2, 0), (1, 384)]
        SO = [0, 512, 896, 1152]
        mr = Ring(ph, "sbm", 2, [128, 1280])
        shr = Ring(ph, "sbh", 1, [128, 1280], FR)
        slr = Ring(ph, "sbl", 1, [128, 1280], FR)
        ar = Ring(ph, "sba", 1, [128, 1280])
        for r in (mr, shr, slr, ar):
            for b in r.b:
                b.free = over
        split_pair = {}

        def make_pair(hp):
            qh, ql, kh, kl = (pair[n].get() for n in ("qh", "ql", "kh", "kl"))
            t1 = split(qh.t[:, :], ql.t[:, :], Q[:, hp, :], tq[hp], qh.free)
            t2 = split(kh.t[:, :], kl.t[:, :], K[:, hp, :], tk[hp], kh.free)
            split_pair[hp] = (qh, ql, kh, kl, [t1, t2])

        def zap(bs, kb):
            j, o = ZB[kb]
            return bs[j].t[:, o:o + W4[kb]]

        def sb_scores(h):
            hp, r = h // 2, slice(64 * (h % 2), 64 * (h % 2) + 64)
            bs = [bank[3 * (h % 2) + i] for i in range(3)]
            if h % 2 == 0:
                make_pair(hp)
            qh, ql, kh, kl, tsp = split_pair[hp]
            toks = [None] * 4
            for kb in range(4):
                z = zap(bs, kb)
                ks, qs = slice(kb * 128, kb * 128 + 128), slice(kb * 128, S)
                fr = bs[ZB[kb][0]].free
                mm(z, kh.t[r, ks], qh.t[r, qs], kb != 3, False, tsp, fr)
                mm(z, kh.t[r, ks], ql.t[r, qs], False, False)
                mm(z, kl.t[r, ks], qh.t[r, qs], False, False)
                toks[kb] = mm(z[:, 0:128], identb[:, :], msb[:, :], False, False, t_cb, inc=True)
            qh.free = kh.free = [toks[3]]
            return bs, toks

        def sb_soft(h, bs, zt):
            m, sh, sl = mr.get(), shr.get(), slr.get()
            tm = []
            for kb in range(4):
                tm.append(act(m.t[:, SO[kb]:SO[kb] + W4[kb]], zap(bs, kb), ACT.Abs, zt[3], m.free))
            t = act(m.t[:, :], m.t[:, :], ACT.Exp, tm, scale=-1.0)
            t = act(m.t[:, :], m.t[:, :], ACT.Ln, t, t_c, bias=1.0)
            tz = []
            for kb in range(4):
                c = slice(SO[kb], SO[kb] + W4[kb])
                tz.append(stt(m.t[:, c], zap(bs, kb), 0.0, m.t[:, c], ALU.max, ALU.add, t))
            t1 = cp(sh.t[:, :], m.t[:, :], tz, sh.free)
            t2 = tt(sl.t[:, :], m.t[:, :], sh.t[:, :].bitcast(F32), ALU.subtract, t1, sl.free)
            m.free = [t1, t2]
            return sh, sl, tz, t2

        def sb_sum(bs, so):
            sh, sl, tz, td = so
            toks = []
            for kb in range(4):
                for k2 in range(kb, 4):
                    z = zap(bs, kb)[:, 128 * (k2 - kb):]
                    c = slice(SO[k2], SO[k2] + W4[k2])
                    l = trir if k2 == kb else onesr
                    mm(z, l[:, :], sh.t[:, c], False, False, td, tz, t_sb)
                    t = mm(z, l[:, :], sl.t[:, c], False, k2 == 3, inc=k2 == 3)
                toks.append(t)
            sh.free = [t]
            sl.free = [t]
            return toks

        def sb_exp(h, bs, zt):
            am = ar.get()
            te = []
            for kb in range(4):
                te.append(act(am.t[:, SO[kb]:SO[kb] + W4[kb]], zap(bs, kb), ACT.Exp, zt[3], am.free))
            for b in bs:
                b.free = [te[-1]]
            return am, te

        def sb_out(h, am, te):
            hp, r = h // 2, slice(64 * (h % 2), 64 * (h % 2) + 64)
            ob = bank[6 + hp % 2]
            for kb in range(4):
                t = mm(ob.t[r, kb * 128:S], V[:, kb, h * 64:h * 64 + 64], am.t[:, SO[kb]:SO[kb] + W4[kb]],
                       kb == 0, kb == 3, te[kb], tv, ob.free if h % 2 == 0 else None, inc=kb == 3)
            am.free = [t]
            if h % 2:
                u = tmp.get()
                t = act(u.t[:, :], ob.t[:, :], ACT.Copy, t, u.free)
                ob.free = [t]
                t = split(xh(hp), xl(hp), u.t[:, :], t, tpx, hi="dve")
                u.free = [t]
                return t

        trir = sb(ph, "trir", [128, 128], FR)
        onesr = sb(ph, "onesr", [128, 128], FR)
        t_on = cp(trir[:, :], C("tri"), over)
        t_on = ts(onesr[:, :], C("ones"), -1.0, None, ALU.mult, None, over)
        t_sb = t_cb + [t_on]
        to = []
        table(LNEXP)
        cur = sb_scores(0)
        so = sb_soft(0, *cur)
        prev = None
        for h in range(16):
            if h < 15:
                nxt = sb_scores(h + 1)
            if prev:
                to.append(sb_out(h - 1, *prev))
            zt = sb_sum(cur[0], so)
            if h < 15:
                so = sb_soft(h + 1, *nxt)
            prev = sb_exp(h, cur[0], zt)
            cur = nxt
        to.append(sb_out(15, *prev))
        to = to[1::2]
        s4 = Stats()

        def evac_wo(c, b, t):
            t = stt(xa(c), xa(c), ALPHA, b[:, :], ALU.mult, ALU.add, t)
            s4.add(xa(c), t)
            return t

        linear("wo", KD, list(range(8)), 1, lambda k: (xh(k), xl(k), to[k]), evac_wo)
        s4.done(D, 1e-5)
        over = q.last()
        ph.close()
        xt = normalise(s4, xa, xa, xh, xl, "mixg1", "mixb1", free=over)
        s5, over = ffn(1, xt, over)
        xt = normalise(s5, xa, xa, xh, xl, "fg1", "fb1")

        ph = ExitStack()
        cosT = sb(ph, "cosT", [128, S])
        sinT = sb(ph, "sinT", [128, S])
        t_rope = []

        def rope_tables():
            ang, rr, kk = sqr.get(), acc_s, acc_q
            posi = rr.t[:, :].bitcast(I32)
            t = dma("d_pos", posi, a["pos"].partition_broadcast(128), rr.free)
            yield
            yield
            t = cp(ang.t[:, :], posi, t, ang.free)
            t = ts(ang.t[:, :], ang.t[:, :], C("invf"), None, ALU.mult, None, t)
            magic = 12582912.0
            p1, p2, p3 = 6.28125, 0.0019340515136718750, 1.2556659146679e-06
            for dst, quarter, shift in ((sinT, 0.0, 0.0), (cosT, 0.25, 1.5707963267948966)):
                t1 = ts(kk.t[:, :], ang.t[:, :], 0.15915494309189535, quarter, ALU.mult, ALU.add, t, kk.free)
                t1 = ts(kk.t[:, :], kk.t[:, :], magic, None, ALU.add, None, t1)
                yield
                t1 = ts(kk.t[:, :], kk.t[:, :], -magic, None, ALU.add, None, t1)
                t1 = stt(rr.t[:, :], kk.t[:, :], -p1, ang.t[:, :], ALU.mult, ALU.add, t1)
                yield
                t1 = stt(rr.t[:, :], kk.t[:, :], -p2, rr.t[:, :], ALU.mult, ALU.add, t1)
                t1 = stt(rr.t[:, :], kk.t[:, :], -p3, rr.t[:, :], ALU.mult, ALU.add, t1)
                yield
                if shift:
                    t1 = ts(rr.t[:, :], rr.t[:, :], shift, None, ALU.add, None, t1)
                t1 = ts(rr.t[:, :], rr.t[:, :], 3.1415925, -3.1415925, ALU.min, ALU.max, t1)
                t = t2 = act(dst[:, :], rr.t[:, :], ACT.Sin, t1, over)
                kk.free = [t1]
                yield
            rr.free = [t2]
            t1 = ts(sinT[:, :], sinT[:, :], C("sgn"), None, ALU.mult, None, t2)
            ang.free = [t1]
            t_rope.append(t1)

        R128 = slice(0, 128)
        wgu = sb(ph, "wgu", [128, 256])
        gq = sb(ph, "gq", [128, 2, S])
        gk = sb(ph, "gk", [128, 2, S])
        gv = sb(ph, "gv", [128, 4, S])
        gates = sb(ph, "gates", [128, 8, S])
        lab = sb(ph, "lab", [128, 2, S])
        eb = sb(ph, "eb", [128, 2, S])
        PT = sb(ph, "PT", [128, 4, S])
        ket = PT[:, 0:2, :].rearrange("p a (b n) -> p (a b) n", b=2)
        atm = [PT[:, 2 + i, :] for i in range(2)]
        stt_ = sb(ph, "states", [128, 2, 8, 128])
        cq = sb(ph, "cq", [128, 2, S])
        ckv = sb(ph, "ckv", [128, S])
        kpa = sb(ph, "kpa", [128, S])
        kpb = sb(ph, "kpb", [128, S])
        cqh, cql, ckh, ckl = XH[:, 4:6, :], XL[:, 4:6, :], XH[:, 6, :], XL[:, 6, :]
        qr, kr = eb, kpb
        rn = [0]
        rmq = Ring(ph, "rmq", 2, [128, S], free=over)
        krh = sb(ph, "krh", [128, 2, S])
        sm = sb(ph, "sm", [128, 64])

        def rms_rows(parts, n, scaled=False):
            b = bank[6 + rn[0] % 2]
            rn[0] += 1
            for i, (x, rows, dep) in enumerate(parts):
                t = mm(b.t[:, :], C("ones", rows), x, i == 0, i == len(parts) - 1, dep,
                       b.free if i == 0 else None, inc=i == len(parts) - 1)
            r = rmq.get()
            t1 = act(r.t[:, :], b.t[:, :], ACT.Ln, t, r.free, t_c, scale=1.0 / n, bias=C("epsr"))
            b.free = [t1]
            t2 = act(r.t[:, :], r.t[:, :], ACT.Exp, t1, t_c, scale=-0.5, bias=C("lnsc") if scaled else None)
            return r, t2, t

        for layer in range(2):
            L = str(layer)
            t_wgu = dma(f"d_g{layer}", wgu[64:80, :], a["wgu"][layer], over if layer == 0 else q.last())
            s = Stats(centred=False)
            for f in range(KD):
                s.add(xa(f), xt[f])
            tprev = ("pe", q.count["pe"])
            s.done(D, 1e-6)
            ht = []
            for f in range(KD):
                u = tmp.get()
                t = stt(u.t[:, :], xa(f), P("ng" + L, f), bank[6].t[:, :], ALU.mult, ALU.mult, s.ta, u.free)
                t1 = split(xh(f), xl(f), u.t[:, :], t, tprev, xt[f])
                u.free = [t1]
                ht.append(t1)
            bank[6].free = [t]
            rh = lambda k: (xh(k), xl(k), ht[k])
            fl = over if layer == 0 else q.last()
            atf = [[q.put("dve", lambda e, i=i: e.memset(atm[i], 0.0), fl)] for i in range(2)]
            lrb = tmp.get()
            lr = lrb.t
            got = {}

            def to_sbuf(dst):
                def evac(c, b, t):
                    t = act(dst(c), b[:, :], ACT.Copy, t, fl)
                    got[c] = t
                    return t
                return evac

            def evac0(c, b, t):
                if c == 0:
                    act(kpa[0:64, :], b[0:64, :], ACT.Copy, t, fl)
                    t1 = act(kpa[64:128, :], b[0:64, :], ACT.Copy, t, fl)
                    t2 = cp(lr[64:80, :], b[64:80, :], t, t1, lrb.free)
                    for r0, r1 in ((0, 32), (32, 0), (64, 32), (96, 0)):
                        t2 = cp(kpb[r0:r0 + 32, :], b[r1:r1 + 32, :], t, t1, fl)
                    got[c] = [t1, t2]
                    return t2
                dst = ckv[:, :] if c == 1 else cq[:, c - 2, :]
                return to_sbuf(lambda c: dst)(c, b, t)

            linear("in" + L, KD, [0, 1, 2, 3], 4, rh, evac0)

            def evac_gate(c, b, t):
                t = act(gates[:, c - 12, :], b[:, :], ACT.Silu, t, fl)
                got[c] = t
                return t

            if layer == 0:
                chains.append(rope_tables())
            linear("in" + L, KD, list(range(12, 20)), 4, rh, evac_gate)
            drain()
            table(LNEXP)

            tb, teb, tcn = [None, None], [None, None], {}

            def forget(i):
                b = bank[6 + i]
                t = mm(b.t[:, :], wgu[64:80, i * 128:(i + 1) * 128], lr[64:80, :], True, True, got[0], t_wgu,
                       b.free, inc=True)
                lrb.free = [t]
                u, v = tmp.get(), tmp.get()
                t = ts(u.t[:, :], b.t[:, :], P("bgg" + L, i), None, ALU.add, None, t, u.free)
                b.free = [t]
                t = stt(v.t[:, :], u.t[:, :], -1.0, u.t[:, :], ALU.mult, ALU.min, t, v.free)
                t = act(v.t[:, :], v.t[:, :], ACT.Exp, t)
                t = act(v.t[:, :], v.t[:, :], ACT.Ln, t, bias=1.0)
                t = stt(u.t[:, :], u.t[:, :], 0.0, v.t[:, :], ALU.min, ALU.subtract, t)
                v.free = [t]
                t = q.put("dve", lambda e, i=i, u=u: e.tensor_tensor_scan(
                    lab[:, i, :], C("scan"), u.t[:, :], 0.0, ALU.mult, ALU.add), t, fl)
                u.free = [t]
                tb[i] = t
                teb[i] = act(eb[:, i, :], lab[:, i, :], ACT.Exp, t, fl, scale=0.0625)
                yield

            def low_rank():
                sq = [sqr.get(), sqr.get()]
                ps = [act(sq[k].t[:, :], cq[:, k, :], ACT.Square, got[2 + k], sq[k].free) for k in range(2)]
                yield
                rs, t, tm = rms_rows([(sq[k].t[:, :], R128, ps[k]) for k in range(2)], 256)
                sq[0].free = sq[1].free = [tm]
                yield
                for k in range(2):
                    t1 = tcn[k] = stt(cq[:, k, :], cq[:, k, :], P("mqg" + L, k), rs.t[:, :], ALU.mult, ALU.mult, t)
                rs.free = [t1]
                sq = sqr.get()
                t = act(sq.t[:, :], ckv[:, :], ACT.Square, got[1], sq.free)
                yield
                rs, t, tm = rms_rows([(sq.t[:, :], R128, t)], 128)
                sq.free = [tm]
                yield
                tcn[2] = stt(ckv[:, :], ckv[:, :], P("mkvg" + L), rs.t[:, :], ALU.mult, ALU.mult, t)
                rs.free = [tcn[2]]

            chains.append(forget(0))
            chains.append(forget(1))
            chains.append(low_rank())
            bb = banks(4)
            tgv = []
            for i, t in enumerate(token_major("in" + L, KD, 8, bb, rh)):
                t = act(gv[:, i, :], bb[i].t[:, :], ACT.Copy, t, fl)
                bb[i].free = [t]
                tgv.append(t)
            linear("in" + L, KD, [4, 5, 6, 7], 4, rh,
                   to_sbuf(lambda c: gq[:, c - 4, :] if c < 6 else gk[:, c - 6, :]))
            drain()
            tx_free = ("pe", q.count["pe"])
            mt = {}

            tqd, tki, tke, vb = [None] * 2, [None] * 2, [None] * 2, [None] * 2
            for i in range(2):
                tqd[i] = stt(gq[:, i, :], gq[:, i, :], 0.125, eb[:, i, :], ALU.mult, ALU.mult, got[4 + i], teb[i])
                u, v = tmp.get(), tmp.get()
                t = act(u.t[:, :], lab[:, i, :], ACT.Exp, tb[i], u.free, scale=-0.0625)
                lc = lab[:, i, :].rearrange("p (c n) -> p c n", c=8)
                bl = lc[:, :, 63:64].broadcast_to([128, 8, 64])
                t2 = tt(v.t[:, :].rearrange("p (c n) -> p c n", c=8), bl, lc, ALU.subtract, tb[i], v.free)
                t2 = act(v.t[:, :], v.t[:, :], ACT.Exp, t2, scale=0.0625)
                t2 = tt(v.t[:, :], v.t[:, :], gk[:, i, :], ALU.mult, t2, got[6 + i])
                tki[i] = tt(gk[:, i, :], gk[:, i, :], u.t[:, :], ALU.mult, t, t2)
                u.free = [tki[i]]
                vb[i] = (v, t2)
            ob, oa = {}, {}

            def gla_turn(i):
                v, t2 = vb[i]
                b, = banks(1)
                for j in range(4):
                    o, x = b.t[:, j * 128:(j + 1) * 128], v.t[:, j * 128:(j + 1) * 128]
                    t3 = q.put("pe", lambda e, o=o, x=x: e.transpose(o, x, C("ident")), t2, b.free, inc=j == 3)
                v.free = [t3]
                t4 = cp(ket[:, :, i * 128:(i + 1) * 128], b.t[:, :].rearrange("p (j n) -> p j n", j=4), t3, fl)
                b.free = [t4]
                tke[i] = t4

            def gla_scores(h):
                i, r = h // 2, slice(64 * (h % 2), 64 * (h % 2) + 64)
                at = atm[h % 2]
                b, = banks(1)
                for p in range(4):
                    c = slice(p * 128, (p + 1) * 128)
                    t = mm(b.t[:, c], gk[r, i, c], gq[r, i, c], True, True, tki[i], tqd[i],
                           b.free if p == 0 else None, inc=p == 3)
                ta_ = []
                for p in range(4):
                    c = slice(p * 128, (p + 1) * 128)
                    ta_.append(q.put("dve", lambda e, at=at, b=b, c=c: e.copy_predicated(
                        at[:, c], C("mgl").bitcast(I32), b.t[:, c]), t, atf[h % 2]))
                b.free = [ta_[-1]]
                oa[h] = ta_

            def gla_out(h):
                i, r = h // 2, slice(64 * (h % 2), 64 * (h % 2) + 64)
                at = atm[h % 2]
                b, = banks(1)
                for p in range(4):
                    c = slice(p * 128, (p + 1) * 128)
                    mm(b.t[:, c], gv[:, p, h * 128:(h + 1) * 128], at[:, c], p == 0, False, oa[h], tgv,
                       b.free if p == 0 else None)
                for n in range(8):
                    c = slice(n * 64, n * 64 + 64)
                    t = mm(b.t[:, c], stt_[r, i, n, :], gq[r, i, c], False, n == 7, tst[i], inc=n == 7)
                atf[h % 2] = [t]
                sq = sqr.get()
                ob[h] = (b, sq, act(sq.t[:, :], b.t[:, :], ACT.Square, t, sq.free))

            def gla_norm(h):
                b, sq, t = ob[h]
                rs, t1, tm = rms_rows([(sq.t[:, :], R128, t)], 128)
                sq.free = [tm]
                u = tmp.get()
                t = stt(u.t[:, :], b.t[:, :], P("glag" + L), rs.t[:, :], ALU.mult, ALU.mult, t1, u.free)
                b.free = [t]
                rs.free = [t]
                t = tt(u.t[:, :], u.t[:, :], gates[:, h, :], ALU.mult, t, got[12 + h])
                mt[h] = split(xh(h), xl(h), u.t[:, :], t, tx_free)
                u.free = [mt[h]]

            tst = [[None] * 8 for _ in range(2)]
            ub = {}

            def gla_updates(i, n0):
                pair = banks(2)
                for m in range(n0, min(n0 + 4, 7)):
                    r = slice(64 * (m % 2), 64 * (m % 2) + 64)
                    b, c = pair[m % 2], (m % 4) // 2 * 256
                    t = mm(b.t[:, c:c + 256], ket[r, m // 2, i * 128:(i + 1) * 128],
                           gv[r, m // 2, i * 256:(i + 1) * 256], True, True, tke[i], tgv, b.free, inc=True)
                    ub[i, m] = (b, b.t[:, c:c + 256])
                for m in range(n0, min(n0 + 4, 7)):
                    ub[i, m] += (t,)

            def gla_states(n0):
                for n in range(n0, min(n0 + 4, 7)):
                    for i in range(2):
                        b, o, t = ub[i, n]
                        for hh in range(2):
                            rr_ = slice(64 * hh, 64 * hh + 64)
                            t2 = stt(stt_[rr_, i, n + 1, :], stt_[rr_, i, n, :], eb[rr_, i, 64 * n + 63:64 * n + 64],
                                     o[rr_, 128 * hh:128 * hh + 128], ALU.mult, ALU.add, t, tst[i][n], teb[i], fl)
                            if hh == 0:
                                t1 = t2
                        b.free = [t2]
                        tst[i][n + 1] = [t1, t2]

            for i in range(2):
                tst[i][0] = q.put("pool", lambda e, i=i: e.memset(stt_[:, i, 0, :], 0.0), fl)
            gla_turn(0)
            gla_turn(1)
            gla_scores(0)
            gla_updates(0, 0)
            gla_updates(1, 0)
            gla_scores(1)
            gla_states(0)
            gla_updates(0, 4)
            gla_updates(1, 4)
            gla_states(4)
            tcq = [split(cqh[:, k, :], cql[:, k, :], cq[:, k, :], tcn[k], tx_free) for k in range(2)]
            tck = split(ckh, ckl, ckv[:, :], tcn[2], tx_free)
            gla_out(0)
            gla_scores(2)
            gla_out(1)
            gla_norm(0)
            gla_scores(3)
            gla_out(2)
            gla_norm(1)
            gla_out(3)

            tla = [("pe", q.count["pe"]), ("dve", q.count["dve"]), ("act", q.count["act"])]
            qraw = [gq[:, 0, :], gq[:, 1, :], gk[:, 0, :], gk[:, 1, :]]
            rb = eb

            def evac_q(c, b, t):
                dst = qraw[c] if c < 4 else (lab[:, c - 4, :] if c < 6 else rb[:, c - 6, :])
                t = act(dst, b[:, :], ACT.Copy, t, tla)
                got[("q", c)] = t
                return t

            def last_norms():
                gla_norm(2)
                yield
                gla_norm(3)
                yield

            chains.append(last_norms())
            linear("uq" + L, 2, [4, 5, 6, 7, 0, 1, 2, 3], 4, lambda k: (cqh[:, k, :], cql[:, k, :], tcq[k]), evac_q)
            kraw = [stt_[:, 0, 0:4, :], stt_[:, 0, 4:8, :], stt_[:, 1, 0:4, :], stt_[:, 1, 4:8, :]]
            kraw = [x.rearrange("p c n -> p (c n)") for x in kraw]

            def evac_k(c, b, t):
                t = act(kraw[c], b[:, :], ACT.Copy, t, tla)
                got[("k", c)] = t
                return t

            rk = lambda k: (ckh, ckl, tck)
            linear("ukv" + L, 1, list(range(4)), 4, rk, evac_k)

            def rope(dst, xa_, xb_, ga, gb, deps, free):
                u, v = tmp.get(), tmp.get()
                t1 = stt(u.t[:, :], xa_, ga, cosT[:, :], ALU.mult, ALU.mult, deps, u.free, t_rope)
                t2 = stt(v.t[:, :], xb_, gb, sinT[:, :], ALU.mult, ALU.mult, deps, v.free)
                t3 = tt(dst, u.t[:, :], v.t[:, :], ALU.add, t1, t2, free)
                u.free = [t3]
                v.free = [t3]
                return t3

            tkr = rope(kr[:, :], kpa[:, :], kpb[:, :], P("kga" + L), P("kgb" + L), got[0], fl)
            tqr = [rope(qr[:, i, :], lab[:, i, :], rb[:, i, :], P("qga" + L), P("qgb" + L),
                        [got[("q", 4 + i)], got[("q", 6 + i)]], tla) for i in range(2)]
            tsk = tt(kpa[:, :], kpa[:, :], kpa[:, :], ALU.mult, tkr)
            tsq = [tt(lab[:, i, :], lab[:, i, :], lab[:, i, :], ALU.mult, tqr[i]) for i in range(2)]
            tqk = [[] for _ in range(4)]

            def norm_square(h, key):
                raw = kraw[h] if key else qraw[h]
                sq = sqr.get()
                return raw, sq, tt(sq.t[:, :], raw, raw, ALU.mult, got[("k" if key else "q", h)], sq.free)

            def norm_head(h, key, raw, sq, t):
                r = slice(64 * (h % 2), 64 * (h % 2) + 64)
                side = (kpa[r, :], r, tsk) if key else (lab[r, h // 2, :], r, tsq[h // 2])
                rs, t, tm = rms_rows([(sq.t[:, :], R128, t), side], 192, scaled=not key)
                sq.free = [tm]
                t1 = stt(raw, raw, P(("kgn" if key else "qgn") + L), rs.t[:, :], ALU.mult, ALU.mult, t)
                if key:
                    t2 = tt(krh[r, h // 2, :], kr[r, :], rs.t[r, :], ALU.mult, t, tkr, fl)
                else:
                    t2 = tt(qr[r, h // 2, :], qr[r, h // 2, :], rs.t[r, :], ALU.mult, t, tqr[h // 2])
                rs.free = [t2]
                tqk[h] += [t1, t2]

            def norms():
                prev = None
                for h in range(4):
                    for key in (False, True):
                        cur = (h, key) + norm_square(h, key)
                        if prev:
                            norm_head(*prev)
                        prev = cur
                norm_head(*prev)

            bb = banks(4)
            tmv = []
            for i, t in enumerate(token_major("ukv" + L, 1, 4, bb, rk)):
                t = act(gv[:, i, :], bb[i].t[:, :], ACT.Copy, t, tla)
                bb[i].free = [t]
                tmv.append(t)
            drain()
            norms()

            ptf = tla
            items = [(h, qb) for h in range(4) for qb in range(4)]
            pp, tpt = {}, [[] for _ in range(4)]

            def att_scores(j):
                h, qb = items[j]
                r = slice(64 * (h % 2), 64 * (h % 2) + 64)
                n, qs = 128 * (qb + 1), slice(qb * 128, qb * 128 + 128)
                b, = banks(1)
                mm(b.t[:, 0:n], qraw[h][:, qs], kraw[h][:, 0:n], True, False, tqk[h], b.free)
                mm(b.t[:, 0:n], qr[r, h // 2, qs], krh[r, h // 2, 0:n], False, False)
                t = mm(b.t[:, qs], identb[:, :], mml[:, :], False, True, t_cb, inc=True)
                c = 3 * j
                nm, sumr, rc = (sm[:, c + i_:c + i_ + 1] for i_ in range(3))
                t = q.put("dve", lambda e: e.reduce_max(nm, b.t[:, 0:n], AX.X, negate=True), t, fl)
                p = tmp.get()
                t = act(p.t[:, 0:n], b.t[:, 0:n], ACT.Exp, t, p.free, bias=nm, accum=sumr)
                b.free = [t]
                t = q.put("dve", lambda e: e.reciprocal(rc, sumr), t)
                pp[j] = (p, ts(p.t[:, 0:n], p.t[:, 0:n], rc, None, ALU.mult, None, t))

            def att_turn(j):
                h, qb = items[j]
                n, qs = 128 * (qb + 1), slice(qb * 128, qb * 128 + 128)
                p, t = pp[j]
                b, = banks(1)
                for kb in range(qb + 1):
                    o, x = b.t[:, kb * 128:(kb + 1) * 128], p.t[:, kb * 128:(kb + 1) * 128]
                    t1 = q.put("pe", lambda e, o=o, x=x: e.transpose(o, x, C("ident")), t, b.free, inc=kb == qb)
                p.free = [t1]
                t = act(PT[:, 0:qb + 1, qs], b.t[:, 0:n].rearrange("p (k n) -> p k n", n=128), ACT.Copy, t1, ptf)
                b.free = [t]
                tpt[h].append(t)

            def att_out(h):
                b = bank[6 + h % 2]
                for kb in range(4):
                    t = mm(b.t[:, kb * 128:S], gv[:, kb, h * 128:(h + 1) * 128], PT[:, kb, kb * 128:S], kb == 0, kb == 3,
                           tpt[h], tmv, b.free if kb == 0 else None, inc=kb == 3)
                u = tmp.get()
                tu = tt(u.t[:, :], b.t[:, :], gates[:, 4 + h, :], ALU.mult, t, got[16 + h], u.free)
                b.free = [tu]
                mt[4 + h] = split(xh(4 + h), xl(4 + h), u.t[:, :], tu, ("pe", q.count["pe"]))
                u.free = [mt[4 + h]]
                return [t]

            for j in range(16 + 3):
                if j < 16:
                    att_scores(j)
                if j >= 6 and j % 4 == 2:
                    ptf = att_out((j - 6) // 4)
                if 2 <= j < 18:
                    att_turn(j - 2)

            xn = [None] * KD

            def evac_out(c, b, t):
                t = tt(xa(c), xa(c), b[:, :], ALU.add, t)
                xn[c] = t
                if layer == 1:
                    dma("d_o", a["o"][:, c * S:(c + 1) * S], xa(c), t)
                return t

            linear("out" + L, KD, list(range(8)), 4, lambda k: (xh(k), xl(k), mt[k]), evac_out)
            xt = xn
        ph.close()

        names = sorted({s for s in q.count})
        sems = {n: ctx.enter_context(nc.semaphore("s_" + n)) for n in names}
        block = ctx.enter_context(nc.Block())

        @block.sync
        def _(e):
            q.emit("sp", e, sems)
            e.wait_ge(sems["d_o"], q.count["d_o"])

        @block.tensor
        def _(e):
            q.emit("pe", e, sems)

        @block.scalar
        def _(e):
            q.emit("act", e, sems)

        @block.vector
        def _(e):
            q.emit("dve", e, sems)

        @block.gpsimd
        def _(e):
            q.emit("pool", e, sems)


def lay_out(x):
    import numpy as np

    f = {k: np.asarray(v) for k, v in x.items()}
    mats = {"pw1": f["a_pw1_w"][0], "pw2": f["a_pw2_w"][0], "wq": f["b_wq"][0], "wk": f["kv_wk"], "wv": f["kv_wv"],
            "wo": f["b_wo"][0]}
    for i in range(2):
        mats[f"up{i}"] = f["ffn_w_up"][i]
        mats[f"gate{i}"] = f["ffn_w_gate"][i]
        mats[f"down{i}"] = f["ffn_w_down"][i]
        mats[f"pg{i}"] = f["ple_w_gate"][i]
        mats[f"pp{i}"] = f["ple_w_proj"][i]
        w = f["w_in_2"][i]
        edges = [0, 256, 512, 1024, 1040, 1552, 1808, 1936, 2000, 2512]
        gq, gk, gv, lr, gg, cq, ck, kp, mg = (w[:, a:b] for a, b in zip(edges, edges[1:]))
        mats[f"in{i}"] = np.concatenate([kp, lr, np.zeros((D, 48), w.dtype), ck, cq, gq, gk, gv, gg, mg], 1)
        w = f["w_uq_2"][i].reshape(256, 4, 192)
        r, s = w[:, :, 128:192], np.concatenate([w[:, :, 160:192], w[:, :, 128:160]], 2)
        mats[f"uq{i}"] = np.concatenate([w[:, :, 0:128].reshape(256, 512), r.reshape(256, 256), s.reshape(256, 256)], 1)
        w = f["w_ukv_2"][i].reshape(128, 4, 256)
        mats[f"ukv{i}"] = np.concatenate([w[:, :, 0:128].reshape(128, 512), w[:, :, 128:256].reshape(128, 512)], 1)
        mats[f"out{i}"] = f["w_out_2"][i]
    order = weight_order()
    ws = np.zeros((len(order) // NU, 128, NU * 128), np.float32)
    for n, w in enumerate(order):
        if w is not None:
            m, k, c = w
            ws[n // NU, :, (n % NU) * 128:(n % NU + 1) * 128] = mats[m][k * 128:(k + 1) * 128, c * 128:(c + 1) * 128]

    at, npar = param_order()
    pr = np.zeros((128, npar), np.float32)

    def put(name, v):
        v = v.reshape(-1, 128).T
        pr[:, at[name]:at[name] + v.shape[1]] = v

    put("b1", f["a_pw1_b"][0])
    put("dww", np.ascontiguousarray(f["a_dw_w"][0].reshape(TAPS, 8, 128).transpose(1, 0, 2)))
    put("dwb", f["a_dw_b"][0])
    put("lng", f["a_ln_g"][0])
    put("lnb", f["a_ln_b"][0])
    put("b2", f["a_pw2_b"][0])
    for i in range(2):
        put(f"mixg{i}", f["ln_mix_g"][i])
        put(f"mixb{i}", f["ln_mix_b"][i])
        put(f"fcw{i}", np.ascontiguousarray(f["ffn_conv_w"][i].reshape(3, FT, 128).transpose(1, 0, 2)))
        put(f"fcb{i}", f["ffn_conv_b"][i])
        put(f"fg{i}", f["ln_ffn_g"][i])
        put(f"fb{i}", f["ln_ffn_b"][i])
        put(f"ng{i}", f["norm_g_2"][i])
        put(f"bgg{i}", f["b_gla_gate_2"][i])
        put(f"glag{i}", f["gla_norm_g_2"][i])
        put(f"mqg{i}", f["mla_q_norm_g_2"][i])
        put(f"mkvg{i}", f["mla_kv_norm_g_2"][i])
        for c, g in (("q", f["q_head_g_2"][i]), ("k", f["k_head_g_2"][i])):
            put(f"{c}gn{i}", g[0:128])
            a, b = g[128:160], g[160:192]
            put(f"{c}ga{i}", np.concatenate([a, b, a, b]))
            put(f"{c}gb{i}", np.concatenate([b, a, b, a]))

    def turn(v, k):
        return np.ascontiguousarray(v.T.reshape(k, 128, S).transpose(1, 0, 2).reshape(128, k * S))

    return {"wstream": ws, "params": pr, "xt": turn(f["x"][0], KD),
            "pt": np.stack([turn(f["p"][i, 0], 2) for i in range(2)]),
            "pos": np.ascontiguousarray(f["positions_2"]), "wgu": np.ascontiguousarray(f["w_gla_gate_up_2"])}


def constants():
    import numpy as np

    c = np.zeros((128, NCONST), np.float32)

    def put(name, v):
        o, n = CONST[name]
        c[:, o:o + n] = v

    i, j = np.meshgrid(np.arange(128), np.arange(128), indexing="ij")
    put("ident", i == j)
    put("ones", 1.0)
    put("tri", np.where(i >= j, -1.0, 0.0))
    put("msb", np.where(i >= j, NEG, 0.0))
    put("mml", np.where(j > i, NEG, 0.0))
    put("mgl", (i <= j) & (i // 64 == j // 64))
    put("scan", np.arange(512)[None, :] % 64 != 0)
    p = np.arange(128)[:, None]
    put("invf", np.float32(10000.0) ** (-(2.0 * (p % 32)).astype(np.float32) / np.float32(64)))
    put("sgn", np.where(p % 64 < 32, -1.0, 1.0))
    put("mhalf", -0.5)
    put("one", 1.0)
    put("epsr", 1e-6)
    put("lnsc", -0.5 * np.log(192.0))
    return c


def kernel(**inputs):
    import numpy as _np
    import concourse.bacc as _bacc
    from concourse import mybir as _mybir
    from concourse.bass_utils import run_bass_kernel_spmd as _run

    nc = _bacc.Bacc("TRN2", target_bir_lowering=False, num_devices=1)
    arrays = lay_out(inputs)
    arrays["consts"] = constants()
    aps = {}
    for name in sorted(arrays):
        v = arrays[name]
        aps[name] = nc.dram_tensor(f"in_{name}", v.shape, _mybir.dt.from_np(v.dtype), kind="ExternalInput").ap()
    aps["o"] = nc.dram_tensor("out_0", (128, KD * S), _mybir.dt.float32, kind="ExternalOutput").ap()
    build(nc, aps, aps["o"])
    r = _run(nc, [{f"in_{n}": arrays[n] for n in arrays}], core_ids=[0])
    o = _np.asarray(r.results[0]["out_0"])
    return _np.ascontiguousarray(o.reshape(128, KD, S).transpose(2, 1, 0).reshape(1, S, D))
```

```python
from contextlib import ExitStack

import concourse.bass as bass
from concourse import mybir

ALU = mybir.AluOpType
ACT = mybir.ActivationFunctionType
AX = mybir.AxisListType
F32 = mybir.dt.float32
FR = mybir.dt.float32r
BF = mybir.dt.bfloat16
I32 = mybir.dt.int32

S = 512
D = 1024
KD = 8
FT = 22
NU = 8
RAW, SLOTS, AHEAD = 3, 4, 3
ALPHA = 4.0 ** 0.25
TAPS = 31
PE_TAPS = 9
POOL_TAPS = 7
PACK = 3
LAST_PE_TAPS, LAST_POOL_TAPS = 15, 6
NEG = -1e30
LNEXP = 6
SILU = 18


def grouped(mat, nk, cols, g):
    out = []
    for c0 in range(0, len(cols), g):
        out += [(mat, k, c) for k in range(nk) for c in cols[c0:c0 + g]]
    return out


def ffn_order(layer):
    out = []
    for f in range(FT):
        out += [(f"up{layer}", k, f) for k in range(KD)] + [(f"gate{layer}", k, f) for k in range(KD)]
    return out


def weight_order():
    o = []

    def align():
        while len(o) % 4:
            o.append(None)

    for f in range(8):
        o.extend([("pw1", k, f) for k in range(KD)] + [("pw1", k, 8 + f) for k in range(KD)])
    o += grouped("pw2", KD, list(range(8)), 1)
    for layer in range(2):
        if layer == 1:
            o += grouped("wq", KD, [0, 1], 2)
            o += grouped("wk", KD, [0, 1], 2)
            align()
            for half in range(2):
                o += [("wv", k, 4 * half + c) for k in range(KD) for c in range(4)]
            for c in range(2, 8):
                o += [("wq", k, c) for k in range(KD)] + [("wk", k, c) for k in range(KD)]
            o += [("wo", k, c) for c in range(8) for k in range(5)]
            o += [("wo", k, c) for k in range(5, KD) for c in range(3)]
            o += [("wo", k, c) for c in range(3, 8) for k in range(5, KD)]
        o += grouped(f"pp{layer}", 2, list(range(8)), 1)
        o += grouped(f"pg{layer}", KD, list(range(8)), 4)
        o += ffn_order(layer)
        o += grouped(f"down{layer}", FT, list(range(8)), 1)
    for layer in range(2):
        align()
        o += grouped(f"in{layer}", KD, list(range(4)), 4)
        o += [(f"in{layer}", k, 8 + c) for k in range(KD) for c in range(4)]
        o += grouped(f"in{layer}", KD, list(range(4, 8)), 4)
        o += grouped(f"in{layer}", KD, list(range(12, 20)), 2)
        o += grouped(f"uq{layer}", 2, [4, 5, 6, 7, 0, 1, 2, 3], 4)
        o += grouped(f"ukv{layer}", 1, list(range(4)), 4)
        align()
        o += [(f"ukv{layer}", 0, 4 + c) for c in range(4)]
        for c in range(8):
            o += [(f"out{layer}", k, c) for k in range(4)]
        o += [(f"out{layer}", k, c) for c in range(8) for k in range(4, KD)]
    while len(o) % NU:
        o.append(None)
    return o


def param_order():
    o = [("b1", 16), ("dww", 8 * TAPS), ("dwb", 8), ("lng", 8), ("lnb", 8), ("b2", 8)]
    for i in range(2):
        o += [(f"mixg{i}", 8), (f"mixb{i}", 8), (f"fcw{i}", 3 * FT), (f"fcb{i}", FT),
              (f"fg{i}", 8), (f"fb{i}", 8), (f"ng{i}", 8), (f"bgg{i}", 2), (f"glag{i}", 1),
              (f"mqg{i}", 2), (f"mkvg{i}", 1), (f"qgn{i}", 1), (f"qga{i}", 1), (f"qgb{i}", 1),
              (f"kgn{i}", 1), (f"kga{i}", 1), (f"kgb{i}", 1)]
    at, n = {}, 0
    for name, w in o:
        at[name] = n
        n += w
    return at, n


CONST = {"ident": (0, 128), "ones": (128, 128), "tri": (256, 128), "msb": (384, 128), "mml": (512, 128),
         "mgl": (640, 128), "scan": (768, 512), "invf": (1280, 1), "sgn": (1281, 1), "mhalf": (1282, 16),
         "one": (1298, 1), "epsr": (1299, 1), "halves": (1300, 2), "first": (1302, 4)}
NCONST = 1306


class Queue:

    def __init__(self):
        self.items = {e: [] for e in ("pe", "act", "dve", "pool", "sp")}
        self.count = {}

    def put(self, eng, fn, *deps, inc=True, sem=None, by=1):
        sem = sem or eng
        tok = None
        if inc:
            self.count[sem] = self.count.get(sem, 0) + by
            tok = (sem, self.count[sem])
        self.items[eng].append((fn, flat(deps), sem if inc else None, by))
        return tok

    def last(self):
        return [(e, self.count[e]) for e in ("pe", "act", "dve", "pool") if e in self.count]

    def emit(self, eng, e, sems):
        seen = {}
        for fn, deps, sem, by in self.items[eng]:
            for s, v in deps:
                if seen.get(s, 0) < v:
                    e.wait_ge(sems[s], v)
                    seen[s] = v
            ins = fn(e)
            if sem is not None:
                ins.then_inc(sems[sem], by)


def flat(deps):
    out = []
    for d in deps:
        if d is None:
            continue
        if isinstance(d, tuple) and len(d) == 2 and isinstance(d[0], str):
            out.append(d)
        else:
            out += flat(d)
    need = {}
    for s, v in out:
        need[s] = max(need.get(s, 0), v)
    return list(need.items())


class Buf:

    def __init__(self, t, free=()):
        self.t = t
        self.free = list(free)


def build(nc, a, out):
    q = Queue()
    ctx = ExitStack()
    par, npar = param_order()
    order = weight_order()
    nunit = len(order) // NU

    def sb(stack, name, shape, dt=F32):
        return stack.enter_context(nc.sbuf_tensor(name, shape, dt))

    with ctx:
        bank = [Buf(ctx.enter_context(nc.psum_tensor(f"bank{i}", [128, 512], F32))) for i in range(8)]
        cst = sb(ctx, "cst", [128, NCONST])
        prm = sb(ctx, "prm", [128, npar])
        identb = sb(ctx, "identb", [128, 128], BF)
        msb = sb(ctx, "msb", [128, 128], BF)
        mml = sb(ctx, "mml", [128, 128], BF)
        acc_s = Buf(sb(ctx, "acc_s", [128, S]))
        acc_q = Buf(sb(ctx, "acc_q", [128, S]))
        X = sb(ctx, "X", [128, KD, S])
        XH = sb(ctx, "XH", [128, KD, S], FR)
        XL = sb(ctx, "XL", [128, KD, S], FR)
        wraw = [Buf(sb(ctx, f"wraw{i}", [128, NU * 128])) for i in range(RAW)]
        wh = [Buf(sb(ctx, f"wh{i}", [128, NU * 128], FR)) for i in range(SLOTS)]
        wl = [sb(ctx, f"wl{i}", [128, NU * 128], FR) for i in range(SLOTS)]
        st = sb(ctx, "st", [128, 64])

        def C(name, rows=slice(0, 128)):
            o, n = CONST[name]
            return cst[rows, o:o + n]

        def P(name, j=0, rows=slice(0, 128)):
            return prm[rows, par[name] + j:par[name] + j + 1]

        def act(o, i, f, *deps, bias=None, scale=None, accum=None):
            kw = {}
            if bias is not None:
                kw["bias"] = bias
            if scale is not None:
                kw["scale"] = scale
            if accum is not None:
                kw["accum_out"] = accum
            return q.put("act", lambda e: e.activation(o, i, f, **kw), *deps)

        def stt(o, i0, s, i1, op0, op1, *deps):
            return q.put("dve", lambda e: e.scalar_tensor_tensor(out=o, in0=i0, scalar=s, in1=i1,
                                                                  op0=op0, op1=op1), *deps)

        def tt(o, i0, i1, op, *deps, eng="dve"):
            return q.put(eng, lambda e: e.tensor_tensor(o, i0, i1, op), *deps)

        def ts(o, i0, s1, s2, op0, op1, *deps, eng="dve"):
            if op1 is None:
                return q.put(eng, lambda e: e.tensor_scalar(o, i0, s1, None, op0), *deps)
            return q.put(eng, lambda e: e.tensor_scalar(o, i0, s1, s2, op0, op1), *deps)

        def cp(o, i, *deps, eng="dve"):
            return q.put(eng, lambda e: e.tensor_copy(o, i), *deps)

        def table(n):
            q.put("act", lambda e: e.add_instruction(mybir.InstLoadActFuncSet(
                name=nc.get_next_instruction_name(), engine=mybir.EngineType.Activation, act_func_set_id=n)), inc=False)

        def mm(o, l, r, start, stop, *deps, inc=False):
            return q.put("pe", lambda e: e.matmul(o, l, r, start=start, stop=stop, skip_group_check=True),
                         *deps, inc=inc)

        def dma(sem, o, i, *deps, eng="sp"):
            return q.put(eng, lambda e: e.dma_start(o, i), *deps, sem=sem, by=16)

        def split(h, l, x, *deps, hi="act"):
            if hi == "act":
                t = act(h, x, ACT.Copy, *deps)
            else:
                t = cp(h, x, *deps)
            return tt(l, x, h.bitcast(F32), ALU.subtract, t, *deps)

        ready = {}
        state = {"pos": 0, "made": 0, "read": 0, "ahead": 1}

        def read_unit(u):
            r = wraw[u % RAW]
            ready[("raw", u)] = dma(f"d_w{u % RAW}", r.t[:, :], a["wstream"][u], r.free)

        def make_unit(u):
            r, h, l = wraw[u % RAW], wh[u % SLOTS], wl[u % SLOTS]
            t1 = act(h.t[:, :], r.t[:, :], ACT.Copy, ready[("raw", u)], h.free)
            t2 = tt(l[:, :], r.t[:, :], h.t[:, :].bitcast(F32), ALU.subtract, t1, ready[("raw", u)], h.free)
            r.free = [t1, t2]
            ready[u] = t2

        def ensure(u):
            while state["made"] <= min(u + state["ahead"], nunit - 1):
                n = state["made"]
                while state["read"] <= min(n + RAW - 1, nunit - 1):
                    read_unit(state["read"])
                    state["read"] += 1
                make_unit(n)
                state["made"] += 1

        def take(what, n=1):
            while order[state["pos"]] is None:
                skip()
            p = state["pos"]
            assert order[p] == what, (order[p], what)
            u, j = p // NU, p % NU
            assert j + n <= NU
            if j == 0 or u >= state["made"]:
                ensure(u)
            state["pos"] += n
            s = u % SLOTS
            ends = state["pos"] % NU == 0
            return (wh[s].t[:, j * 128:(j + n) * 128], wl[s][:, j * 128:(j + n) * 128], ready[u], ends, wh[s])

        def skip():
            p = state["pos"]
            if p % NU == 0:
                ensure(p // NU)
            state["pos"] += 1
            if state["pos"] % NU == 0:
                wh[(p // NU) % SLOTS].free = [("pe", q.count["pe"])]

        chains = []

        def step():
            if chains:
                c = chains.pop(0)
                try:
                    next(c)
                    chains.append(c)
                except StopIteration:
                    pass

        def drain():
            while chains:
                step()

        def group(mat, nk, cols, banks, rhs, n=S, k0=0, more=False, resume=False):
            toks = []
            for k in range(k0, nk):
                xh, xl, dep = rhs(k)
                for c, b in zip(cols, banks):
                    h, l, wd, ends, slot = take((mat, k, c))
                    o = b.t[:, 0:n]
                    last = k == nk - 1 and not more
                    first = k == k0 and not resume
                    mm(o, h, xh, first, False, wd, dep, b.free if first else None)
                    mm(o, h, xl, False, False)
                    t = mm(o, l, xh, False, last, inc=last or ends)
                    if ends:
                        slot.free = [t]
                    if last:
                        toks.append(t)
                if (k + 1) * len(cols) % 4 == 0:
                    step()
            return toks

        nb = [0]

        def banks(n, pool=6):
            got = [bank[(nb[0] + i) % pool] for i in range(n)]
            nb[0] += n
            return got

        def linear(mat, nk, cols, g, rhs, evac, pool=6, k0=0):
            for c0 in range(0, len(cols), g):
                cc = cols[c0:c0 + g]
                bb = banks(len(cc), pool)
                for c, b, t in zip(cc, bb, group(mat, nk, cc, bb, rhs, k0=k0)):
                    b.free = [evac(c, b.t, t)]

        def token_major(mat, nk, c0, bb, lhs):
            toks = []
            for k in range(nk):
                h, l, wd, ends, slot = take((mat, k, c0), 4)
                xh, xl, dep = lhs(k)
                for i, b in enumerate(bb):
                    ts_ = slice(i * 128, (i + 1) * 128)
                    last = k == nk - 1
                    mm(b.t[:, :], xh[:, ts_], h, k == 0, False, wd, dep, b.free if k == 0 else None)
                    mm(b.t[:, :], xl[:, ts_], h, False, False)
                    t = mm(b.t[:, :], xh[:, ts_], l, False, last, inc=last or (ends and i == 3))
                    if last:
                        toks.append(t)
                if ends:
                    slot.free = [t]
                step()
            return toks

        class Ring:
            def __init__(self, stack, name, n, shape, dt=F32, free=()):
                self.b = [Buf(sb(stack, f"{name}{i}", shape, dt), free) for i in range(n)]
                self.n = 0

            def get(self):
                self.n += 1
                return self.b[(self.n - 1) % len(self.b)]

        tmp = Ring(ctx, "tmp", 4, [128, S])
        sqr = Ring(ctx, "sqr", 2, [128, S])

        t_x = {}

        def read_x(*ks):
            for k in ks:
                t_x[k] = dma(f"d_x{k}", X[:, k, :], a["xt"][:, k * S:(k + 1) * S])

        def read_next():
            read_unit(state["read"])
            state["read"] += 1

        def make_next():
            make_unit(state["made"])
            state["made"] += 1

        read_x(0)
        read_next()
        read_x(1, 2, 3)
        read_next()
        read_x(4, 5, 6, 7)
        t_p = dma("d_p", prm[:, :], a["params"])
        t_c = dma("d_c", cst[:, :], a["consts"])
        read_next()
        xt = {}

        def split_x(*ks):
            for k in ks:
                xt[k] = split(XH[:, k, :], XL[:, k, :], X[:, k, :], t_x[k])

        split_x(0)
        make_next()
        split_x(1, 2, 3)
        make_next()
        split_x(4, 5, 6, 7)

        act(identb[:, :], C("ident"), ACT.Copy, t_c)
        act(msb[:, :], C("msb"), ACT.Copy, t_c)
        act(mml[:, :], C("mml"), ACT.Copy, t_c)
        t_cb = [("act", q.count["act"])]

        def spread_row(o, v, *deps):
            for j in range(4):
                t = mm(o[:, j * 128:(j + 1) * 128], v[:, j:j + 1].broadcast_to([128, 128]), C("ident"), True, True,
                       *(deps if j == 0 else ()), inc=j == 3)
            return t

        class Stats:

            def __init__(self, centred=True, eng="dve", direct=False, sums="dve"):
                self.c, self.eng, self.sums, self.n, self.direct = centred, eng, sums, 0, direct
                self.b = bank[5 if direct else 6]
                self.square = None

            def add(self, x, dep):
                if self.direct:
                    s = sqr.get()
                    t = act(s.t[:, :], x, ACT.Square, dep, s.free)
                    for j in range(4):
                        first = self.n + j == 0
                        self.t = mm(self.b.t[:, 4 + j:5 + j], s.t[:, j * 128:(j + 1) * 128], C("ones")[:, 0:1], first, False,
                                    t, t_c, self.b.free if first else None, inc=j == 3)
                    s.free = [self.t]
                    self.n += 1
                    return
                if self.n == 0:
                    self.x0, self.d0 = x, dep
                    self.tq = act(acc_q.t[:, :], x, ACT.Square, dep, acc_q.free)
                else:
                    s = sqr.get()
                    t = act(s.t[:, :], x, ACT.Square, dep, s.free)
                    if self.c:
                        a0 = self.x0 if self.n == 1 else acc_s.t[:, :]
                        self.ts = tt(acc_s.t[:, :], a0, x, ALU.add, self.d0, dep,
                                     acc_s.free if self.n == 1 else self.ts,
                                     eng=self.sums if self.n < KD - 1 else self.eng)
                    self.add_square()
                    self.square = (s, t)
                self.n += 1

            def add_square(self):
                if self.square:
                    s, t = self.square
                    self.tq = tt(acc_q.t[:, :], acc_q.t[:, :], s.t[:, :], ALU.add, t, self.tq, eng=self.eng)
                    s.free = [self.tq]
                    self.square = None

            def rows(self):
                self.add_square()
                for i, (a, t) in enumerate([(acc_s, self.ts), (acc_q, self.tq)] if self.c else [(acc_q, self.tq)]):
                    for j in range(4):
                        o = self.b.t[:, 4 * (i + (not self.c)) + j:][:, 0:1]
                        self.t = mm(o, a.t[:, j * 128:(j + 1) * 128], C("ones")[:, 0:1], i == 0 and j == 0, False, t, t_c,
                                    self.b.free if i == 0 and j == 0 else None, inc=j == 3)
                    a.free = [self.t]

            def done(self, n, eps, fill=None):
                fill = fill or iter(())
                m, v, r, nm = st[:, 0:4], st[:, 4:8], st[:, 8:12], st[:, 12:16]
                inv = 1.0 / n
                if not self.direct:
                    self.rows()
                if self.c:
                    t = ts(m, self.b.t[:, 0:4], inv, None, ALU.mult, None, self.t)
                    t1 = stt(v, m, -1.0, m, ALU.mult, ALU.mult, t)
                    t1 = stt(v, self.b.t[:, 4:8], inv, v, ALU.mult, ALU.add, t1)
                    t1 = ts(v, v, 0.0, eps, ALU.max, ALU.add, t1)
                else:
                    t1 = ts(v, self.b.t[:, 4:8], inv, eps, ALU.mult, ALU.add, self.t)
                    self.b.free = [t1]
                tr = q.put("pool", lambda e: e.tensor_tensor(r, v, C("mhalf")[:, 0:4], ALU.pow), t1, t_c)
                if self.c:
                    t3 = stt(nm, m, -1.0, r, ALU.mult, ALU.mult, tr)
                for _ in range(3):
                    next(fill, None)
                ta = spread_row(bank[6].t, r, tr, t1, bank[6].free)
                self.tb = spread_row(bank[7].t, nm, t3, bank[7].free) if self.c else None
                self.ta = ta
                return ta

        def normalise(sx, src, dst, dh, dl, g, b, func=ACT.Identity, free=(), fill=None, split_=True, then=None):
            toks, low = [], None
            fill = fill or iter(())

            def rest():
                f, t = low
                toks.append(tt(dl(f), dst(f), dh(f).bitcast(F32), ALU.subtract, t))

            for f in range(KD):
                u = tmp.get()
                t = tt(u.t[:, :], src(f), bank[6].t[:, :], ALU.mult, sx.ta, u.free)
                t = tt(u.t[:, :], u.t[:, :], bank[7].t[:, :], ALU.add, t, sx.tb)
                tb = t
                t1 = act(dst(f), u.t[:, :], func, t, free, bias=P(b, f), scale=P(g, f))
                u.free = [t1]
                if low:
                    rest()
                if split_:
                    low = (f, act(dh(f), dst(f), ACT.Copy, t1))
                else:
                    toks.append(t1)
                if then:
                    then(dst(f), t1)
                if f:
                    next(fill, None)
            if low:
                rest()
            for _ in fill:
                pass
            bank[6].free = [tb]
            bank[7].free = [tb]
            return toks

        xa = lambda f: X[:, f, :]
        xh = lambda f: XH[:, f, :]
        xl = lambda f: XL[:, f, :]

        def ffn_open(layer, over):
            ph = ExitStack()
            with ExitStack() as same:
                PP = sb(same, f"PP{layer}", [128, KD, S])
            HH = sb(ph, f"HH{layer}", [128, FT, S], FR)
            HL = sb(ph, f"HL{layer}", [128, FT, S], FR)
            pth = HH[:, FT - 2:FT, :]
            ptl = HL[:, FT - 2:FT, :]
            tp = []
            for k in range(2):
                pt = tmp.get()
                t = dma(f"d_p{layer}{k}", pt.t[:, :], a["pt"][layer][:, k * S:(k + 1) * S], pt.free)
                tp.append(split(pth[:, k, :], ptl[:, k, :], pt.t[:, :], t, over))
                pt.free = [tp[-1]]
            tpp = []

            def embed():
                for c in range(8):
                    b, = banks(1)
                    t, = group(f"pp{layer}", 2, [c], [b], lambda k: (pth[:, k, :], ptl[:, k, :], tp))
                    b.free = [act(PP[:, c, :], b.t[:, :], ACT.Copy, t)]
                    tpp.append(b.free[0])
                    yield
            return ph, HH, HL, tpp, PP, embed()

        def ffn(layer, xt, opened):
            ph, HH, HL, tpp, PP, _ = opened
            rx = lambda k: (xh(k), xl(k), xt[k])
            for f0 in range(0, 8, 4):
                cols = list(range(f0, f0 + 4))
                b1 = banks(4)
                t1 = group(f"pg{layer}", KD, cols, b1, rx)
                for i, c in enumerate(cols):
                    u = tmp.get()
                    t = act(u.t[:, :], b1[i].t[:, :], ACT.Sigmoid, t1[i], u.free)
                    b1[i].free = [t]
                    tpe = t = tt(u.t[:, :], u.t[:, :], PP[:, c, :], ALU.mult, t, tpp[c])
                    t = stt(xa(c), xa(c), ALPHA, u.t[:, :], ALU.mult, ALU.add, t, xt)
                    u.free = [t]
            th = []
            fcw, fcb = f"fcw{layer}", f"fcb{layer}"
            for f in range(FT):
                bu, bg = banks(2)
                tu, = group(f"up{layer}", KD, [f], [bu], rx)
                tg, = group(f"gate{layer}", KD, [f], [bg], rx)
                u = tmp.get()
                w = lambda j: P(fcw, 3 * f + j)
                t = act(u.t[:, :], bg.t[:, :], ACT.Identity, tg, u.free, scale=w(2), bias=P(fcb, f))
                t = stt(u.t[:, 1:S], bg.t[:, 0:S - 1], w(1), u.t[:, 1:S], ALU.mult, ALU.add, t)
                t = stt(u.t[:, 2:S], bg.t[:, 0:S - 2], w(0), u.t[:, 2:S], ALU.mult, ALU.add, t)
                bg.free = [t]
                t = act(u.t[:, :], u.t[:, :], ACT.Silu, t)
                v = tmp.get()
                t = tt(v.t[:, :], u.t[:, :], bu.t[:, :], ALU.mult, t, tu, v.free)
                u.free = [t]
                bu.free = [t]
                t = split(HH[:, f, :], HL[:, f, :], v.t[:, :], t, tpe)
                v.free = [t]
                th.append(t)
            s = Stats()

            def evac(c, b, t):
                t = tt(xa(c), xa(c), b[:, :], ALU.add, t)
                s.add(xa(c), t)
                return t

            linear(f"down{layer}", FT, list(range(8)), 1, lambda k: (HH[:, k, :], HL[:, k, :], th[k]), evac)
            s.done(D, 1e-5)
            over = q.last()
            ph.close()
            return s, over

        ph = ExitStack()
        Y = sb(ph, "Y", [128, KD, S])
        PAD = TAPS - 1
        cr = Ring(ph, "cin", 2, [128, PAD + S])
        chr_ = Ring(ph, "cinh", 2, [128, PAD + S], FR)
        clr = Ring(ph, "cinl", 2, [128, PAD + S], FR)
        accr = Ring(ph, "acc", 4, [128, S])
        prr = Ring(ph, "prod", 2, [128, S])
        acp = Ring(ph, "accp", 1, [128, S])
        dgh = Ring(ph, "dgh", 10, [128, PACK, 128], FR)
        dgl = Ring(ph, "dgl", 10, [128, PACK, 128], FR)
        dwh = sb(ph, "dwh", [128, 8 * TAPS], FR)
        dwl = sb(ph, "dwl", [128, 8 * TAPS])
        dww = prm[:, par["dww"]:par["dww"] + 8 * TAPS]
        t = cp(dwh[:, :], dww, t_p)
        t_dw = tt(dwl[:, :], dww, dwh[:, :].bitcast(F32), ALU.subtract, t)
        for b in cr.b:
            b.free = [q.put("dve", lambda e, b=b: e.memset(b.t[:, 0:PAD], 0.0))]

        rx = lambda k: (xh(k), xl(k), xt[k])

        s1 = Stats(eng="pool", sums="pool")
        taps = []

        def make_diags(f):
            got = []
            npe = LAST_PE_TAPS if f == 7 else PE_TAPS
            for k in range(TAPS - npe, TAPS, PACK):
                h, l = dgh.get(), dgl.get()
                c = f * TAPS + k
                for b, w in ((h, dwh[:, c:c + PACK].bitcast(F32)), (l, dwl[:, c:c + PACK])):
                    t = tt(b.t[:, :, :], C("ident").unsqueeze(1).broadcast_to([128, PACK, 128]),
                           w.unsqueeze(2).broadcast_to([128, PACK, 128]), ALU.mult, b.free, t_c, t_dw, eng="pool")
                got.append((k, h, l, t))
            return got

        def pe_taps():
            late = []
            for f, ch, cl, tsp, b, diags, dv in taps:
                for k0, h, l, td in diags:
                    for n in range(PACK):
                        k = k0 + n
                        mm(b.t[:, :], h.t[:, n, :], ch.t[:, k:k + S], k == diags[0][0], False, td, tsp, b.free)
                        mm(b.t[:, :], h.t[:, n, :], cl.t[:, k:k + S], False, False)
                        t = mm(b.t[:, :], l.t[:, n, :], ch.t[:, k:k + S], False, k == TAPS - 1, inc=n == PACK - 1)
                    h.free = l.free = [t]
                ch.free = [t]
                cl.free = [t]
                late.append(lambda: dv(t))
            taps.clear()
            return late

        diags = make_diags(0)
        for f in range(8):
            ba, bg = banks(2)
            ta, = group("pw1", KD, [f], [ba], rx)
            state["ahead"] = AHEAD
            tg, = group("pw1", KD, [8 + f], [bg], rx)
            late = pe_taps()
            sg = tmp.get()
            t = act(sg.t[:, :], bg.t[:, :], ACT.Sigmoid, tg, sg.free, t_p, bias=P("b1", 8 + f))
            bg.free = [t]
            ci, ch, cl = cr.get(), chr_.get(), clr.get()
            tc_ = stt(ci.t[:, PAD:], ba.t[:, :], P("b1", f), sg.t[:, :], ALU.add, ALU.mult, t, ta, ci.free)
            ba.free = [tc_]
            sg.free = [tc_]
            tsp = split(ch.t[:, :], cl.t[:, :], ci.t[:, :], tc_, ch.free, cl.free)
            for add in late:
                add()
            npe, npl = (LAST_PE_TAPS, LAST_POOL_TAPS) if f == 7 else (PE_TAPS, POOL_TAPS)
            nv = TAPS - npe - npl
            if f == 7:
                table(SILU)
                s1.eng = "dve"
            ap_ = acp.get()
            tpl = ap_.free
            for k in range(nv, nv + npl):
                w, src = P("dww", f * TAPS + k), ci.t[:, k:k + S]
                if k == nv:
                    tpl = act(ap_.t[:, :], src, ACT.Copy, tc_, tpl, scale=w)
                else:
                    pb = prr.get()
                    t1 = act(pb.t[:, :], src, ACT.Copy, pb.free, scale=w)
                    tpl = tt(ap_.t[:, :], ap_.t[:, :], pb.t[:, :], ALU.add, t1, tpl, eng="pool")
                    pb.free = [tpl]
            accs = [accr.get(), accr.get()]
            last = [None, None]
            for k in range(nv):
                j = k % 2
                ac = accs[j]
                w = P("dww", f * TAPS + k)
                src = ci.t[:, k:k + S]
                if k == 0:
                    last[j] = ts(ac.t[:, :], src, w, P("dwb", f), ALU.mult, ALU.add, tc_, ac.free)
                elif k == 1:
                    last[j] = ts(ac.t[:, :], src, w, None, ALU.mult, None, tc_, ac.free)
                else:
                    last[j] = stt(ac.t[:, :], src, w, ac.t[:, :], ALU.mult, ALU.add, last[j])
            ci.free = [last[0], last[1], tsp, t1]
            t = tt(accs[0].t[:, :], accs[0].t[:, :], accs[1].t[:, :], ALU.add, last)
            accs[1].free = [t]
            bt = bank[6 + f % 2]

            def dv(tp, f=f, bt=bt, t=t, ac=accs[0], ap_=ap_, tpl=tpl):
                t = tt(ac.t[:, :], ac.t[:, :], ap_.t[:, :], ALU.add, t, tpl)
                ap_.free = [t]
                t = tt(Y[:, f, :], ac.t[:, :], bt.t[:, :], ALU.add, t, tp)
                ac.free = [t]
                bt.free = [t]
                s1.add(Y[:, f, :], t)
            taps.append((f, ch, cl, tsp, bt, diags, dv))
            if f < 7:
                diags = make_diags(f + 1)
        for add in pe_taps():
            add()
        s1.done(D, 1e-5)
        ty = normalise(s1, lambda f: Y[:, f, :], lambda f: Y[:, f, :], xh, xl, "lng", "lnb", ACT.Silu,
                       free=("pe", q.count["pe"]))

        s2 = Stats(sums="pool")

        def evac_mix(c, b, t):
            u = tmp.get()
            t1 = act(u.t[:, :], b[:, :], ACT.Identity, t, u.free, bias=P("b2", c))
            t2 = stt(xa(c), xa(c), ALPHA, u.t[:, :], ALU.mult, ALU.add, t1)
            u.free = [t2]
            s2.add(xa(c), t2)
            return t1

        ph.close()
        opened = ffn_open(0, q.last())
        linear("pw2", KD, list(range(8)), 1, lambda k: (xh(k), xl(k), ty[k]), evac_mix)
        s2.done(D, 1e-5, opened[5])
        xt = normalise(s2, xa, xa, xh, xl, "mixg0", "mixb0", fill=opened[5])

        s3, over = ffn(0, xt, opened)
        xt = normalise(s3, xa, xa, xh, xl, "fg0", "fb0")

        ph = ExitStack()
        with ExitStack() as same:
            Q = sb(same, "Q", [128, KD, S])
            K = sb(same, "K", [128, KD, S])
        OH = sb(ph, "OH", [128, KD, S], FR)
        OL = sb(ph, "OL", [128, KD, S], FR)
        pair = {n: Ring(ph, n, 2, [128, S], FR, over) for n in ("qh", "ql", "kh", "kl")}
        V = sb(ph, "V", [128, 4, D])
        rx = lambda k: (xh(k), xl(k), xt[k])
        tq, tk = {}, {}

        def evac_qk(dst, scale, toks):
            def evac(c, b, t):
                toks[c] = act(dst[:, c, :], b[:, :], ACT.Copy, t, over, scale=scale)
                return toks[c]
            return evac

        linear("wq", KD, [0, 1], 2, rx, evac_qk(Q, 0.125, tq))
        linear("wk", KD, [0, 1], 2, rx, evac_qk(K, 1.0, tk))
        tv = []
        for half in range(2):
            bb = banks(4)
            for i, t in enumerate(token_major("wv", KD, 4 * half, bb, rx)):
                t = act(V[:, i, half * 512:(half + 1) * 512], bb[i].t[:, :], ACT.Copy, t, over)
                bb[i].free = [t]
                tv.append(t)

        def more_pairs():
            for c in range(2, 8):
                for mat, dst, scale, toks in (("wq", Q, 0.125, tq), ("wk", K, 1.0, tk)):
                    b = bank[7]
                    for k in range(KD):
                        h, l, wd, ends, slot = take((mat, k, c))
                        mm(b.t[:, :], h, xh(k), k == 0, False, wd, xt[k], b.free if k == 0 else None)
                        mm(b.t[:, :], h, xl(k), False, False)
                        t = mm(b.t[:, :], l, xh(k), False, k == 7, inc=k == 7 or ends)
                        if ends:
                            slot.free = [t]
                        if k == 7:
                            toks[c] = ts(dst[:, c, :], b.t[:, :], scale, None, ALU.mult, None, t, over)
                            b.free = [toks[c]]
                        yield

        W4 = [512, 384, 256, 128]
        ZB = [(0, 0), (1, 0), (2, 0), (2, 256)]
        GR = [(2, slice(896, 1280), (3, 2)), (1, slice(512, 896), (1,)), (0, slice(0, 512), (0,))]
        SO = [0, 512, 896, 1152]
        mr = Ring(ph, "sbm", 2, [128, 1280])
        shr = Ring(ph, "sbh", 1, [128, 1280], FR)
        slr = Ring(ph, "sbl", 1, [128, 1280], FR)
        ar = Ring(ph, "sba", 1, [128, 1280])
        for r in (mr, shr, slr, ar):
            for b in r.b:
                b.free = over
        split_pair = {}

        def make_pair(hp):
            qh, ql, kh, kl = (pair[n].get() for n in ("qh", "ql", "kh", "kl"))
            t1 = split(qh.t[:, :], ql.t[:, :], Q[:, hp, :], tq[hp], qh.free, hi="dve")
            t2 = split(kh.t[:, :], kl.t[:, :], K[:, hp, :], tk[hp], kh.free, hi="dve")
            split_pair[hp] = (qh, ql, kh, kl, [t1, t2])

        def zap(bs, kb):
            j, o = ZB[kb]
            return bs[j].t[:, o:o + W4[kb]]

        def sb_scores(h):
            hp, r = h // 2, slice(64 * (h % 2), 64 * (h % 2) + 64)
            bs = [bank[3 * (h % 2) + i] for i in range(3)]
            qh, ql, kh, kl, tsp = split_pair[hp]
            toks = [None] * 4
            for kb in range(4):
                z = zap(bs, kb)
                ks, qs = slice(kb * 128, kb * 128 + 128), slice(kb * 128, S)
                fr = bs[ZB[kb][0]].free
                mm(z, kh.t[r, ks], qh.t[r, qs], kb < 3, False, tsp, fr)
                mm(z, kh.t[r, ks], ql.t[r, qs], False, False)
                mm(z, kl.t[r, ks], qh.t[r, qs], False, False)
                toks[kb] = mm(z[:, 0:128], identb[:, :], msb[:, :], False, False, t_cb, inc=True)
            qh.free = kh.free = [toks[3]]
            return bs, toks

        def sb_abs(bs, zt):
            m = mr.get()
            tm = [act(m.t[:, c], bs[j].t[:, 0:c.stop - c.start], ACT.Abs, zt[kbs[0]], m.free) for j, c, kbs in GR]
            return m, tm

        def sb_soft(bs, m, tm):
            sh, sl = shr.get(), slr.get()
            t = act(m.t[:, :], m.t[:, :], ACT.Exp, tm, scale=-1.0)
            t = act(m.t[:, :], m.t[:, :], ACT.Ln, t, t_c, bias=1.0)
            td = []
            for j, c, kbs in GR:
                t1 = stt(m.t[:, c], bs[j].t[:, 0:c.stop - c.start], 0.0, m.t[:, c], ALU.max, ALU.add, t)
                t1 = cp(sh.t[:, c], m.t[:, c], t1, sh.free)
                td.append(tt(sl.t[:, c], m.t[:, c], sh.t[:, c].bitcast(F32), ALU.subtract, t1, sl.free))
            m.free = [td[-1]]
            return sh, sl, td

        def sb_sum(bs, so):
            sh, sl, td = so
            toks = []
            for (j, _, kbs), t in zip(GR, td):
                for kb in kbs:
                    for k2 in range(3, kb - 1, -1):
                        z = zap(bs, kb)[:, 128 * (k2 - kb):]
                        c = slice(SO[k2], SO[k2] + W4[k2])
                        l = trir if k2 == kb else onesr
                        mm(z, l[:, :], sh.t[:, c], False, False, t, t_sb)
                        t1 = mm(z, l[:, :], sl.t[:, c], False, k2 == kb, inc=k2 == kb)
                toks.append(t1)
            sh.free = [t1]
            sl.free = [t1]
            return toks

        def sb_exp(bs, zt):
            am = ar.get()
            te = [None] * 4
            for (j, c, kbs), t in zip(GR, zt):
                t = act(am.t[:, c], bs[j].t[:, 0:c.stop - c.start], ACT.Exp, t, am.free)
                bs[j].free = [t]
                for kb in kbs:
                    te[kb] = t
            return am, te

        def sb_out(h, am, te):
            hp, r = h // 2, slice(64 * (h % 2), 64 * (h % 2) + 64)
            ob = bank[6]
            for kb in range(4):
                t = mm(ob.t[r, kb * 128:S], V[:, kb, h * 64:h * 64 + 64], am.t[:, SO[kb]:SO[kb] + W4[kb]],
                       kb == 0, kb == 3, te[kb], tv, ob.free if h % 2 == 0 else None, inc=kb == 3)
            am.free = [t]
            if h % 2:
                u = tmp.get()
                t = act(u.t[:, :], ob.t[:, :], ACT.Copy, t, u.free)
                ob.free = [t]
                t = split(OH[:, hp, :], OL[:, hp, :], u.t[:, :], t, split_pair[hp][4], hi="dve")
                u.free = [t]
                return t

        trir = sb(ph, "trir", [128, 128], FR)
        onesr = sb(ph, "onesr", [128, 128], FR)
        t_on = cp(trir[:, :], C("tri"), over)
        t_on = ts(onesr[:, :], C("ones"), -1.0, None, ALU.mult, None, over)
        t_sb = t_cb + [t_on]
        to = []
        table(LNEXP)
        make_pair(0)
        make_pair(1)
        def first_pairs_out():
            for c in range(8):
                b = bank[7]
                for k in range(5):
                    h, l, wd, ends, slot = take(("wo", k, c))
                    mm(b.t[:, :], h, OH[:, k, :], k == 0, False, wd, to[2 * k + 1], b.free if k == 0 else None)
                    mm(b.t[:, :], h, OL[:, k, :], False, False)
                    t = mm(b.t[:, :], l, OH[:, k, :], False, k == 4, inc=k == 4 or ends)
                    if ends:
                        slot.free = [t]
                    if k == 4:
                        txo[c] = stt(xa(c), xa(c), ALPHA, b.t[:, :], ALU.mult, ALU.add, t, xt)
                        b.free = [txo[c]]
                    yield

        txo = [None] * KD
        fillers = [more_pairs(), first_pairs_out()]

        def fill(n, i=0):
            for _ in range(n):
                next(fillers[i], None)

        cur = sb_scores(0)
        so = sb_soft(cur[0], *sb_abs(*cur))
        prev = None
        for h in range(16):
            if h < 15:
                nxt = sb_scores(h + 1)
                nabs = sb_abs(*nxt)
                fill(2, h > 11)
            if prev:
                to.append(sb_out(h - 1, *prev))
            fill(3 + 2 * (h == 15), h > 11)
            zt = sb_sum(cur[0], so)
            fill(3 + 2 * (h > 11), h > 11)
            prev = sb_exp(cur[0], zt)
            if h % 2 and h < 13:
                make_pair(h // 2 + 2)
            if h < 15:
                so = sb_soft(nxt[0], *nabs)
                cur = nxt
        to = to[1::2]
        rw = lambda k: (OH[:, k, :], OL[:, k, :], to[k])
        bb = [bank[i] for i in range(3)]
        group("wo", 7, range(3), bb, rw, k0=5, more=True)
        to.append(sb_out(15, *prev))
        tpx = ("pe", q.count["pe"])
        s4 = Stats(sums="pool")

        def evac_wo(c, b, t):
            t = tt(xa(c), xa(c), b[:, :], ALU.add, t, txo[c])
            s4.add(xa(c), t)
            return t

        ph.close()
        opened = ffn_open(1, q.last())
        for c, b, t in zip(range(3), bb, group("wo", KD, range(3), bb, rw, k0=7, resume=True)):
            b.free = [evac_wo(c, b.t, t)]
        nb[0] = 3
        linear("wo", KD, list(range(3, 8)), 1, rw, evac_wo, k0=5)
        s4.done(D, 1e-5, opened[5])
        xt = normalise(s4, xa, xa, xh, xl, "mixg1", "mixb1", free=tpx, fill=opened[5])
        s5, over = ffn(1, xt, opened)
        sr = Stats(centred=False, direct=True)
        xt = normalise(s5, xa, xa, xh, xl, "fg1", "fb1", split_=False, then=sr.add)

        ph = ExitStack()
        cosT = sb(ph, "cosT", [128, S])
        sinT = sb(ph, "sinT", [128, S])
        t_rope = []

        def rope_tables():
            ang, rr, kk = sqr.get(), acc_s, acc_q
            posi = rr.t[:, :].bitcast(I32)
            t = dma("d_pos", posi, a["pos"].partition_broadcast(128), rr.free)
            yield
            yield
            t = cp(ang.t[:, :], posi, t, ang.free)
            t = ts(ang.t[:, :], ang.t[:, :], C("invf"), None, ALU.mult, None, t)
            magic = 12582912.0
            p1, p2, p3 = 6.28125, 0.0019340515136718750, 1.2556659146679e-06
            for dst, quarter, shift in ((sinT, 0.0, 0.0), (cosT, 0.25, 1.5707963267948966)):
                t1 = ts(kk.t[:, :], ang.t[:, :], 0.15915494309189535, quarter, ALU.mult, ALU.add, t, kk.free)
                t1 = ts(kk.t[:, :], kk.t[:, :], magic, None, ALU.add, None, t1)
                yield
                t1 = ts(kk.t[:, :], kk.t[:, :], -magic, None, ALU.add, None, t1)
                t1 = stt(rr.t[:, :], kk.t[:, :], -p1, ang.t[:, :], ALU.mult, ALU.add, t1)
                yield
                t1 = stt(rr.t[:, :], kk.t[:, :], -p2, rr.t[:, :], ALU.mult, ALU.add, t1)
                t1 = stt(rr.t[:, :], kk.t[:, :], -p3, rr.t[:, :], ALU.mult, ALU.add, t1)
                yield
                if shift:
                    t1 = ts(rr.t[:, :], rr.t[:, :], shift, None, ALU.add, None, t1)
                t1 = ts(rr.t[:, :], rr.t[:, :], 3.1415925, -3.1415925, ALU.min, ALU.max, t1)
                t = t2 = act(dst[:, :], rr.t[:, :], ACT.Sin, t1, over)
                kk.free = [t1]
                yield
            rr.free = [t2]
            t1 = ts(sinT[:, :], sinT[:, :], C("sgn"), None, ALU.mult, None, t2)
            ang.free = [t1]
            t_rope.append(t1)

        ONE = C("ones")[:, 0:1]
        wgu = sb(ph, "wgu", [128, 256])
        gq = sb(ph, "gq", [128, 2, S])
        gk = sb(ph, "gk", [128, 2, S])
        gv = sb(ph, "gv", [128, 4, S])
        gates = sb(ph, "gates", [128, 8, S])
        lab = sb(ph, "lab", [128, 2, S])
        eb = sb(ph, "eb", [128, 2, S])
        PT = sb(ph, "PT", [128, 4, S])
        ket = PT[:, 0:2, :].rearrange("p a (b n) -> p (a b) n", b=2)
        atm = [PT[:, 2 + i, :] for i in range(2)]
        stt_ = sb(ph, "states", [128, 2, 8, 128])
        cq = sb(ph, "cq", [128, 2, S])
        ckv = sb(ph, "ckv", [128, S])
        kpa = sb(ph, "kpa", [128, S])
        kpb = sb(ph, "kpb", [128, S])
        cqh, cql, ckh, ckl = XH[:, 4:6, :], XL[:, 4:6, :], XH[:, 6, :], XL[:, 6, :]
        qr, kr = eb, kpb
        rn, rb_ = [0], [0]
        krh = sb(ph, "krh", [128, 2, S])
        sm = sb(ph, "sm", [128, 64])

        vr = sb(ph, "vr", [128, 128])

        def pair_take():
            rb_[0] += 1
            return bank[6 + rb_[0] % 2]

        def pair_give(b, t):
            b.free = [t]

        def rms(norms, n, get, give, scale=1.0, shared=()):
            m = len(norms)
            w = get()
            for i, parts in enumerate(norms):
                for k, (x, one, dep) in enumerate(parts):
                    for j in range(4):
                        first = i + k + j == 0
                        tm = mm(w.t[:, 4 * i + j:4 * i + j + 1], x[:, j * 128:(j + 1) * 128], one,
                                first, False, dep, t_c, w.free if first else None, inc=j == 3)
            for x, h0, ones, dep in shared:
                k = ones.shape[-1]
                for j in range(4):
                    tm = mm(w.t[:, 4 * h0 + j:4 * (h0 + k - 1) + j + 1:4], x[:, j * 128:(j + 1) * 128], ones, False, False,
                            dep, inc=j == 3)
            c = 32 * (rn[0] % 4)
            v, r = vr[:, c:c + 4 * m], vr[:, c + 16:c + 16 + 4 * m]
            rn[0] += 1
            yield
            c = scale ** -2
            t = ts(v, w.t[:, 0:4 * m], c / n, c * 1e-6, ALU.mult, ALU.add, tm)
            give(w, t)
            tr = q.put("pool", lambda e: e.tensor_tensor(r, v, C("mhalf")[:, 0:4 * m], ALU.pow), t, t_c)
            yield

            def spread(i):
                b = get()
                t = spread_row(b.t, r[:, 4 * i:4 * i + 4], tr, b.free)
                return b, t

            return tm, spread

        for layer in range(2):
            L = str(layer)
            t_wgu = dma(f"d_g{layer}", wgu[64:80, :], a["wgu"][layer], over if layer == 0 else q.last())
            s = sr
            tprev = ("pe", q.count["pe"])
            s.done(D, 1e-6)
            ht = []

            def rest():
                f, u, t = low
                ht.append(tt(xl(f), u.t[:, :], xh(f).bitcast(F32), ALU.subtract, t, tprev))
                u.free = [ht[-1]]

            low = None
            for f in range(KD):
                u = tmp.get()
                t = stt(u.t[:, :], xa(f), P("ng" + L, f), bank[6].t[:, :], ALU.mult, ALU.mult, s.ta, u.free)
                if low:
                    rest()
                low = (f, u, act(xh(f), u.t[:, :], ACT.Copy, t, tprev, xt[f]))
            rest()
            bank[6].free = [t]
            rh = lambda k: (xh(k), xl(k), ht[k])
            fl = over if layer == 0 else q.last()
            atf = [[q.put("dve", lambda e, i=i: e.memset(atm[i], 0.0), fl)] for i in range(2)]
            lrb = tmp.get()
            lr = lrb.t
            got = {}

            def to_sbuf(dst):
                def evac(c, b, t):
                    t = act(dst(c), b[:, :], ACT.Copy, t, fl)
                    got[c] = t
                    return t
                return evac

            def evac0(c, b, t):
                if c == 0:
                    act(kpa[0:64, :], b[0:64, :], ACT.Copy, t, fl)
                    t1 = act(kpa[64:128, :], b[0:64, :], ACT.Copy, t, fl)
                    t2 = cp(lr[64:80, :], b[64:80, :], t, t1, lrb.free)
                    for r0, r1 in ((0, 32), (32, 0), (64, 32), (96, 0)):
                        t2 = cp(kpb[r0:r0 + 32, :], b[r1:r1 + 32, :], t, t1, fl)
                    got[c] = [t1, t2]
                    return t2
                dst = ckv[:, :] if c == 1 else cq[:, c - 2, :]
                return to_sbuf(lambda c: dst)(c, b, t)

            if layer == 0:
                chains.append(rope_tables())
            linear("in" + L, KD, [0, 1, 2, 3], 4, rh, evac0)
            drain()
            table(LNEXP)

            def evac_gate(c, b, t):
                t = act(gates[:, c - 12, :], b[:, :], ACT.Silu, t, fl)
                got[c] = t
                return t


            tb, teb, tcn = [None, None], [None, None], {}

            def forget(i):
                b = bank[6 + i]
                t = mm(b.t[:, :], wgu[64:80, i * 128:(i + 1) * 128], lr[64:80, :], True, True, got[0], t_wgu,
                       b.free, inc=True)
                lrb.free = [t]
                u, v = tmp.get(), tmp.get()
                t = ts(u.t[:, :], b.t[:, :], P("bgg" + L, i), None, ALU.add, None, t, u.free)
                b.free = [t]
                t = stt(v.t[:, :], u.t[:, :], -1.0, u.t[:, :], ALU.mult, ALU.min, t, v.free)
                t = act(v.t[:, :], v.t[:, :], ACT.Exp, t)
                t = act(v.t[:, :], v.t[:, :], ACT.Ln, t, bias=1.0)
                t = stt(u.t[:, :], u.t[:, :], 0.0, v.t[:, :], ALU.min, ALU.subtract, t)
                v.free = [t]
                t = q.put("dve", lambda e, i=i, u=u: e.tensor_tensor_scan(
                    lab[:, i, :], C("scan"), u.t[:, :], 0.0, ALU.mult, ALU.add), t, fl)
                u.free = [t]
                tb[i] = t
                teb[i] = act(eb[:, i, :], lab[:, i, :], ACT.Exp, t, fl, scale=0.0625)
                yield

            def low_rank():
                sq = [sqr.get(), sqr.get()]
                ps = [act(sq[k].t[:, :], cq[:, k, :], ACT.Square, got[2 + k], sq[k].free) for k in range(2)]
                yield
                tm, spread = yield from rms([[(sq[k].t[:, :], ONE, ps[k]) for k in range(2)]], 256, pair_take, pair_give)
                sq[0].free = sq[1].free = [tm]
                rs, t = spread(0)
                for k in range(2):
                    t1 = tcn[k] = stt(cq[:, k, :], cq[:, k, :], P("mqg" + L, k), rs.t[:, :], ALU.mult, ALU.mult, t)
                rs.free = [t1]
                sq = sqr.get()
                t = act(sq.t[:, :], ckv[:, :], ACT.Square, got[1], sq.free)
                yield
                tm, spread = yield from rms([[(sq.t[:, :], ONE, t)]], 128, pair_take, pair_give)
                sq.free = [tm]
                rs, t = spread(0)
                tcn[2] = stt(ckv[:, :], ckv[:, :], P("mkvg" + L), rs.t[:, :], ALU.mult, ALU.mult, t)
                rs.free = [tcn[2]]

            chains.append(forget(0))
            chains.append(forget(1))
            chains.append(low_rank())
            bb = banks(4)
            tgv = []
            for i, t in enumerate(token_major("in" + L, KD, 8, bb, rh)):
                t = act(gv[:, i, :], bb[i].t[:, :], ACT.Copy, t, fl)
                bb[i].free = [t]
                tgv.append(t)
            linear("in" + L, KD, [4, 5, 6, 7], 4, rh,
                   to_sbuf(lambda c: gq[:, c - 4, :] if c < 6 else gk[:, c - 6, :]))
            drain()
            mt = {}
            gfree = [bank[i] for i in range(4, 8)]

            def gtake():
                return gfree.pop(0)

            def give(b, t):
                b.free = [t]
                gfree.append(b)

            tqd, tki, tke, vb = [None] * 2, [None] * 2, [None] * 2, [None] * 2
            for i in range(2):
                tqd[i] = stt(gq[:, i, :], gq[:, i, :], 0.125, eb[:, i, :], ALU.mult, ALU.mult, got[4 + i], teb[i])
                u, v = tmp.get(), tmp.get()
                t = act(u.t[:, :], lab[:, i, :], ACT.Exp, tb[i], u.free, scale=-0.0625)
                lc = lab[:, i, :].rearrange("p (c n) -> p c n", c=8)
                bl = lc[:, :, 63:64].broadcast_to([128, 8, 64])
                t2 = tt(v.t[:, :].rearrange("p (c n) -> p c n", c=8), bl, lc, ALU.subtract, tb[i], v.free)
                t2 = act(v.t[:, :], v.t[:, :], ACT.Exp, t2, scale=0.0625)
                t2 = tt(v.t[:, :], v.t[:, :], gk[:, i, :], ALU.mult, t2, got[6 + i])
                tki[i] = tt(gk[:, i, :], gk[:, i, :], u.t[:, :], ALU.mult, t, t2)
                u.free = [tki[i]]
                vb[i] = (v, t2)
            ob, oa, to = {}, {}, {}

            def gla_turn(i):
                v, t2 = vb[i]
                b = gtake()
                for j in range(4):
                    o, x = b.t[:, j * 128:(j + 1) * 128], v.t[:, j * 128:(j + 1) * 128]
                    t3 = q.put("pe", lambda e, o=o, x=x: e.transpose(o, x, C("ident")), t2, b.free, inc=j == 3)
                v.free = [t3]
                t4 = cp(ket[:, :, i * 128:(i + 1) * 128], b.t[:, :].rearrange("p (j n) -> p j n", j=4), t3, fl)
                give(b, t4)
                tke[i] = t4

            def gla_scores(h):
                i, r = h // 2, slice(64 * (h % 2), 64 * (h % 2) + 64)
                at = atm[h % 2]
                b = gtake()
                for p in range(4):
                    c = slice(p * 128, (p + 1) * 128)
                    t = mm(b.t[:, c], gk[r, i, c], gq[r, i, c], True, True, tki[i], tqd[i],
                           b.free if p == 0 else None, inc=p == 3)
                ta_ = []
                for p in range(4):
                    c = slice(p * 128, (p + 1) * 128)
                    ta_.append(q.put("dve", lambda e, at=at, b=b, c=c: e.copy_predicated(
                        at[:, c], C("mgl").bitcast(I32), b.t[:, c]), t, atf[h % 2]))
                give(b, ta_[-1])
                oa[h] = ta_

            def gla_out(h):
                i, r = h // 2, slice(64 * (h % 2), 64 * (h % 2) + 64)
                at = atm[h % 2]
                b = gtake()
                for p in range(4):
                    c = slice(p * 128, (p + 1) * 128)
                    mm(b.t[:, c], gv[:, p, h * 128:(h + 1) * 128], at[:, c], p == 0, False, oa[h], tgv,
                       b.free if p == 0 else None)
                for n in range(8):
                    c = slice(n * 64, n * 64 + 64)
                    t = mm(b.t[:, c], stt_[r, i, n, :], gq[r, i, c], False, n == 7, tst[i], inc=n == 7)
                atf[h % 2] = [t]
                sq = sqr.get()
                ob[h] = (b, sq, act(sq.t[:, :], b.t[:, :], ACT.Square, t, sq.free))

            def gla_norms(hs):
                tm, spread = yield from rms([[(ob[h][1].t[:, :], ONE, ob[h][2])] for h in hs], 128, gtake, give)
                for i, h in enumerate(hs):
                    b, sq, t = ob[h]
                    sq.free = [tm]
                    rs, t1 = spread(i)
                    gt = gates[:, h, :]
                    t = stt(gt, b.t[:, :], P("glag" + L), gt, ALU.mult, ALU.mult, t, got[12 + h])
                    give(b, t)
                    to[h] = tt(gt, gt, rs.t[:, :], ALU.mult, t, t1)
                    give(rs, to[h])
                    yield

            tst = [[None] * 8 for _ in range(2)]
            ub = {}

            def gla_updates(i, n0):
                pair = [gtake(), gtake()]
                for m in range(n0, min(n0 + 4, 7)):
                    r = slice(64 * (m % 2), 64 * (m % 2) + 64)
                    b, c = pair[m % 2], (m % 4) // 2 * 256
                    t = mm(b.t[:, c:c + 256], ket[r, m // 2, i * 128:(i + 1) * 128],
                           gv[r, m // 2, i * 256:(i + 1) * 256], True, True, tke[i], tgv, b.free, inc=True)
                    ub[i, m] = (b, b.t[:, c:c + 256])
                for m in range(n0, min(n0 + 4, 7)):
                    ub[i, m] += (t,)

            def gla_states(i, n0):
                for n in range(n0, min(n0 + 4, 7)):
                    b, o, t = ub[i, n]
                    for hh in range(2):
                        rr_ = slice(64 * hh, 64 * hh + 64)
                        t2 = stt(stt_[rr_, i, n + 1, :], stt_[rr_, i, n, :], eb[rr_, i, 64 * n + 63:64 * n + 64],
                                 o[rr_, 128 * hh:128 * hh + 128], ALU.mult, ALU.add, t, tst[i][n], teb[i], fl)
                        if hh == 0:
                            t1 = t2
                    tst[i][n + 1] = [t1, t2]
                    if n + 2 >= min(n0 + 4, 7):
                        give(b, t2)

            for i in range(2):
                tst[i][0] = q.put("pool", lambda e, i=i: e.memset(stt_[:, i, 0, :], 0.0), fl)

            def gla():
                gla_turn(0)
                yield
                gla_turn(1)
                yield
                gla_updates(0, 0)
                gla_scores(0)
                yield
                gla_states(0, 0)
                gla_updates(0, 4)
                gla_scores(1)
                yield
                gla_states(0, 4)
                gla_updates(1, 0)
                yield
                gla_out(0)
                gla_states(1, 0)
                gla_updates(1, 4)
                yield
                gla_states(1, 4)
                gla_out(1)
                gla_scores(2)
                yield
                yield from gla_norms([0, 1])
                gla_scores(3)
                yield
                gla_out(2)
                yield
                gla_out(3)
                yield
                yield from gla_norms([2, 3])

            chains.append(gla())
            linear("in" + L, KD, list(range(12, 20)), 2, rh, evac_gate, pool=4)
            tx_free = ("pe", q.count["pe"])
            tcq = [split(cqh[:, k, :], cql[:, k, :], cq[:, k, :], tcn[k], tx_free) for k in range(2)]
            tck = split(ckh, ckl, ckv[:, :], tcn[2], tx_free)
            drain()
            for h in range(4):
                mt[h] = split(xh(h), xl(h), gates[:, h, :], to[h], tx_free)

            tla = [("pe", q.count["pe"]), ("dve", q.count["dve"]), ("act", q.count["act"])]
            qraw = [gq[:, 0, :], gq[:, 1, :], gk[:, 0, :], gk[:, 1, :]]
            rb = eb

            def evac_q(c, b, t):
                dst = qraw[c] if c < 4 else (lab[:, c - 4, :] if c < 6 else rb[:, c - 6, :])
                t = act(dst, b[:, :], ACT.Copy, t, tla)
                got[("q", c)] = t
                return t

            linear("uq" + L, 2, [4, 5, 6, 7, 0, 1, 2, 3], 4, lambda k: (cqh[:, k, :], cql[:, k, :], tcq[k]), evac_q)
            kraw = [stt_[:, 0, 0:4, :], stt_[:, 0, 4:8, :], stt_[:, 1, 0:4, :], stt_[:, 1, 4:8, :]]
            kraw = [x.rearrange("p c n -> p (c n)") for x in kraw]

            def evac_k(c, b, t):
                t = act(kraw[c], b[:, :], ACT.Copy, t, tla)
                got[("k", c)] = t
                return t

            rk = lambda k: (ckh, ckl, tck)
            linear("ukv" + L, 1, list(range(4)), 4, rk, evac_k)

            def rope(dst, xa_, xb_, ga, gb, deps, free):
                u, v = tmp.get(), tmp.get()
                t1 = stt(u.t[:, :], xa_, ga, cosT[:, :], ALU.mult, ALU.mult, deps, u.free, t_rope)
                t2 = stt(v.t[:, :], xb_, gb, sinT[:, :], ALU.mult, ALU.mult, deps, v.free)
                t3 = tt(dst, u.t[:, :], v.t[:, :], ALU.add, t1, t2, free)
                u.free = [t3]
                v.free = [t3]
                return t3

            tkr = rope(kr[:, :], kpa[:, :], kpb[:, :], P("kga" + L), P("kgb" + L), got[0], fl)
            tqr = [rope(qr[:, i, :], lab[:, i, :], rb[:, i, :], P("qga" + L), P("qgb" + L),
                        [got[("q", 4 + i)], got[("q", 6 + i)]], tla) for i in range(2)]
            tsk = tt(kpa[:, :], kpa[:, :], kpa[:, :], ALU.mult, tkr)
            tsq = [tt(lab[:, i, :], lab[:, i, :], lab[:, i, :], ALU.mult, tqr[i]) for i in range(2)]
            tqk = [[] for _ in range(4)]

            def halves():
                for c in range(8):
                    b = bank[4 + c % 2]
                    for k in range(4):
                        h, l, wd, ends, slot = take(("out" + L, k, c))
                        mm(b.t[:, :], h, xh(k), k == 0, False, wd, mt[k], b.free if k == 0 else None)
                        mm(b.t[:, :], h, xl(k), False, False)
                        t = mm(b.t[:, :], l, xh(k), False, k == 3, inc=k == 3 or ends)
                        if ends:
                            slot.free = [t]
                        if k == 3:
                            t = tt(xa(c), xa(c), b.t[:, :], ALU.add, t)
                            b.free = [t]
                            xn[c] = t
                        if k % 2 == 1:
                            yield

            xn = [None] * KD
            sides = {False: [(lab[:, i, :], 2 * i, C("halves"), tsq[i]) for i in range(2)],
                     True: [(kpa[:, :], 0, C("first"), tsk)]}

            def head_norms(key):
                parts = []
                for h in range(4):
                    sq = sqr.get() if h < 2 else tmp.get()
                    raw, t = (kraw if key else qraw)[h], got[("k" if key else "q", h)]
                    if h % 2:
                        t = tt(sq.t[:, :], raw, raw, ALU.mult, t, sq.free)
                    else:
                        t = act(sq.t[:, :], raw, ACT.Square, t, sq.free)
                    parts.append((sq, t))
                tm, spread = yield from rms([[(sq.t[:, :], ONE, t)] for sq, t in parts], 192, pair_take, pair_give,
                                            1.0 if key else 192 ** -0.5, sides[key])
                for sq, _ in parts:
                    sq.free = [tm]
                for h in range(4):
                    r = slice(64 * (h % 2), 64 * (h % 2) + 64)
                    b, t = spread(h)
                    if key:
                        t1 = stt(kraw[h], kraw[h], P("kgn" + L), b.t[:, :], ALU.mult, ALU.mult, t)
                        t2 = tt(krh[r, h // 2, :], kr[r, :], b.t[r, :], ALU.mult, t, tkr, fl)
                    else:
                        t1 = stt(qraw[h], qraw[h], P("qgn" + L), b.t[:, :], ALU.mult, ALU.mult, t)
                        t2 = tt(qr[r, h // 2, :], qr[r, h // 2, :], b.t[r, :], ALU.mult, t, tqr[h // 2])
                    b.free = [t2]
                    tqk[h] += [t1, t2]
                    yield

            bb = banks(4)
            tmv = []
            for i, t in enumerate(token_major("ukv" + L, 1, 4, bb, rk)):
                t = act(gv[:, i, :], bb[i].t[:, :], ACT.Copy, t, tla)
                bb[i].free = [t]
                tmv.append(t)
            drain()
            chains.append(halves())
            for key in (False, True):
                for _ in head_norms(key):
                    step()

            ptf = tla
            items = [(h, qb) for h in range(4) for qb in range(4)]
            pp, tpt = {}, [[] for _ in range(4)]

            def att_scores(j):
                h, qb = items[j]
                r = slice(64 * (h % 2), 64 * (h % 2) + 64)
                n, qs = 128 * (qb + 1), slice(qb * 128, qb * 128 + 128)
                b, = banks(1, 4)
                mm(b.t[:, 0:n], qraw[h][:, qs], kraw[h][:, 0:n], True, False, tqk[h], b.free)
                mm(b.t[:, 0:n], qr[r, h // 2, qs], krh[r, h // 2, 0:n], False, False)
                t = mm(b.t[:, qs], identb[:, :], mml[:, :], False, True, t_cb, inc=True)
                c = 3 * j
                nm, sumr, rc = (sm[:, c + i_:c + i_ + 1] for i_ in range(3))
                t = q.put("dve", lambda e: e.reduce_max(nm, b.t[:, 0:n], AX.X, negate=True), t, fl)
                p = tmp.get()
                t = act(p.t[:, 0:n], b.t[:, 0:n], ACT.Exp, t, p.free, bias=nm, accum=sumr)
                b.free = [t]
                t = q.put("dve", lambda e: e.reciprocal(rc, sumr), t)
                pp[j] = (p, ts(p.t[:, 0:n], p.t[:, 0:n], rc, None, ALU.mult, None, t))

            def att_turn(j):
                h, qb = items[j]
                n, qs = 128 * (qb + 1), slice(qb * 128, qb * 128 + 128)
                p, t = pp[j]
                b, = banks(1, 4)
                for kb in range(qb + 1):
                    o, x = b.t[:, kb * 128:(kb + 1) * 128], p.t[:, kb * 128:(kb + 1) * 128]
                    t1 = q.put("pe", lambda e, o=o, x=x: e.transpose(o, x, C("ident")), t, b.free, inc=kb == qb)
                p.free = [t1]
                t = act(PT[:, 0:qb + 1, qs], b.t[:, 0:n].rearrange("p (k n) -> p k n", n=128), ACT.Copy, t1, ptf)
                b.free = [t]
                tpt[h].append(t)

            def att_out(h):
                b = bank[6 + h % 2]
                for kb in range(4):
                    t = mm(b.t[:, kb * 128:S], gv[:, kb, h * 128:(h + 1) * 128], PT[:, kb, kb * 128:S], kb == 0, kb == 3,
                           tpt[h], tmv, b.free if kb == 0 else None, inc=kb == 3)
                u = tmp.get()
                tu = tt(u.t[:, :], b.t[:, :], gates[:, 4 + h, :], ALU.mult, t, got[16 + h], u.free)
                b.free = [tu]
                mt[4 + h] = split(xh(4 + h), xl(4 + h), u.t[:, :], tu, ("pe", q.count["pe"]))
                u.free = [mt[4 + h]]
                return [t]

            for j in range(16 + 3):
                if j < 16:
                    att_scores(j)
                if j >= 6 and j % 4 == 2:
                    ptf = att_out((j - 6) // 4)
                if 2 <= j < 18:
                    att_turn(j - 2)
                step()
            drain()

            sr = Stats(centred=False)

            def evac_out(c, b, t):
                t = tt(xa(c), xa(c), b[:, :], ALU.add, t, xn[c])
                xn[c] = t
                if layer == 0:
                    sr.add(xa(c), t)
                if layer == 1:
                    dma("d_o", a["o"][:, c * S:(c + 1) * S], xa(c), t)
                return t

            linear("out" + L, KD, list(range(8)), 1, lambda k: (xh(k), xl(k), mt[k]), evac_out, k0=4)
            xt = xn
        ph.close()

        names = sorted({s for s in q.count})
        sems = {n: ctx.enter_context(nc.semaphore("s_" + n)) for n in names}
        block = ctx.enter_context(nc.Block())

        @block.sync
        def _(e):
            q.emit("sp", e, sems)
            e.wait_ge(sems["d_o"], q.count["d_o"])

        @block.tensor
        def _(e):
            q.emit("pe", e, sems)

        @block.scalar
        def _(e):
            q.emit("act", e, sems)

        @block.vector
        def _(e):
            q.emit("dve", e, sems)

        @block.gpsimd
        def _(e):
            q.emit("pool", e, sems)


def lay_out(x):
    import numpy as np

    f = {k: np.asarray(v) for k, v in x.items()}
    mats = {"pw1": f["a_pw1_w"][0], "pw2": f["a_pw2_w"][0], "wq": f["b_wq"][0], "wk": f["kv_wk"], "wv": f["kv_wv"],
            "wo": f["b_wo"][0]}
    for i in range(2):
        mats[f"up{i}"] = f["ffn_w_up"][i]
        mats[f"gate{i}"] = f["ffn_w_gate"][i]
        mats[f"down{i}"] = f["ffn_w_down"][i]
        mats[f"pg{i}"] = f["ple_w_gate"][i]
        mats[f"pp{i}"] = f["ple_w_proj"][i]
        w = f["w_in_2"][i]
        edges = [0, 256, 512, 1024, 1040, 1552, 1808, 1936, 2000, 2512]
        gq, gk, gv, lr, gg, cq, ck, kp, mg = (w[:, a:b] for a, b in zip(edges, edges[1:]))
        mats[f"in{i}"] = np.concatenate([kp, lr, np.zeros((D, 48), w.dtype), ck, cq, gq, gk, gv, gg, mg], 1)
        w = f["w_uq_2"][i].reshape(256, 4, 192)
        r, s = w[:, :, 128:192], np.concatenate([w[:, :, 160:192], w[:, :, 128:160]], 2)
        mats[f"uq{i}"] = np.concatenate([w[:, :, 0:128].reshape(256, 512), r.reshape(256, 256), s.reshape(256, 256)], 1)
        w = f["w_ukv_2"][i].reshape(128, 4, 256)
        mats[f"ukv{i}"] = np.concatenate([w[:, :, 0:128].reshape(128, 512), w[:, :, 128:256].reshape(128, 512)], 1)
        mats[f"out{i}"] = f["w_out_2"][i]
    order = weight_order()
    ws = np.zeros((len(order) // NU, 128, NU * 128), np.float32)
    for n, w in enumerate(order):
        if w is not None:
            m, k, c = w
            ws[n // NU, :, (n % NU) * 128:(n % NU + 1) * 128] = mats[m][k * 128:(k + 1) * 128, c * 128:(c + 1) * 128]

    at, npar = param_order()
    pr = np.zeros((128, npar), np.float32)

    def put(name, v):
        v = v.reshape(-1, 128).T
        pr[:, at[name]:at[name] + v.shape[1]] = v

    put("b1", f["a_pw1_b"][0])
    put("dww", np.ascontiguousarray(f["a_dw_w"][0].reshape(TAPS, 8, 128).transpose(1, 0, 2)))
    put("dwb", f["a_dw_b"][0])
    put("lng", f["a_ln_g"][0])
    put("lnb", f["a_ln_b"][0])
    put("b2", f["a_pw2_b"][0])
    for i in range(2):
        put(f"mixg{i}", f["ln_mix_g"][i])
        put(f"mixb{i}", f["ln_mix_b"][i])
        put(f"fcw{i}", np.ascontiguousarray(f["ffn_conv_w"][i].reshape(3, FT, 128).transpose(1, 0, 2)))
        put(f"fcb{i}", f["ffn_conv_b"][i])
        put(f"fg{i}", f["ln_ffn_g"][i])
        put(f"fb{i}", f["ln_ffn_b"][i])
        put(f"ng{i}", f["norm_g_2"][i])
        put(f"bgg{i}", f["b_gla_gate_2"][i])
        put(f"glag{i}", f["gla_norm_g_2"][i])
        put(f"mqg{i}", f["mla_q_norm_g_2"][i])
        put(f"mkvg{i}", f["mla_kv_norm_g_2"][i])
        for c, g in (("q", f["q_head_g_2"][i]), ("k", f["k_head_g_2"][i])):
            put(f"{c}gn{i}", g[0:128])
            a, b = g[128:160], g[160:192]
            put(f"{c}ga{i}", np.concatenate([a, b, a, b]))
            put(f"{c}gb{i}", np.concatenate([b, a, b, a]))

    def turn(v, k):
        return np.ascontiguousarray(v.T.reshape(k, 128, S).transpose(1, 0, 2).reshape(128, k * S))

    return {"wstream": ws, "params": pr, "xt": turn(f["x"][0], KD),
            "pt": np.stack([turn(f["p"][i, 0], 2) for i in range(2)]),
            "pos": np.ascontiguousarray(f["positions_2"]), "wgu": np.ascontiguousarray(f["w_gla_gate_up_2"])}


def constants():
    import numpy as np

    c = np.zeros((128, NCONST), np.float32)

    def put(name, v):
        o, n = CONST[name]
        c[:, o:o + n] = v

    i, j = np.meshgrid(np.arange(128), np.arange(128), indexing="ij")
    put("ident", i == j)
    put("ones", 1.0)
    put("tri", np.where(i >= j, -1.0, 0.0))
    put("msb", np.where(i >= j, NEG, 0.0))
    put("mml", np.where(j > i, NEG, 0.0))
    put("mgl", (i <= j) & (i // 64 == j // 64))
    put("scan", np.arange(512)[None, :] % 64 != 0)
    p = np.arange(128)[:, None]
    put("invf", np.float32(10000.0) ** (-(2.0 * (p % 32)).astype(np.float32) / np.float32(64)))
    put("sgn", np.where(p % 64 < 32, -1.0, 1.0))
    put("mhalf", -0.5)
    put("halves", np.repeat(np.eye(2), 64, 0))
    put("first", np.arange(128)[:, None] < 64)
    put("one", 1.0)
    put("epsr", 1e-6)
    return c


def kernel(**inputs):
    import numpy as _np
    import concourse.bacc as _bacc
    from concourse import mybir as _mybir
    from concourse.bass_utils import run_bass_kernel_spmd as _run

    nc = _bacc.Bacc("TRN2", target_bir_lowering=False, num_devices=1)
    arrays = lay_out(inputs)
    arrays["consts"] = constants()
    aps = {}
    for name in sorted(arrays):
        v = arrays[name]
        aps[name] = nc.dram_tensor(f"in_{name}", v.shape, _mybir.dt.from_np(v.dtype), kind="ExternalInput").ap()
    aps["o"] = nc.dram_tensor("out_0", (128, KD * S), _mybir.dt.float32, kind="ExternalOutput").ap()
    build(nc, aps, aps["o"])
    r = _run(nc, [{f"in_{n}": arrays[n] for n in arrays}], core_ids=[0])
    o = _np.asarray(r.results[0]["out_0"])
    return _np.ascontiguousarray(o.reshape(128, KD, S).transpose(2, 1, 0).reshape(1, S, D))
```
